# Optimizing a Trainium2 kernel written in Bass

```python
import jax, jax.numpy as jnp
from jax import lax
import numpy as np

D_MODEL = 1024
BATCH = 1
SEQ = 256
DEPTH = 2

RET_HEADS = 4
RET_DK = 64
RET_DV = 128
RET_CHUNK = 128
RET_THETA = 10000.0
DSA_HEADS = 8
DSA_KV_HEADS = 2
DSA_DH = 64
DSA_ROT = DSA_DH // 4
ROPE_THETA = 500000.0
IDX_HEADS = 4
IDX_DH = 64
IDX_ROT = IDX_DH // 4
TOPK_MAX = 256
Q_BLOCK = 128
GLA_HEADS = 4
GLA_DK = 64
GLA_DV = 128
GLA_RANK = 16
GLA_TAU = 16.0
GLA_CHUNK = 64

N_BRANCH = 3
RMS_EPS = 1e-6
RET_W = RET_HEADS * RET_DV
DSA_W = DSA_HEADS * DSA_DH
GLA_W = GLA_HEADS * GLA_DV

IN_SPLITS = (
    ("ret_q", RET_HEADS * RET_DK), ("ret_k", RET_HEADS * RET_DK),
    ("ret_v", RET_W), ("ret_g", RET_W),
    ("dsa_q", DSA_W), ("dsa_k", DSA_KV_HEADS * DSA_DH), ("dsa_v", DSA_KV_HEADS * DSA_DH),
    ("dsa_g", DSA_W),
    ("idx_q", IDX_HEADS * IDX_DH), ("idx_k", IDX_DH), ("idx_w", IDX_HEADS),
    ("gla_q", GLA_HEADS * GLA_DK), ("gla_k", GLA_HEADS * GLA_DK),
    ("gla_v", GLA_W), ("gla_g", GLA_W), ("gla_a", GLA_RANK),
    ("merge", N_BRANCH * D_MODEL),
)
IN_WIDTH = sum(w for _, w in IN_SPLITS)


def rms_norm(x, gain=None):
    xf = x.astype(jnp.float32)
    y = xf * lax.rsqrt(jnp.mean(xf * xf, axis=-1, keepdims=True) + RMS_EPS)
    if gain is not None:
        y = y * gain.astype(jnp.float32)
    return y.astype(x.dtype)

def split_proj(p):
    bounds = np.cumsum([w for _, w in IN_SPLITS])[:-1].tolist()
    parts = jnp.split(p, bounds, axis=-1)
    return {name: t for (name, _), t in zip(IN_SPLITS, parts)}

def rope(x, pos, rot_dim, theta):
    half = rot_dim // 2
    freqs = theta ** (-jnp.arange(half, dtype=jnp.float32) * 2.0 / rot_dim)
    ang = pos.astype(jnp.float32)[..., None] * freqs
    cos = jnp.cos(ang)[:, :, None, :]
    sin = jnp.sin(ang)[:, :, None, :]
    xf = x.astype(jnp.float32)
    x1 = xf[..., :half]
    x2 = xf[..., half:rot_dim]
    out = jnp.concatenate([x1 * cos - x2 * sin, x2 * cos + x1 * sin, xf[..., rot_dim:]], axis=-1)
    return out.astype(x.dtype)

def retention(q, k, v, pos):
    dt = v.dtype
    B, S, H, dk = q.shape
    dv = v.shape[-1]
    C = RET_CHUNK
    n = S // C
    q = rope(q, pos, dk, RET_THETA).astype(jnp.float32) * (dk ** -0.5)
    k = rope(k, pos, dk, RET_THETA).astype(jnp.float32)
    v = v.astype(jnp.float32)
    log_g = jnp.log1p(-jnp.exp2(-5.0 - jnp.arange(H, dtype=jnp.float32)))
    idx = jnp.arange(C, dtype=jnp.float32)
    rel = idx[:, None] - idx[None, :]
    decay = jnp.where(rel >= 0, jnp.exp(log_g[:, None, None] * jnp.maximum(rel, 0.0)), 0.0)
    qc = q.reshape(B, n, C, H, dk)
    kc = k.reshape(B, n, C, H, dk)
    vc = v.reshape(B, n, C, H, dv)
    scores = jnp.einsum('bnihd,bnjhd->bnhij', qc, kc) * decay
    o_intra = jnp.einsum('bnhij,bnjhe->bnihe', scores, vc)
    to_end = jnp.exp((C - 1 - idx)[:, None] * log_g[None, :])
    kv = jnp.einsum('bnjhd,bnjhe->bnhde', kc * to_end[None, None, :, :, None], vc)
    chunk_decay = jnp.exp(C * log_g)[None, :, None, None]

    def step(state, kv_n):
        return chunk_decay * state + kv_n, state

    _, prev = lax.scan(step, jnp.zeros((B, H, dk, dv), jnp.float32), jnp.moveaxis(kv, 1, 0))
    prev = jnp.moveaxis(prev, 0, 1)
    q_dec = qc * jnp.exp((idx + 1.0)[:, None] * log_g[None, :])[None, None, :, :, None]
    o_cross = jnp.einsum('bnihd,bnhde->bnihe', q_dec, prev)
    return (o_intra + o_cross).reshape(B, S, H, dv).astype(dt)

def gla(q, k, v, log_a):
    dt = v.dtype
    B, S, H, dk = q.shape
    dv = v.shape[-1]
    C = GLA_CHUNK
    n = S // C
    q = q.astype(jnp.float32) * (dk ** -0.5)
    k = k.astype(jnp.float32)
    v = v.astype(jnp.float32)
    log_a = log_a.astype(jnp.float32)
    causal = jnp.tril(jnp.ones((C, C), bool))

    def to_chunks(t):
        return jnp.moveaxis(t.reshape(B, n, C, H, t.shape[-1]), 1, 0)

    def step(state, inp):
        qn, kn, vn, an = inp
        bcum = jnp.cumsum(an, axis=1)
        diff = bcum[:, :, None] - bcum[:, None, :]
        w = jnp.exp(jnp.where(causal[None, :, :, None, None], diff, -jnp.inf))
        attn = jnp.einsum('bihd,bjhd,bijhd->bhij', qn, kn, w)
        o = (jnp.einsum('bhij,bjhe->bihe', attn, vn)
             + jnp.einsum('bihd,bhde->bihe', qn * jnp.exp(bcum), state))
        b_last = bcum[:, -1]
        new = (jnp.exp(b_last)[..., None] * state
               + jnp.einsum('bjhd,bjhe->bhde', kn * jnp.exp(b_last[:, None] - bcum), vn))
        return new, o

    _, o = lax.scan(step, jnp.zeros((B, H, dk, dv), jnp.float32),
                    (to_chunks(q), to_chunks(k), to_chunks(v), to_chunks(log_a)))
    return jnp.moveaxis(o, 0, 1).reshape(B, S, H, dv).astype(dt)

def dsa_attention(q, k, v, q_idx, k_idx, w_idx, pos):
    B, S, H, dh = q.shape
    KV = k.shape[2]
    G = H // KV
    topk = min(TOPK_MAX, S // 4)
    QB = Q_BLOCK
    nb = S // QB
    q = rope(q, pos, DSA_ROT, ROPE_THETA)
    k = rope(k, pos, DSA_ROT, ROPE_THETA)
    q_idx = rope(q_idx, pos, IDX_ROT, ROPE_THETA)
    k_idx_f = rope(k_idx[:, :, None], pos, IDX_ROT, ROPE_THETA)[:, :, 0].astype(jnp.float32)
    w_f = w_idx.astype(jnp.float32) * (IDX_HEADS ** -0.5)
    key_pos = jnp.arange(S)

    def blockify(t):
        return jnp.moveaxis(t.reshape(B, nb, QB, *t.shape[2:]), 1, 0)

    def one_block(inp):
        qb, qib, wb, tb = inp
        s = jnp.einsum('bqhd,bsd->bqhs', qib.astype(jnp.float32), k_idx_f) * (IDX_DH ** -0.5)
        score = jnp.einsum('bqh,bqhs->bqs', wb, jax.nn.relu(s))
        visible = key_pos[None, :] <= tb[:, None]
        score = jnp.where(visible[None], score, -jnp.inf)
        _, sel = lax.top_k(score, topk)
        valid = sel <= tb[None, :, None]
        ks = jax.vmap(lambda kk, ii: kk[ii])(k, sel)
        vs = jax.vmap(lambda vv, ii: vv[ii])(v, sel)
        qg = qb.reshape(B, QB, KV, G, dh)
        logits = jnp.einsum('bqngd,bqknd->bqngk', qg, ks).astype(jnp.float32) * (dh ** -0.5)
        logits = jnp.where(valid[:, :, None, None, :], logits, -jnp.inf)
        p = jax.nn.softmax(logits, axis=-1).astype(vs.dtype)
        o = jnp.einsum('bqngk,bqknd->bqngd', p, vs)
        return o.reshape(B, QB, H * dh)

    t_blocks = jnp.arange(S).reshape(nb, QB)
    out = lax.map(one_block, (blockify(q), blockify(q_idx), blockify(w_f), t_blocks))
    return jnp.moveaxis(out, 0, 1).reshape(B, S, H * dh)

def first_inputs(seed: int = 0) -> dict:
    key = jax.random.key(seed)
    ks = jax.random.split(key, 16)
    D = D_MODEL
    nrm = jax.random.normal
    x = nrm(ks[0], (BATCH, SEQ, D), jnp.float32)
    c = nrm(ks[1], (BATCH, D), jnp.float32)
    positions = (jnp.arange(SEQ, dtype=jnp.int32)[None, :]
                 + jax.random.randint(ks[2], (BATCH, 1), 0, 4096, dtype=jnp.int32))
    ada_w = nrm(ks[3], (DEPTH, D, 3 * D), jnp.float32) * (0.1 * D ** -0.5)
    ada_b = nrm(ks[4], (DEPTH, 3 * D), jnp.float32) * 0.02
    pre_norm = 1.0 + 0.05 * nrm(ks[5], (DEPTH, D), jnp.float32)
    post_norm = 1.0 + 0.05 * nrm(ks[6], (DEPTH, D), jnp.float32)
    w_in = nrm(ks[7], (DEPTH, D, IN_WIDTH), jnp.float32) * (D ** -0.5)
    gla_w_lr = nrm(ks[8], (DEPTH, GLA_RANK, GLA_HEADS * GLA_DK), jnp.float32) * (GLA_RANK ** -0.5)
    gla_b_lr = 0.1 * nrm(ks[9], (DEPTH, GLA_HEADS * GLA_DK), jnp.float32)
    w_br_ret = nrm(ks[10], (DEPTH, RET_W, D), jnp.float32) * (RET_W ** -0.5)
    w_br_dsa = nrm(ks[11], (DEPTH, DSA_W, D), jnp.float32) * (DSA_W ** -0.5)
    w_br_gla = nrm(ks[12], (DEPTH, GLA_W, D), jnp.float32) * (GLA_W ** -0.5)
    w_out = nrm(ks[13], (DEPTH, D, D), jnp.float32) * (D ** -0.5)
    return {"x": x, "c": c, "positions": positions, "ada_w": ada_w, "ada_b": ada_b,
            "pre_norm": pre_norm, "post_norm": post_norm, "w_in": w_in,
            "gla_w_lr": gla_w_lr, "gla_b_lr": gla_b_lr, "w_br_ret": w_br_ret,
            "w_br_dsa": w_br_dsa, "w_br_gla": w_br_gla, "w_out": w_out}

def first_block(x, c, positions, ada_w, ada_b, pre_norm, post_norm, w_in, gla_w_lr, gla_b_lr,
              w_br_ret, w_br_dsa, w_br_gla, w_out):
    B, S, D = x.shape
    c_act = jax.nn.silu(c)
    for l in range(DEPTH):
        mod = c_act @ ada_w[l] + ada_b[l]
        shift, scale, gate = jnp.split(mod, 3, axis=-1)
        h = rms_norm(x, pre_norm[l]) * (1.0 + scale[:, None]) + shift[:, None]
        p = split_proj(h @ w_in[l])
        ret = retention(p["ret_q"].reshape(B, S, RET_HEADS, RET_DK),
                        p["ret_k"].reshape(B, S, RET_HEADS, RET_DK),
                        p["ret_v"].reshape(B, S, RET_HEADS, RET_DV), positions)
        ret = rms_norm(ret).reshape(B, S, RET_W) * jax.nn.silu(p["ret_g"])
        dsa = dsa_attention(p["dsa_q"].reshape(B, S, DSA_HEADS, DSA_DH),
                            p["dsa_k"].reshape(B, S, DSA_KV_HEADS, DSA_DH),
                            p["dsa_v"].reshape(B, S, DSA_KV_HEADS, DSA_DH),
                            p["idx_q"].reshape(B, S, IDX_HEADS, IDX_DH),
                            p["idx_k"], p["idx_w"], positions)
        dsa = dsa * jax.nn.silu(p["dsa_g"])
        log_a = jax.nn.log_sigmoid((p["gla_a"] @ gla_w_lr[l] + gla_b_lr[l]).astype(jnp.float32)) / GLA_TAU
        gl = gla(p["gla_q"].reshape(B, S, GLA_HEADS, GLA_DK),
                 p["gla_k"].reshape(B, S, GLA_HEADS, GLA_DK),
                 p["gla_v"].reshape(B, S, GLA_HEADS, GLA_DV),
                 log_a.reshape(B, S, GLA_HEADS, GLA_DK))
        gl = rms_norm(gl).reshape(B, S, GLA_W) * jax.nn.silu(p["gla_g"])
        g = jax.nn.sigmoid(p["merge"]).reshape(B, S, N_BRANCH, D)
        y = (g[:, :, 0] * (ret @ w_br_ret[l])
             + g[:, :, 1] * (dsa @ w_br_dsa[l])
             + g[:, :, 2] * (gl @ w_br_gla[l]))
        y = y @ w_out[l]
        x = x + gate[:, None] * rms_norm(y, post_norm[l])
    return x


CTX_LEN = 256
GRID_W = 64
ROPE_BASE = 10000.0
NORM_EPS = 1e-6
NEG_INF = -1e30

A_HEADS = 8
A_KV_HEADS = 2
A_HEAD_DIM = 64
A_WIDTH = A_HEADS * A_HEAD_DIM
A_KV_WIDTH = A_KV_HEADS * A_HEAD_DIM
WINDOW = 128
A_BLOCK = 128
B_GROUPS = 8
B_WIDTH = D_MODEL // 2
B_GROUP_DIM = B_WIDTH // B_GROUPS
CHUNK = 128
EVEN_MIX = A_WIDTH + B_WIDTH
EVEN_SPLITS = [A_WIDTH, A_WIDTH + A_KV_WIDTH, A_WIDTH + 2 * A_KV_WIDTH,
               A_WIDTH + 2 * A_KV_WIDTH + B_WIDTH, A_WIDTH + 2 * A_KV_WIDTH + 2 * B_WIDTH]
EVEN_IN = A_WIDTH + 2 * A_KV_WIDTH + 2 * B_WIDTH + EVEN_MIX

C_HEADS = 16
C_NOPE = 64
C_ROPE = 32
C_V = 64
Q_RANK = 256
KV_RANK = 128
C_WIDTH = C_HEADS * C_V
ODD_SPLITS = [Q_RANK, Q_RANK + KV_RANK, Q_RANK + KV_RANK + C_ROPE]
ODD_IN = Q_RANK + KV_RANK + C_ROPE + C_WIDTH

N_EVEN = (DEPTH + 1) // 2
N_ODD = DEPTH // 2


def rms_norm_2(x, g):
    xf = x.astype(jnp.float32)
    y = xf * lax.rsqrt(jnp.mean(xf * xf, axis=-1, keepdims=True) + NORM_EPS)
    return (y * g.astype(jnp.float32)).astype(x.dtype)

def layer_norm(x, g, b):
    xf = x.astype(jnp.float32)
    mu = jnp.mean(xf, axis=-1, keepdims=True)
    xc = xf - mu
    y = xc * lax.rsqrt(jnp.mean(xc * xc, axis=-1, keepdims=True) + NORM_EPS)
    return (y * g.astype(jnp.float32) + b.astype(jnp.float32)).astype(x.dtype)

def grid_positions(n):
    rows = n // GRID_W
    row = jnp.broadcast_to(jnp.arange(rows, dtype=jnp.float32)[:, None], (rows, GRID_W)).reshape(-1)
    col = jnp.broadcast_to(jnp.arange(GRID_W, dtype=jnp.float32)[None, :], (rows, GRID_W)).reshape(-1)
    return row, col

def rope_1d(x, pos):
    half = x.shape[-1] // 2
    inv = ROPE_BASE ** (-jnp.arange(half, dtype=jnp.float32) / half)
    ang = pos[:, None] * inv[None, :]
    cos = jnp.cos(ang)[None, :, None, :]
    sin = jnp.sin(ang)[None, :, None, :]
    x1, x2 = x[..., :half], x[..., half:]
    return jnp.concatenate([x1 * cos - x2 * sin, x1 * sin + x2 * cos], axis=-1)

def rope_2d(x, row, col):
    d = x.shape[-1] // 2
    xf = x.astype(jnp.float32)
    out = jnp.concatenate([rope_1d(xf[..., :d], row), rope_1d(xf[..., d:], col)], axis=-1)
    return out.astype(x.dtype)

def windowed_sink_gqa(q, k, v, kc, vc, sink):
    B_, S, Hq, Dh = q.shape
    Hkv = k.shape[2]
    G = Hq // Hkv
    blk = A_BLOCK
    nb = S // blk
    C = kc.shape[1]
    scale = Dh ** -0.5
    qb = q.reshape(B_, nb, blk, Hkv, G, Dh)
    pad = ((0, 0), (blk, blk), (0, 0), (0, 0))
    kp = jnp.pad(k, pad).reshape(B_, nb + 2, blk, Hkv, Dh)
    vp = jnp.pad(v, pad).reshape(B_, nb + 2, blk, Hkv, Dh)
    kb = jnp.concatenate([kp[:, :-2], kp[:, 1:-1], kp[:, 2:]], axis=2)
    vb = jnp.concatenate([vp[:, :-2], vp[:, 1:-1], vp[:, 2:]], axis=2)
    qi = jnp.arange(nb)[:, None, None] * blk + jnp.arange(blk)[None, :, None]
    kj = jnp.arange(nb)[:, None, None] * blk - blk + jnp.arange(3 * blk)[None, None, :]
    valid = (jnp.abs(qi - kj) <= WINDOW) & (kj >= 0) & (kj < S)
    s_loc = jnp.einsum('bnqhgd,bnkhd->bhgnqk', qb, kb).astype(jnp.float32) * scale
    s_loc = jnp.where(valid, s_loc, NEG_INF)
    s_ctx = jnp.einsum('bnqhgd,bchd->bhgnqc', qb, kc).astype(jnp.float32) * scale
    s_sink = jnp.broadcast_to(sink.astype(jnp.float32).reshape(1, Hkv, G, 1, 1, 1), s_loc.shape[:-1] + (1,))
    p = jax.nn.softmax(jnp.concatenate([s_loc, s_ctx, s_sink], axis=-1), axis=-1).astype(v.dtype)
    nk = 3 * blk
    o = (jnp.einsum('bhgnqk,bnkhd->bnqhgd', p[..., :nk], vb)
         + jnp.einsum('bhgnqc,bchd->bnqhgd', p[..., nk:nk + C], vc))
    return o.reshape(B_, S, Hq * Dh)

def context_sink_gqa(qc, kc, vc, sink):
    B_, C, Hq, Dh = qc.shape
    Hkv = kc.shape[2]
    G = Hq // Hkv
    scale = Dh ** -0.5
    qg = qc.reshape(B_, C, Hkv, G, Dh)
    s = jnp.einsum('bqhgd,bkhd->bhgqk', qg, kc).astype(jnp.float32) * scale
    s_sink = jnp.broadcast_to(sink.astype(jnp.float32).reshape(1, Hkv, G, 1, 1), s.shape[:-1] + (1,))
    p = jax.nn.softmax(jnp.concatenate([s, s_sink], axis=-1), axis=-1)[..., :C].astype(vc.dtype)
    return jnp.einsum('bhgqk,bkhd->bqhgd', p, vc).reshape(B_, C, Hq * Dh)

def chunk_gmlp(u, v, ln_g, ln_b, w_s, b_s):
    B_, L, _ = v.shape
    n = L // CHUNK
    vn = layer_norm(v, ln_g, ln_b).reshape(B_, n, CHUNK, B_GROUPS, B_GROUP_DIM)
    s = jnp.einsum('gpq,bnqgc->bnpgc', w_s, vn) + jnp.transpose(b_s)[None, None, :, :, None]
    return u * s.reshape(B_, L, B_WIDTH)

def even_layer(hl, hc, w_in, sink, ln_g, ln_b, w_s, b_s, w_out, row, col, need_ctx):
    B_, S, _ = hl.shape
    C = hc.shape[1]
    gelu = lambda t: jax.nn.gelu(t, approximate=False)
    q, k, v, u, vv, gate = jnp.split(hl @ w_in, EVEN_SPLITS, axis=-1)
    q = rope_2d(q.reshape(B_, S, A_HEADS, A_HEAD_DIM), row, col)
    k = rope_2d(k.reshape(B_, S, A_KV_HEADS, A_HEAD_DIM), row, col)
    v = v.reshape(B_, S, A_KV_HEADS, A_HEAD_DIM)
    if need_ctx:
        qc, kc, vc, uc, vvc, gate_c = jnp.split(hc @ w_in, EVEN_SPLITS, axis=-1)
    else:
        kc, vc = jnp.split(hc @ w_in[:, A_WIDTH:A_WIDTH + 2 * A_KV_WIDTH], 2, axis=-1)
    kc = kc.reshape(B_, C, A_KV_HEADS, A_HEAD_DIM)
    vc = vc.reshape(B_, C, A_KV_HEADS, A_HEAD_DIM)
    a = windowed_sink_gqa(q, k, v, kc, vc, sink)
    b = chunk_gmlp(gelu(u), gelu(vv), ln_g, ln_b, w_s, b_s)
    y = (jnp.concatenate([a, b], axis=-1) * jax.nn.silu(gate)) @ w_out
    if need_ctx:
        ac = context_sink_gqa(qc.reshape(B_, C, A_HEADS, A_HEAD_DIM), kc, vc, sink)
        bc = chunk_gmlp(gelu(uc), gelu(vvc), ln_g, ln_b, w_s, b_s)
        yc = (jnp.concatenate([ac, bc], axis=-1) * jax.nn.silu(gate_c)) @ w_out
    else:
        yc = None
    return y, yc

def mla_queries(q_a, q_norm, w_qb, row, col):
    B_, L, _ = q_a.shape
    q = (rms_norm_2(q_a, q_norm) @ w_qb).reshape(B_, L, C_HEADS, C_NOPE + C_ROPE)
    q_nope, q_pe = q[..., :C_NOPE], q[..., C_NOPE:]
    if row is not None:
        q_pe = rope_2d(q_pe, row, col)
    return jnp.concatenate([q_nope, q_pe], axis=-1)

def mla_keys_values(kv_a, k_pe, kv_norm, w_kvb, row, col):
    B_, L, _ = kv_a.shape
    kv = (rms_norm_2(kv_a, kv_norm) @ w_kvb).reshape(B_, L, C_HEADS, C_NOPE + C_V)
    k_nope, v = kv[..., :C_NOPE], kv[..., C_NOPE:]
    k_pe = k_pe[:, :, None, :]
    if row is not None:
        k_pe = rope_2d(k_pe, row, col)
    k = jnp.concatenate([k_nope, jnp.broadcast_to(k_pe, (B_, L, C_HEADS, C_ROPE))], axis=-1)
    return k, v

def block_attention(q, k, v):
    B_, Lq, H, dk = q.shape
    nb = Lq // Q_BLOCK
    scale = dk ** -0.5
    qb = jnp.moveaxis(q.reshape(B_, nb, Q_BLOCK, H, dk), 1, 0)

    def one(qblk):
        s = jnp.einsum('bqhd,bkhd->bhqk', qblk, k).astype(jnp.float32) * scale
        p = jax.nn.softmax(s, axis=-1).astype(v.dtype)
        return jnp.einsum('bhqk,bkhd->bqhd', p, v)

    o = lax.map(one, qb)
    return jnp.moveaxis(o, 0, 1).reshape(B_, Lq, H * v.shape[-1])

def odd_layer(hl, hc, w_in, q_norm, w_qb, kv_norm, w_kvb, w_out, row, col, need_ctx):
    q_a, kv_a, k_pe, gate = jnp.split(hl @ w_in, ODD_SPLITS, axis=-1)
    q = mla_queries(q_a, q_norm, w_qb, row, col)
    k, v = mla_keys_values(kv_a, k_pe, kv_norm, w_kvb, row, col)
    if need_ctx:
        q_ac, kv_ac, k_pec, gate_c = jnp.split(hc @ w_in, ODD_SPLITS, axis=-1)
    else:
        kv_ac, k_pec = jnp.split(hc @ w_in[:, Q_RANK:Q_RANK + KV_RANK + C_ROPE], [KV_RANK], axis=-1)
    kc, vc = mla_keys_values(kv_ac, k_pec, kv_norm, w_kvb, None, None)
    o = block_attention(q, jnp.concatenate([k, kc], axis=1), jnp.concatenate([v, vc], axis=1))
    y = (o * jax.nn.silu(gate)) @ w_out
    if need_ctx:
        qc = mla_queries(q_ac, q_norm, w_qb, None, None)
        oc = block_attention(qc, kc, vc)
        yc = (oc * jax.nn.silu(gate_c)) @ w_out
    else:
        yc = None
    return y, yc

def second_inputs(seed: int = 0) -> dict:
    key = jax.random.key(seed)
    ks = jax.random.split(key, 24)
    f32 = jnp.float32

    def nrm(k, shape, s=1.0):
        return jax.random.normal(k, shape, f32) * s

    def w(k, shape, fan_in, g=1.0):
        return nrm(k, shape, g * fan_in ** -0.5)

    def gain(k, shape):
        return 1.0 + nrm(k, shape, 0.05)

    return {
        'x': nrm(ks[0], (BATCH, SEQ, D_MODEL)),
        'c': nrm(ks[1], (BATCH, D_MODEL)),
        'ctx': nrm(ks[2], (BATCH, CTX_LEN, D_MODEL)),
        'c_ctx': nrm(ks[3], (D_MODEL,)),
        'norm_g': gain(ks[4], (DEPTH, D_MODEL)),
        'w_ada': w(ks[5], (DEPTH, D_MODEL, 3 * D_MODEL), D_MODEL, 0.5),
        'b_ada': nrm(ks[6], (DEPTH, 3 * D_MODEL), 0.02),
        'w_in0': w(ks[7], (N_EVEN, D_MODEL, EVEN_IN), D_MODEL),
        'sink0': nrm(ks[8], (N_EVEN, A_HEADS), 0.5),
        'gm_ln_g': gain(ks[9], (N_EVEN, B_WIDTH)),
        'gm_ln_b': nrm(ks[10], (N_EVEN, B_WIDTH), 0.02),
        'gm_ws': w(ks[11], (N_EVEN, B_GROUPS, CHUNK, CHUNK), CHUNK),
        'gm_bs': 1.0 + nrm(ks[12], (N_EVEN, B_GROUPS, CHUNK), 0.02),
        'w_out0': w(ks[13], (N_EVEN, EVEN_MIX, D_MODEL), EVEN_MIX),
        'w_in1': w(ks[14], (N_ODD, D_MODEL, ODD_IN), D_MODEL),
        'q_norm': gain(ks[15], (N_ODD, Q_RANK)),
        'w_qb': w(ks[16], (N_ODD, Q_RANK, C_HEADS * (C_NOPE + C_ROPE)), Q_RANK),
        'kv_norm': gain(ks[17], (N_ODD, KV_RANK)),
        'w_kvb': w(ks[18], (N_ODD, KV_RANK, C_HEADS * (C_NOPE + C_V)), KV_RANK),
        'w_out1': w(ks[19], (N_ODD, C_WIDTH, D_MODEL), C_WIDTH),
        'final_g': gain(ks[20], (D_MODEL,)),
    }

def second_block(x, c, ctx, c_ctx, norm_g, w_ada, b_ada, w_in0, sink0, gm_ln_g, gm_ln_b, gm_ws, gm_bs,
              w_out0, w_in1, q_norm, w_qb, kv_norm, w_kvb, w_out1, final_g):
    S = x.shape[1]
    row, col = grid_positions(S)
    cond_l = jax.nn.silu(c)[:, None, :]
    cond_c = jax.nn.silu(c_ctx)[None, None, :]
    xc = ctx
    for layer in range(DEPTH):
        need_ctx = layer < DEPTH - 1
        shift_l, scale_l, gate_l = jnp.split(cond_l @ w_ada[layer] + b_ada[layer], 3, axis=-1)
        shift_c, scale_c, gate_c = jnp.split(cond_c @ w_ada[layer] + b_ada[layer], 3, axis=-1)
        hl = rms_norm_2(x, norm_g[layer]) * (1.0 + scale_l) + shift_l
        hc = rms_norm_2(xc, norm_g[layer]) * (1.0 + scale_c) + shift_c
        i = layer // 2
        if layer % 2 == 0:
            yl, yc = even_layer(hl, hc, w_in0[i], sink0[i], gm_ln_g[i], gm_ln_b[i], gm_ws[i], gm_bs[i],
                                w_out0[i], row, col, need_ctx)
        else:
            yl, yc = odd_layer(hl, hc, w_in1[i], q_norm[i], w_qb[i], kv_norm[i], w_kvb[i], w_out1[i],
                               row, col, need_ctx)
        x = x + gate_l * yl
        if need_ctx:
            xc = xc + gate_c * yc
    return rms_norm_2(x, final_g)


def setup_inputs(seed=0):
    out = dict(first_inputs(seed))
    for name, value in second_inputs(seed + 1).items():
        if name != "x":
            out[name + "_2"] = value
    return out


def reference(
    x, c, positions, ada_w, ada_b, pre_norm, post_norm, w_in, gla_w_lr, gla_b_lr, w_br_ret,
    w_br_dsa, w_br_gla, w_out, c_2, ctx_2, c_ctx_2, norm_g_2, w_ada_2, b_ada_2, w_in0_2,
    sink0_2, gm_ln_g_2, gm_ln_b_2, gm_ws_2, gm_bs_2, w_out0_2, w_in1_2, q_norm_2, w_qb_2,
    kv_norm_2, w_kvb_2, w_out1_2, final_g_2,
):
    x = first_block(
        x, c, positions, ada_w, ada_b, pre_norm, post_norm, w_in, gla_w_lr, gla_b_lr, w_br_ret,
        w_br_dsa, w_br_gla, w_out,
    )
    return second_block(
        x, c_2, ctx_2, c_ctx_2, norm_g_2, w_ada_2, b_ada_2, w_in0_2, sink0_2, gm_ln_g_2,
        gm_ln_b_2, gm_ws_2, gm_bs_2, w_out0_2, w_in1_2, q_norm_2, w_qb_2, kv_norm_2, w_kvb_2,
        w_out1_2, final_g_2,
    )


_drawn_inputs = setup_inputs


def setup_inputs(seed=0):
    import zlib

    import numpy as np

    out = dict(_drawn_inputs(seed))
    spreads = {}
    factors = {'pre_norm': 5.281,
     'post_norm': 8.0,
     'gla_w_lr': 8.0,
     'gla_b_lr': 8.0,
     'w_br_dsa': 3.219,
     'ctx_2': 3.865,
     'norm_g_2': 4.465,
     'b_ada_2': 4.242,
     'sink0_2': 8.0,
     'gm_ln_g_2': 8.0,
     'gm_ln_b_2': 8.0,
     'gm_bs_2': 8.0,
     'q_norm_2': 8.0,
     'w_qb_2': 2.836,
     'kv_norm_2': 8.0}
    for name, (base, spread) in spreads.items():
        noise = np.random.default_rng([zlib.crc32(name.encode()), seed]).standard_normal(out[name].shape)
        drawn = base * np.exp(spread * noise) if base else spread * noise
        out[name] = __import__('jax').numpy.asarray(drawn.astype(out[name].dtype))
    for name, factor in factors.items():
        out[name] = (out[name] * factor).astype(out[name].dtype)
    return out
```

```python
from contextlib import ExitStack

import numpy as np
import concourse.bass as bass
from concourse import mybir
from concourse.alu_op_type import AluOpType as ALU

F32 = mybir.dt.float32
I32 = mybir.dt.int32
U8 = mybir.dt.uint8
ACT = mybir.ActivationFunctionType
AX = mybir.AxisListType.X

P = 128
D = 1024
KD = D // P
S = 256
TT = S // P
CT = 256 // P
DEPTH = 2
EPS = 1e-6
NEG = -1e30
TAKEN = -3e38
TOPK = 64
RING = 3
SLOT = 4096

IN1 = {}
_at = 0
for _n, _w in (("ret_q", 256), ("ret_k", 256), ("ret_v", 512), ("ret_g", 512), ("dsa_q", 512),
               ("dsa_k", 128), ("dsa_v", 128), ("dsa_g", 512), ("idx_q", 256), ("idx_k", 64),
               ("idx_w", 4), ("gla_q", 256), ("gla_k", 256), ("gla_v", 512), ("gla_g", 512),
               ("gla_a", 16), ("merge", 3072)):
    IN1[_n] = (_at, _w)
    _at += _w
RANK = 16

MERGES = 6
CH1 = [("idx", KD * 340), ("dsa_q", KD * 512), ("gla_qk", KD * 512), ("dsa_kv", KD * 256),
       ("ret_qk", KD * 512), ("ret_v", KD * 512), ("gla_v", KD * 512), ("ret_g", KD * 512),
       ("dsa_g", KD * 512), ("gla_g", KD * 512)]
for _m in range(MERGES):
    CH1 += [(f"merge{_m}", KD * 512), (f"ada{_m}", KD * 512)]
CH1 += [("br0", 4 * D), ("br1", 4 * D), ("br2", 4 * D), ("out0", KD * 512), ("out1", KD * 512)]
CH0 = [(f"ada{_m}", KD * 512) for _m in range(MERGES)]
CHE = [("e_kv", KD * 256), ("e_q", KD * 512), ("e_u", KD * 512), ("e_vv", KD * 512),
       ("e_g0", KD * 512), ("ada0", KD * 512), ("e_g1", KD * 512), ("ada1", KD * 512), ("ada2", KD * 512),
       ("e_ws", KD * P), ("ada3", KD * 512), ("ada4", KD * 512), ("ada5", KD * 512),
       ("e_o0", KD * 512), ("e_o1", KD * 512)]
CHO = [("o_kv", KD * 160), ("o_q", KD * 256), ("o_g0", KD * 512), ("o_kvb", 2048), ("o_qb", 2 * 1536),
       ("o_g1", KD * 512), ("o_o0", KD * 512), ("o_o1", KD * 512)]
CH2 = CHE + CHO
NT = TT + CT
E_UNITS = [(t, (h,)) for t in range(TT) for h in (0, 2, 4, 6, 1, 3, 5, 7)]
E_UNITS += [(t, hs) for t in range(TT, NT) for hs in ((0, 2), (4, 6), (1, 3), (5, 7))]
E_ADA = {2: 0, 6: 1, 7: 2, 10: 3, 11: 4, 12: 5}
E_LAST = {t: max(i for i, (a, _) in enumerate(E_UNITS) if a == t) for t in range(NT)}
MLA_HEADS, MLA_QK, MLA_NOPE, MLA_V = 16, 96, 64, 64
O_UNITS = [(t, h) for t in range(TT) for h in range(MLA_HEADS)]
MLA_SCALE = MLA_QK ** -0.5
assert len(CH1) % RING == 0 and len(CH0) % RING == 0

HALVES = [1, 2, 4, 8, 16, 32, 64]
LEVELS = ["diag"] + HALVES + ["cross"]
GLA_CHUNK = 64

DSA_UNITS = [(0, (0, 2, 4, 6)), (0, (1, 3, 5, 7)), (1, (0, 2)), (1, (4, 6)), (1, (1, 3)), (1, (5, 7))]
PARTS = [0, 4, 0, 2, 4, 6]

ACT_STEPS = 35
DVE_STEPS = 227
POOL_STEPS = 13
LOADS = 7 * 16
TWO_PI = (6.28125, 0.0019350051879882812, 3.0199159819567e-07)
ROUND = 12582912.0
PI_BELOW = 3.1415925

C_CT, C_ADAB, C_LAY, C_NG, C_QN, C_KVN, C_BS, C_SINK = 0, 24, 120, 156, 172, 174, 175, 183
N_COLS = 191
LAYC = 18
K_DECAY, K_CM, K_RESET, K_FREQ = 0, 1536, 1792, 2048
N_K1 = 2088
K_EROT, K_OROT, K_NEAR, K_LNG, K_LNB, K_FING = 0, 128, 192, 1216, 1728, 2240
N_K2 = 2240


class Units:

    def __init__(self, units, before=None):
        self.start = dict(before.end) if before else {b: 0 for b in range(8)}
        self.at, self.per = {}, {b: 0 for b in range(8)}
        for name, bank in units:
            assert name not in self.at, name
            self.at[name] = (bank, self.per[bank])
            self.per[bank] += 1
        self.end = {b: self.start[b] + self.per[b] for b in range(8)}

    def repeated(self, times):
        self.end = {b: self.start[b] + times * self.per[b] for b in range(8)}
        return self

    def count(self, name, rep=0):
        bank, n = self.at[name]
        return bank, rep * self.per[bank] + (self.start[bank] + n)


def units_of_layer1():
    u = [(f"xT{t}{h}", 2 + 2 * t + h) for t in range(TT) for h in range(2)]
    u += [("gb0", 6), ("gb1", 7)]
    u += [("idx0", 0), ("idx1", 1), ("aT", 5), ("dsa_q0", 0), ("dsa_q1", 1)]
    u += [("qiT", 2), ("kiT", 3), ("gq", 0), ("gk", 1)]
    u += [("s00", 2), ("s01", 3), ("s10", 4), ("s11", 5), ("z", 2)]
    u += [("dsa_kv0", 0), ("dsa_kv1", 1), ("ret_qk0", 0), ("ret_qk1", 1)]
    u += [("dqT0", 2), ("dqT1", 3), ("dkT", 4)]
    u += [("ret_v0", 0), ("ret_v1", 1), ("gla_v0", 0), ("gla_v1", 1), ("rqT", 2), ("rkT", 3)]
    gap = [[("rs0", 4), ("ro0", 6), ("ro1", 7), ("g0_0", 2), ("g0_1", 3)]]
    gap += [[(f"rs{g}", 4), (f"g{g}_0", 2), (f"g{g}_1", 3)] for g in (1, 2, 3)]
    gap += [[("g4_0", 2), ("g4_1", 3)]]
    gap += [[("dl0", 4), ("g5_0", 2), ("g5_1", 3)]]
    gap += [[("dl1", 4), ("dp0", 5), ("g6_0", 2), ("g6_1", 3)]]
    gap += [[("dl2", 4), ("dp1", 5), ("do0", 6), ("g7_0", 2), ("g7_1", 3)]]
    gap += [[("dl3", 4), ("dp2", 5), ("g8_0", 2), ("g8_1", 3)]]
    gap += [[("dl4", 4), ("dp3", 5), ("do1", 7), ("go0", 2), ("go1", 3)]]
    gap += [[("dl5", 4), ("dp4", 5)]]
    gap += [[("dp5", 5), ("retT0", 2), ("retT1", 3)]]
    gap += [[("glaT0", 2), ("glaT1", 3)]]
    gap += [[("dsaT0", 4), ("dsaT1", 5)]]
    proj = ["ret_g0", "ret_g1", "dsa_g0", "dsa_g1", "gla_g0", "gla_g1"]
    for m in range(MERGES):
        proj += [f"merge{m}0", f"merge{m}1"]
    n = 0
    for g, name in enumerate(proj):
        u.append((name, n % 2))
        n += 1
        if g < len(gap):
            u += gap[g]
        if name.startswith("merge") and name.endswith("1") and name[5] != "0":
            u.append((f"ada{int(name[5]) - 1}", n % 2))
            n += 1
    n = 3
    for b in range(3):
        for t in range(TT):
            for h in range(2):
                u.append((f"br{b}{t}{h}", n % 8))
                n += 1
        if b == 0:
            u.append((f"ada{MERGES - 1}", n % 8))
            n += 1
    u += [(f"yT{t}{h}", 4 + 2 * t + h) for t in range(TT) for h in range(2)]
    u += [(f"out{t}{h}", 2 * t + h) for t in range(TT) for h in range(2)]
    return u


def units_of_layer_e():
    n = [0, 0]

    def turn():
        n[0] += 1
        return 2 + (n[0] - 1) % 6

    def proj():
        n[1] += 1
        return (n[1] - 1) % 2

    u = [(f"xT{t}{h}", turn()) for t in range(NT) for h in range(2)]
    u += [(f"gb{v}{h}", turn()) for v in range(2) for h in range(2)]
    for name in ("e_kv", "e_q", "e_u", "e_vv"):
        u += [(f"{name}{t}", proj()) for t in range(NT)]
    u += [(f"ekT{j}", turn()) for j in range(2)] + [(f"eqT{j}", turn()) for j in range(4)]
    for g in range(14):
        if g < 8:
            u.append((f"e_g{g // 4}{g % 4}", proj()))
        if g in E_ADA:
            u.append((f"ada{E_ADA[g]}", proj()))
        if g < 12:
            u += [(f"el{2 * g}", 4), (f"el{2 * g + 1}", 5)]
        if 1 <= g < 13:
            u += [(f"ep{2 * g - 2}", 6), (f"ep{2 * g - 1}", 7)]
        if g >= 2:
            for i in (2 * g - 4, 2 * g - 3):
                t = E_UNITS[i][0]
                if E_UNITS[i - 1][0] != t or i == 0:
                    u.append((f"eo{t}", 2 + t % 2))
        if g == 7:
            u += [(f"gs{j}", proj()) for j in range(4)]
    u += [(f"eyT{t}{h}", turn()) for t in range(NT) for h in range(2)]
    u += [(f"eout{t}{h}", proj()) for t in range(NT) for h in range(2)]
    return u


def units_of_layer_o():
    n = [0, 0]

    def turn():
        n[0] += 1
        return 2 + (n[0] - 1) % 6

    def proj():
        n[1] += 1
        return (n[1] - 1) % 2

    u = [(f"xT{t}{h}", turn()) for t in range(NT) for h in range(2)]
    u += [(f"gb0{h}", turn()) for h in range(2)]
    u += [(f"o_kv{t}", proj()) for t in range(NT)] + [(f"o_q{t}", proj()) for t in range(TT)]
    u += [(f"o_g0{t}", proj()) for t in range(TT)]
    u += [("kvT", turn()), ("kpT", turn())]
    u += [(f"on{h}", turn()) for h in range(MLA_HEADS)]
    u += [(f"ov{t}{h}", turn()) for t in range(NT) for h in range(2)]
    u += [("qaT", turn())]
    u += [(f"oqb{t}{c}", turn()) for t in range(TT) for c in range(3)]
    u += [(f"o_g1{t}", proj()) for t in range(TT)]
    u += [(f"oqT{j}", turn()) for j in range(8)]
    for p in range(16 + 2):
        if p < 16:
            b = (4, 0)[p % 2]
            u += [(f"ml{2 * p}", b), (f"ml{2 * p + 1}", b + 1)]
        if 1 <= p < 17:
            u += [(f"mp{2 * p - 2}", 6), (f"mp{2 * p - 1}", 7)]
        if p >= 2:
            i = 2 * p - 4
            if i % 8 == 0:
                u.append((f"mo{i // 8}", 2 + (i // 8) % 2))
    u += [(f"oyT{t}{h}", turn()) for t in range(TT) for h in range(2)]
    u += [(f"oout{t}{h}", turn()) for t in range(TT) for h in range(2)]
    return u


def build(nc, x, pos, weights, cols, k1, gmask, ident_in, wlr, context, k2, out):
    ctx = ExitStack()
    with ctx:
        def sem(name):
            return ctx.enter_context(nc.semaphore(name))

        def pool_of(stack):
            return lambda name, shape, dt=F32: stack.enter_context(nc.sbuf_tensor(name, shape, dt))

        sb = pool_of(ctx)
        bank = [ctx.enter_context(nc.psum_tensor(f"bank{b}", [P, 512], F32)) for b in range(8)]
        ring = sb("ring", [P, RING, SLOT])
        X = sb("X", [P, TT + CT, D])
        ident = sb("ident", [P, P])
        ones = sb("ones", [P, P])
        col = sb("col", [P, N_COLS])
        cact = sb("cact", [P, KD, 3])
        mod = sb("mod", [P, 24, 2])
        cnow = sb("cnow", [P, KD, 2])
        pw = sb("pw", [P, 2])

        one = ExitStack()
        sb1 = pool_of(one)
        Y = sb1("Y", [P, TT, D])
        hT = sb1("hT", [P, KD, S])
        retqkv = sb1("retqkv", [P, TT, D])
        retg = sb1("retg", [P, TT, 512])
        dsaqkv = sb1("dsaqkv", [P, TT, 768])
        dsag = sb1("dsag", [P, TT, 512])
        idx = sb1("idx", [P, TT, 324])
        glav = sb1("glav", [P, TT, 512])
        glag = sb1("glag", [P, TT, 512])
        G = sb1("G", [P, TT, 3 * D])
        kc = sb1("kc", [P, N_K1])
        gm = sb1("gm", [P, len(HALVES), P], U8)
        wl_all = sb1("wl_all", [RANK, DEPTH, 256])
        wl = sb1("wl", [RANK, 256])
        lay = sb1("lay", [P, LAYC])
        hsc = sb1("hsc", [P, KD])
        hsh = sb1("hsh", [P, KD])
        gpo = sb1("gpo", [P, KD])
        gpb = sb1("gpb", [P, D])
        posi = sb1("posi", [P, TT], I32)
        posf = sb1("posf", [P, TT])
        ang = sb1("ang", [P, TT, 40])
        turn = sb1("turn", [P, TT, 40])
        cosT = sb1("cosT", [P, TT, 40])
        sinT = sb1("sinT", [P, TT, 40])
        st = sb1("st", [P, 96])
        junk = sb1("junk", [P, P])
        cw = sb1("cw", [P, 64])
        ti = sb1("ti", [P, 4, TT * 40])
        kdi = sb1("kdi", [P, TT, 2, 64])
        kdd = sb1("kdd", [P, TT, 2, 2, 64])
        qiT = sb1("qiT", [P, 2, S])
        kiT = sb1("kiT", [P, S])
        qdT = sb1("qdT", [P, 4, S])
        kdT = sb1("kdT", [P, 2, S])
        qrT = sb1("qrT", [P, 2, S])
        krT = sb1("krT", [P, 2, S])
        gqT = sb1("gqT", [P, 2, S])
        gkT = sb1("gkT", [P, 2, S])
        bcum = sb1("bcum", [P, 2, S])
        KL = sb1("KL", [P, 2, 2, S])
        AT = sb1("AT", [P, 2, 3, 2, P])
        RS = sb1("RS", [P, 2, 384])
        L = sb1("L", [P, 2, 512])
        PT = sb1("PT", [P, 2, 512])
        sc = sb1("sc", [P, 384])
        wk = sb1("wk", [P, 384])
        m8 = sb1("m8", [P, 8])
        mx = sb1("mx", [P, TT, 8])
        sm = sb1("sm", [P, TT, 8])
        aT = sb1("aT", [RANK, S])
        retT = X[:, 2, :].rearrange("p (k s) -> p k s", k=4)
        dsaT = X[:, 3, :].rearrange("p (k s) -> p k s", k=4)
        glaT = dsaqkv[:].rearrange("p t c -> p (t c)")[:, 0:1024].rearrange("p (k s) -> p k s", k=4)
        branchT = [retT, dsaT, glaT]
        DG = G[:, 0, 0:D].rearrange("p (k s) -> p k s", k=KD)
        RI = G[:, 0, D:D + 1536]
        Z = G[:, 1, 0:512].rearrange("p (f s) -> p f s", f=2)
        AZ = G[:, 1, 512:1024].rearrange("p (f s) -> p f s", f=2)
        LG = G[:, 1, 1024:1536].rearrange("p (f s) -> p f s", f=2)
        Yf = Y[:].rearrange("p t d -> p (t d)")
        msum = retqkv[:].rearrange("p b (v c) -> p b v c", v=2)
        rt = Yf.rearrange("p (q n) -> p q n", q=4)
        gmf = Yf[:, 0:len(HALVES) * P].rearrange("p (n c) -> p n c", n=len(HALVES))
        E = [Yf[:, 512 * i:512 * i + 512].rearrange("p (f s) -> p f s", f=2) for i in range(2)]
        QL = [Yf[:, 1024 + 512 * i:1536 + 512 * i].rearrange("p (f s) -> p f s", f=2) for i in range(2)]
        decay = kc[:, K_DECAY:K_DECAY + 1536].rearrange("p (h c) -> p h c", h=4)
        cm = kc[:, K_CM:K_CM + 256]
        reset = kc[:, K_RESET:K_RESET + 256]
        freq = kc[:, K_FREQ:K_FREQ + 40]
        one.close()

        two = ExitStack()
        sb2 = pool_of(two)
        Y2 = sb2("Y2", [P, NT, D])
        hT2 = sb2("hT2", [P, KD, NT * P])
        L2 = sb2("L2", [P, 4, 512])
        PT2 = sb2("PT2", [P, 4, 512])
        gbr = sb2("gbr", [P, 2, D])
        hsc2 = sb2("hsc2", [P, 2, KD])
        hsh2 = sb2("hsh2", [P, 2, KD])
        st2 = sb2("st2", [P, 64])
        mx2 = sb2("mx2", [P, NT, 16])
        sm2 = sb2("sm2", [P, NT, 16])
        es2 = sb2("es2", [P, NT, 8])
        r2 = sb2("r2", [P, NT, 16])
        nsink = sb2("nsink", [P, 8])
        kk = sb2("kk", [P, N_K2])
        lay_e, lay_o = ExitStack(), ExitStack()
        sbe = pool_of(lay_e)
        eqk = sbe("eqk", [P, NT, 640])
        ev = sbe("ev", [P, NT, P])
        eu = sbe("eu", [P, NT, 512])
        evv = sbe("evv", [P, NT, 512])
        eg = sbe("eg", [P, NT, D])
        eqT = sbe("eqT", [P, 4, NT * P])
        ekT = sbe("ekT", [P, 2, NT * P])
        ekd = sbe("ekd", [P, NT, 2, 2, 64])
        ert = sbe("ert", [P, 4, 320])
        lay_e.close()
        sbo = pool_of(lay_o)
        okT = sbo("okT", [MLA_QK, MLA_HEADS, NT * P])
        oqT = sbo("oqT", [MLA_QK, MLA_HEADS, S])
        ova = sbo("ova", [P, NT, D])
        og = sbo("og", [P, TT, D])
        lay_o.close()
        two.close()
        q2 = Y2[:].rearrange("p t d -> p (t d)")[:, 0:TT * 1536].rearrange("p (t c) -> p t c", t=TT)
        DG2 = [eu[:].rearrange("p t d -> p (t d)")[:, D * v:D * v + D].rearrange("p (k c) -> p k c", k=KD) for v in range(2)]
        DG3 = og[:, 0, :].rearrange("p (k c) -> p k c", k=KD)
        e_rot = kk[:, K_EROT:K_EROT + 128].rearrange("p (q t c) -> p q t c", q=2, t=TT)
        o_rot = kk[:, K_OROT:K_OROT + 64].rearrange("p (q t c) -> p q t c", q=2, t=TT)
        near = kk[:, K_NEAR:K_NEAR + 1024].rearrange("p (t c) -> p t c", t=TT)
        lng, lnb = kk[:, K_LNG:K_LNG + 512], kk[:, K_LNB:K_LNB + 512]
        fing = gbr[:, 1, :]
        etmp = evv[:, 0, :]
        msum2 = [ekd[:].rearrange("p t a b c -> p (t a b c)").rearrange("p (v c) -> p v c", v=2),
                 ert[:].rearrange("p q c -> p (q c)")[:, 0:D].rearrange("p (v c) -> p v c", v=2)]
        otmp = Y2[:].rearrange("p t d -> p (t d)")[:, TT * 1536:TT * 1536 + 512]
        ort = near.rearrange("p t c -> p (t c)").rearrange("p (q c) -> p q c", q=4)
        okv = kk[:, K_LNG:K_LNG + NT * 160].rearrange("p (t c) -> p t c", t=NT)
        okp = kk[:, K_LNG + NT * 160:K_LNG + NT * (160 + MLA_QK)].rearrange("p (t c) -> p t c", t=NT)
        kvT, kpe = X[:, TT, 0:NT * P], X[0:MLA_QK, TT, NT * P:2 * NT * P]
        oqa = X[:, TT + 1, 0:TT * 256].rearrange("p (t c) -> p t c", t=TT)
        qaT = X[:, TT + 1, 512:512 + 2 * S].rearrange("p (k s) -> p k s", k=2)

        bank_full = [sem(f"bank_full{b}") for b in range(8)]
        bank_free = [sem(f"bank_free{b}") for b in range(8)]
        slot_full = [sem(f"slot_full{s}") for s in range(RING)]
        loaded = sem("loaded")
        stored = sem("stored")
        E_ = {}

        def event(name):
            if name not in E_:
                E_[name] = sem(name)
            return E_[name]

        pro = Units([(f"ada{m}", m % 2) for m in range(MERGES)])
        lay1 = Units(units_of_layer1(), pro).repeated(DEPTH)
        le = Units(units_of_layer_e(), lay1)
        lo = Units(units_of_layer_o(), le)
        BASE2 = len(CH0) + DEPTH * len(CH1)

        def last1(c):
            name = CH1[c][0]
            if name == "idx":
                return "aT"
            if name == "gla_qk":
                return "gk"
            if name.startswith("br"):
                return name + "11"
            if name.startswith("out"):
                return "out1" + name[3]
            return name + "1"

        def filled(eng, u, name, rep=0):
            b, n = u.count(name, rep)
            eng.wait_ge(bank_full[b], n + 1)
            return bank[b]

        def emptied(eng, u, name, rep=0):
            b, n = u.count(name, rep)
            eng.wait_ge(bank_free[b], n + 2)

        def free(u, name):
            return bank_free[u.at[name][0]]

        def shape_like(ps, dst):
            return ps if len(dst.shape) == 2 else ps.rearrange("p (a b) -> p a b", a=dst.shape[1])

        def counted(name, got, want):
            assert got == want, f"{name} has to be {got}"

        block = ctx.enter_context(nc.Block())

        @block.sync
        def _(sp):
            def load(n, slot, width):
                sp.dma_start(ring[:, slot, 0:width], weights[n][:, 0:width]).then_inc(slot_full[slot], 16)

            for c in range(RING):
                load(c, c, CH0[c][1])
            for c in range(RING, len(CH0)):
                sp.wait_ge(event("ada_sum"), c - RING + 1)
                load(c, c % RING, CH0[c][1])
            with sp.Fori(0, DEPTH) as l:
                for c, (name, width) in enumerate(CH1):
                    if c < RING:
                        sp.wait_ge(event("ada_sum"), len(CH0) - RING + c + 1)
                        b, n = lay1.count(("out00", "out10", "out11")[c])
                        assert n + 1 - lay1.per[b] == lay1.start[b]
                        sp.wait_ge(bank_full[b], l * lay1.per[b] + lay1.start[b])
                    elif CH1[c - RING][0].startswith("ada"):
                        sp.wait_ge(event("ada_sum"), l * MERGES + (MERGES + int(CH1[c - RING][0][3]) + 1))
                    else:
                        filled(sp, lay1, last1(c - RING), l)
                    sp.dma_start(ring[:, c % RING, 0:width],
                                 weights[l * len(CH1) + (len(CH0) + c)][:, 0:width]).then_inc(slot_full[c % RING], 16)

            last2 = []
            for name, _ in CHE:
                last2.append((le, "gs3" if name == "e_ws" else name if name[0] == "a" else
                              f"eout{NT - 1}{name[3]}" if name[2] == "o" else f"{name}{NT - 1}"))
            for name, _ in CHO:
                last2.append((lo, {"o_kv": f"o_kv{NT - 1}", "o_q": "o_q1", "o_kvb": f"ov{NT - 1}1", "o_qb": "oqb12",
                                   "o_g0": "o_g01", "o_g1": "o_g11", "o_o0": "oout10", "o_o1": "oout11"}[name]))
            for c, (name, width) in enumerate(CH2):
                if c < RING:
                    filled(sp, lay1, ("out00", "out10", "out11")[c], DEPTH - 1)
                elif CH2[c - RING][0].startswith("ada"):
                    sp.wait_ge(event("ada_sum"), (DEPTH + 1) * MERGES + int(CH2[c - RING][0][3]) + 1)
                else:
                    filled(sp, last2[c - RING][0], last2[c - RING][1])
                load(BASE2 + c, (BASE2 + c) % RING, width)
                if c == 0:
                    sp.dma_start(X[:, TT:NT, :], context.rearrange("(t p) d -> p t d", p=P)).then_inc(event("ctx_in"), 16)
                if c == RING - 1:
                    sp.wait_ge(event("x_ready"), DEPTH * TT + 1)
                    sp.dma_start(kk[:], k2[:, 0:N_K2]).then_inc(event("ctx_in"), 16)
            sp.wait_ge(event("x2_ready"), NT)
            sp.dma_start(fing, k2[:, N_K2:N_K2 + D]).then_inc(event("fing_in"), 16)
            for t in range(TT):
                sp.wait_ge(event("out_ready"), t + 1)
                sp.dma_start(out[0, t * P:(t + 1) * P, :], Y2[:, t, :]).then_inc(stored, 16)
            sp.wait_ge(stored, 16 * TT)

        def arrived(eng, chunks, c, base, rep=0):
            eng.wait_ge(slot_full[c % RING], rep * (16 * len(chunks) // RING) + 16 * ((base + c) // RING + 1))

        @block.tensor
        def _(pe):
            def begin(u, name, rep=0):
                b, n = u.count(name, rep)
                pe.wait_ge(bank_free[b], n + 1)
                return bank[b]

            def done(u, name, ins):
                ins.then_inc(bank_full[u.at[name][0]], 1)

            def ada(u, name, sums, vectors, count, rep=0):
                pe.wait_ge(event("ada_sum"), count)
                ps = begin(u, name, rep)
                for j in range(4):
                    for v in range(vectors):
                        at = 64 * (vectors * j + v)
                        mm = pe.matmul(ps[:, at:at + 64], sums[:, v, j * P:(j + 1) * P], ones[:, 0:64],
                                       start=True, stop=True)
                done(u, name, mm)

            def turn_blocks(ps, blocks):
                for i, blk in enumerate(blocks):
                    n = blk.shape[1]
                    mm = pe.transpose(ps[0:n, i * P:(i + 1) * P], blk, ident[:])
                return mm

            def project(u, name, slot, t, width, rep, stride=None, w0=0):
                stride = stride or width
                ps = begin(u, name, rep)
                for k in range(KD):
                    mm = pe.matmul(ps[:, 0:width], hT[:, k, t * P:(t + 1) * P],
                                   ring[:, slot, k * stride + w0:k * stride + w0 + width],
                                   start=(k == 0), stop=(k == KD - 1))
                done(u, name, mm)

            for m in range(MERGES):
                ada(pro, f"ada{m}", msum[:, m % 2], 1, m + 1)

            with pe.Fori(0, DEPTH) as l:
                u = lay1
                chunk = {n: c for c, (n, _) in enumerate(CH1)}

                def landed(name):
                    arrived(pe, CH1, chunk[name], len(CH0), l)
                    return chunk[name] % RING

                for t in range(TT):
                    pe.wait_ge(event("xn_ready"), l * TT + (t + 1))
                    for h in range(2):
                        ps = begin(u, f"xT{t}{h}", l)
                        done(u, f"xT{t}{h}", turn_blocks(ps, [Y[:, t, (4 * h + i) * P:(4 * h + i + 1) * P] for i in range(4)]))
                pe.wait_ge(event("diag_ready"), l + 1)
                for h in range(2):
                    ps = begin(u, f"gb{h}", l)
                    done(u, f"gb{h}", pe.matmul(ps[:, :], ones[:], DG[:, 4 * h:4 * h + 4, :], start=True, stop=True))
                for t in range(TT):
                    for h in range(2):
                        emptied(pe, u, f"xT{t}{h}", l)

                slot = landed("idx")
                for t in range(TT):
                    project(u, f"idx{t}", slot, t, 324, l, stride=340)
                ps = begin(u, "aT", l)
                for k in range(KD):
                    mm = pe.matmul(ps[0:RANK, 0:S], ring[:, slot, k * 340 + 324:k * 340 + 340], hT[:, k, :],
                                   start=(k == 0), stop=(k == KD - 1))
                done(u, "aT", mm)
                slot = landed("dsa_q")
                for t in range(TT):
                    project(u, f"dsa_q{t}", slot, t, 512, l)

                pe.wait_ge(event("idx_rot"), l + 1)
                ps = begin(u, "qiT", l)
                done(u, "qiT", turn_blocks(ps, [idx[:, t, j * P:(j + 1) * P] for j in range(2) for t in range(TT)]))
                ps = begin(u, "kiT", l)
                done(u, "kiT", turn_blocks(ps, [kdi[:, t, :, :].rearrange("p a b -> p (a b)") for t in range(TT)]))

                slot = landed("gla_qk")
                for i, name in enumerate(("gq", "gk")):
                    ps = begin(u, name, l)
                    for f in range(2):
                        for k in range(KD):
                            at = k * 512 + (2 * i + f) * P
                            mm = pe.matmul(ps[:, f * S:(f + 1) * S], ring[:, slot, at:at + P], hT[:, k, :],
                                           start=(k == 0), stop=(k == KD - 1))
                    done(u, name, mm)

                emptied(pe, u, "qiT", l)
                emptied(pe, u, "kiT", l)
                for t in range(TT):
                    for r in range(2):
                        ps = begin(u, f"s{t}{r}", l)
                        n = P * (t + 1)
                        for j in range(2):
                            mm = pe.matmul(ps[:, j * n:(j + 1) * n], qiT[64 * r:64 * r + 64, j, t * P:(t + 1) * P],
                                           kiT[64 * r:64 * r + 64, 0:n], start=True, stop=True)
                        done(u, f"s{t}{r}", mm)
                emptied(pe, u, "aT", l)
                pe.wait_ge(event("wl_ready"), l + 1)
                ps = begin(u, "z", l)
                for f in range(2):
                    mm = pe.matmul(ps[:, f * S:(f + 1) * S], wl[:, f * P:(f + 1) * P], aT[:, :], start=True, stop=True)
                done(u, "z", mm)

                slot = landed("dsa_kv")
                for t in range(TT):
                    project(u, f"dsa_kv{t}", slot, t, 256, l)
                slot = landed("ret_qk")
                for t in range(TT):
                    project(u, f"ret_qk{t}", slot, t, 512, l)
                pe.wait_ge(event("dsa_rot"), l + 1)
                for i in range(2):
                    ps = begin(u, f"dqT{i}", l)
                    done(u, f"dqT{i}", turn_blocks(ps, [dsaqkv[:, t, (2 * i + j) * P:(2 * i + j + 1) * P]
                                                        for j in range(2) for t in range(TT)]))
                ps = begin(u, "dkT", l)
                done(u, "dkT", turn_blocks(ps, [kdd[:, t, j, :, :].rearrange("p a b -> p (a b)")
                                                for j in range(2) for t in range(TT)]))
                for name in ("ret_v", "gla_v"):
                    slot = landed(name)
                    for t in range(TT):
                        project(u, f"{name}{t}", slot, t, 512, l)
                pe.wait_ge(event("ret_rot"), l + 1)
                for name, at in (("rqT", 0), ("rkT", 256)):
                    ps = begin(u, name, l)
                    done(u, name, turn_blocks(ps, [retqkv[:, t, at + j * P:at + (j + 1) * P]
                                                   for j in range(2) for t in range(TT)]))
                emptied(pe, u, "rqT", l)
                emptied(pe, u, "rkT", l)

                def ret_scores(h):
                    r, j = h % 2, h // 2
                    ps = begin(u, f"rs{h}", l)
                    pe.matmul(ps[:, 0:S], krT[64 * r:64 * r + 64, j, 0:P], qrT[64 * r:64 * r + 64, j, 0:S],
                              start=True, stop=True)
                    done(u, f"rs{h}", pe.matmul(ps[:, S:S + P], krT[64 * r:64 * r + 64, j, P:S],
                                                qrT[64 * r:64 * r + 64, j, P:S], start=True, stop=True))

                def ret_values(h):
                    emptied(pe, u, f"rs{h}", l)
                    if h == 0:
                        begin(u, "ro0", l)
                        begin(u, "ro1", l)
                    v = [retqkv[:, t, 512 + h * P:512 + (h + 1) * P] for t in range(TT)]
                    o = [bank[u.at[f"ro{t}"][0]][:, h * P:(h + 1) * P] for t in range(TT)]
                    m0 = pe.matmul(o[0], RS[:, h % 2, 0:P], v[0], start=True, stop=True)
                    pe.matmul(o[1], RS[:, h % 2, P:2 * P], v[0], start=True, stop=False)
                    m1 = pe.matmul(o[1], RS[:, h % 2, 2 * P:3 * P], v[1], start=False, stop=True)
                    if h == 3:
                        done(u, "ro0", m0)
                        done(u, "ro1", m1)

                def gla_scores(i):
                    if i:
                        pe.wait_ge(event("gql"), l * 8 + i)
                        pe.wait_ge(event("gkl"), l * 8 + i)
                    else:
                        emptied(pe, u, "gq", l)
                        emptied(pe, u, "gk", l)
                    q, k = (QL[i % 2], KL[:, i % 2]) if i else (gqT, gkT)
                    pairs = [(1, 0)] if LEVELS[i] == "cross" else [(t, t) for t in range(TT)]
                    for r in range(2):
                        ps = begin(u, f"g{i}_{r}", l)
                        n = 0
                        for tq, tk in pairs:
                            for j in range(2):
                                mm = pe.matmul(ps[:, n:n + P], k[64 * r:64 * r + 64, j, tk * P:(tk + 1) * P],
                                               q[64 * r:64 * r + 64, j, tq * P:(tq + 1) * P], start=True, stop=True)
                                n += P
                        done(u, f"g{i}_{r}", mm)

                def gla_values():
                    pe.wait_ge(event("at_ready"), l + 1)
                    ps0, ps1 = begin(u, "go0", l), begin(u, "go1", l)
                    for h in range(4):
                        r, j = h % 2, h // 2
                        v = [glav[:, t, h * P:(h + 1) * P] for t in range(TT)]
                        c = slice(h * P, (h + 1) * P)
                        m0 = pe.matmul(ps0[:, c], AT[:, r, 0, j, :], v[0], start=True, stop=True)
                        if h == 3:
                            done(u, "go0", m0)
                        pe.matmul(ps1[:, c], AT[:, r, 2, j, :], v[0], start=True, stop=False)
                        m1 = pe.matmul(ps1[:, c], AT[:, r, 1, j, :], v[1], start=False, stop=True)
                    done(u, "go1", m1)

                def dsa_logits(i):
                    if i == 0:
                        for name in ("dqT0", "dqT1", "dkT"):
                            emptied(pe, u, name, l)
                    t, heads = DSA_UNITS[i]
                    ps = begin(u, f"dl{i}", l)
                    n = P * (t + 1)
                    for a, h in enumerate(heads):
                        r = 64 * (h % 2)
                        mm = pe.matmul(ps[:, a * n:(a + 1) * n], qdT[r:r + 64, h // 2, t * P:(t + 1) * P],
                                       kdT[r:r + 64, h // 4, 0:n], start=True, stop=True)
                    done(u, f"dl{i}", mm)

                def dsa_turn(i):
                    pe.wait_ge(event("dexp"), l * 6 + (i + 1))
                    ps = begin(u, f"dp{i}", l)
                    done(u, f"dp{i}", turn_blocks(ps, [L[:, i % 2, b * P:(b + 1) * P] for b in range(4)]))

                def dsa_values(i):
                    emptied(pe, u, f"dp{i}", l)
                    t, heads = DSA_UNITS[i]
                    if i in (0, 2):
                        begin(u, f"do{t}", l)
                    o = bank[u.at[f"do{t}"][0]]
                    for a, h in enumerate(heads):
                        for b in range(t + 1):
                            at = (a * (t + 1) + b) * P
                            mm = pe.matmul(o[:, h * 64:(h + 1) * 64], PT[:, i % 2, at:at + P],
                                           dsaqkv[:, b, 640 + (h // 4) * 64:704 + (h // 4) * 64],
                                           start=(b == 0), stop=(b == t))
                    if i in (1, 5):
                        done(u, f"do{t}", mm)

                def turn_branch(name, src, ready):
                    for t in range(TT):
                        pe.wait_ge(event(ready), l * TT + (t + 1))
                        ps = begin(u, f"{name}{t}", l)
                        done(u, f"{name}{t}", turn_blocks(ps, [src[:, t, j * P:(j + 1) * P] for j in range(4)]))

                def gap(g):
                    if g < 4:
                        ret_scores(g)
                    if 1 <= g <= 4:
                        ret_values(g - 1)
                    if 5 <= g <= 10:
                        dsa_logits(g - 5)
                    if 6 <= g <= 11:
                        dsa_turn(g - 6)
                    if 7 <= g <= 12:
                        dsa_values(g - 7)
                    if g < len(LEVELS):
                        gla_scores(g)
                    if g == 9:
                        gla_values()
                    if g == 11:
                        turn_branch("retT", retg, "ret_ready")
                    if g == 12:
                        turn_branch("glaT", glag, "gla_ready")
                    if g == 13:
                        turn_branch("dsaT", dsag, "dsa_ready")

                g = 0
                for name in ("ret_g", "dsa_g", "gla_g") + tuple(f"merge{m}" for m in range(MERGES)):
                    slot = landed(name)
                    for t in range(TT):
                        project(u, f"{name}{t}", slot, t, 512, l)
                        gap(g)
                        g += 1
                    if name.startswith("merge") and name != "merge0":
                        m = int(name[5]) - 1
                        ada(u, f"ada{m}", msum[:, m % 2], 2, l * MERGES + (MERGES + m + 1), l)

                for b, name in enumerate(("retT", "dsaT", "glaT")):
                    slot = landed(f"br{b}")
                    for t in range(TT):
                        emptied(pe, u, f"{name}{t}", l)
                        for h in range(2):
                            ps = begin(u, f"br{b}{t}{h}", l)
                            for k in range(4):
                                mm = pe.matmul(ps[:, :], branchT[b][:, k, t * P:(t + 1) * P],
                                               ring[:, slot, k * D + h * 512:k * D + h * 512 + 512],
                                               start=(k == 0), stop=(k == 3))
                            done(u, f"br{b}{t}{h}", mm)
                    if b == 0:
                        m = MERGES - 1
                        ada(u, f"ada{m}", msum[:, m % 2], 2, l * MERGES + (MERGES + m + 1), l)
                for t in range(TT):
                    pe.wait_ge(event("y_ready"), l * TT + (t + 1))
                    for h in range(2):
                        ps = begin(u, f"yT{t}{h}", l)
                        done(u, f"yT{t}{h}", turn_blocks(ps, [Y[:, t, (4 * h + i) * P:(4 * h + i + 1) * P] for i in range(4)]))
                slots = [landed("out0"), landed("out1")]
                for t in range(TT):
                    for h in range(2):
                        emptied(pe, u, f"yT{t}{h}", l)
                    for h in range(2):
                        project(u, f"out{t}{h}", slots[h], t, 512, l)

            def landed2(name):
                c = [n for n, _ in CH2].index(name)
                arrived(pe, CH2, c, BASE2)
                return c % RING

            def project2(u, name, slot, t, width):
                ps = begin(u, name)
                for k in range(KD):
                    mm = pe.matmul(ps[:, 0:width], hT2[:, k, t * P:(t + 1) * P],
                                   ring[:, slot, k * width:(k + 1) * width], start=(k == 0), stop=(k == KD - 1))
                done(u, name, mm)

            def turn_x2(u, first):
                for t in range(NT):
                    pe.wait_ge(event("h2_ready"), first + t + 1)
                    for h in range(2):
                        ps = begin(u, f"xT{t}{h}")
                        done(u, f"xT{t}{h}", turn_blocks(ps, [Y2[:, t, (4 * h + i) * P:(4 * h + i + 1) * P] for i in range(4)]))

            def turned_x2(u):
                for t in range(NT):
                    for h in range(2):
                        emptied(pe, u, f"xT{t}{h}")

            u = le
            turn_x2(u, 0)
            for v in range(2):
                pe.wait_ge(event("diag_ready"), DEPTH + v + 1)
                for h in range(2):
                    ps = begin(u, f"gb{v}{h}")
                    done(u, f"gb{v}{h}", pe.matmul(ps[:, :], ones[:], DG2[v][:, 4 * h:4 * h + 4, :], start=True, stop=True))
            turned_x2(u)
            for name, width in CHE[0:4]:
                slot = landed2(name)
                for t in range(NT):
                    project2(u, f"{name}{t}", slot, t, width // KD)
            pe.wait_ge(event("e_rot"), 1)
            for t in range(NT):
                emptied(pe, u, f"e_q{t}")
                emptied(pe, u, f"e_kv{t}")
            for j in range(2):
                ps = begin(u, f"ekT{j}")
                done(u, f"ekT{j}", turn_blocks(ps, [ekd[:, t, j].rearrange("p a b -> p (a b)") for t in range(NT)]))
            for j in range(4):
                ps = begin(u, f"eqT{j}")
                done(u, f"eqT{j}", turn_blocks(ps, [eqk[:, t, j * P:(j + 1) * P] for t in range(NT)]))

            def e_logits(i):
                t, heads = E_UNITS[i]
                k0 = 0 if t < TT else TT * P
                n = NT * P - k0
                ps = begin(u, f"el{i}")
                for a, h in enumerate(heads):
                    r = 64 * (h % 2)
                    mm = pe.matmul(ps[:, a * n:(a + 1) * n], eqT[r:r + 64, h // 2, t * P:(t + 1) * P],
                                   ekT[r:r + 64, h // 4, k0:k0 + n], start=True, stop=True)
                done(u, f"el{i}", mm)

            def e_turn(i):
                if E_UNITS[i][0] < TT:
                    pe.wait_ge(event("e_exp"), i + 1)
                else:
                    emptied(pe, u, f"el{i}")
                ps = begin(u, f"ep{i}")
                done(u, f"ep{i}", turn_blocks(ps, [L2[:, i % 4, b * P:(b + 1) * P] for b in range(4)]))

            def e_values(i):
                emptied(pe, u, f"ep{i}")
                t, heads = E_UNITS[i]
                b0 = 0 if t < TT else TT
                nb = NT - b0
                if i == 0 or E_UNITS[i - 1][0] != t:
                    begin(u, f"eo{t}")
                o = bank[u.at[f"eo{t}"][0]]
                for a, h in enumerate(heads):
                    for b in range(nb):
                        mm = pe.matmul(o[:, h * 64:(h + 1) * 64], PT2[:, i % 4, (a * nb + b) * P:(a * nb + b + 1) * P],
                                       ev[:, b0 + b, (h // 4) * 64:(h // 4) * 64 + 64], start=(b == 0), stop=(b == nb - 1))
                if i == E_LAST[t]:
                    done(u, f"eo{t}", mm)

            for j in range(2):
                emptied(pe, u, f"ekT{j}")
            for j in range(4):
                emptied(pe, u, f"eqT{j}")
            for g in range(14):
                if g < 8:
                    name = f"e_g{g // 4}"
                    slot = landed2(name)
                    project2(u, f"{name}{g % 4}", slot, g % 4, 512)
                if g in E_ADA:
                    m = E_ADA[g]
                    ada(u, f"ada{m}", msum2[m % 2], 2, (DEPTH + 1) * MERGES + m + 1)
                if g < 12:
                    e_logits(2 * g)
                    e_logits(2 * g + 1)
                if 1 <= g < 13:
                    e_turn(2 * g - 2)
                    e_turn(2 * g - 1)
                if g >= 2:
                    e_values(2 * g - 4)
                    e_values(2 * g - 3)
                if g == 7:
                    slot = landed2("e_ws")
                    pe.wait_ge(event("ln_ready"), NT)
                    for j in range(4):
                        ps = begin(u, f"gs{j}")
                        for a in range(2):
                            q = 2 * j + a
                            mm = pe.matmul(ps[:, a * 256:(a + 1) * 256].rearrange("p (t c) -> p t c", t=NT),
                                           ring[:, slot, q * P:(q + 1) * P], evv[:, :, q * 64:(q + 1) * 64],
                                           start=True, stop=True)
                        done(u, f"gs{j}", mm)
            for t in range(NT):
                pe.wait_ge(event("em_ready"), t + 1)
                for h in range(2):
                    ps = begin(u, f"eyT{t}{h}")
                    done(u, f"eyT{t}{h}", turn_blocks(ps, [eg[:, t, (4 * h + i) * P:(4 * h + i + 1) * P] for i in range(4)]))
            slots = [landed2("e_o0"), landed2("e_o1")]
            for t in range(NT):
                for h in range(2):
                    emptied(pe, u, f"eyT{t}{h}")
                for h in range(2):
                    project2(u, f"eout{t}{h}", slots[h], t, 512)

            u = lo
            turn_x2(u, NT)
            pe.wait_ge(event("diag_ready"), DEPTH + 3)
            for h in range(2):
                ps = begin(u, f"gb0{h}")
                done(u, f"gb0{h}", pe.matmul(ps[:, :], ones[:], DG3[:, 4 * h:4 * h + 4, :], start=True, stop=True))
            turned_x2(u)
            slot = landed2("o_kv")
            for t in range(NT):
                project2(u, f"o_kv{t}", slot, t, 160)
            slot = landed2("o_q")
            for t in range(TT):
                project2(u, f"o_q{t}", slot, t, 256)
            slot = landed2("o_g0")
            for t in range(TT):
                project2(u, f"o_g0{t}", slot, t, 512)
            pe.wait_ge(event("okv_ready"), 1)
            ps = begin(u, "kvT")
            done(u, "kvT", turn_blocks(ps, [okv[:, t, 0:P] for t in range(NT)]))
            pe.wait_ge(event("okp_ready"), 1)
            ps = begin(u, "kpT")
            done(u, "kpT", turn_blocks(ps, [okp[:, t, :] for t in range(NT)]))
            emptied(pe, u, "kvT")
            slot = landed2("o_kvb")
            for h in range(MLA_HEADS):
                ps = begin(u, f"on{h}")
                done(u, f"on{h}", pe.matmul(ps[0:MLA_NOPE, :], ring[:, slot, h * MLA_NOPE:(h + 1) * MLA_NOPE],
                                            kvT[:, :], start=True, stop=True))
            for t in range(NT):
                for h in range(2):
                    ps = begin(u, f"ov{t}{h}")
                    done(u, f"ov{t}{h}", pe.matmul(ps[:, :], kvT[:, t * P:(t + 1) * P],
                                                   ring[:, slot, D + h * 512:D + h * 512 + 512], start=True, stop=True))
            pe.wait_ge(event("oqa_ready"), 1)
            ps = begin(u, "qaT")
            done(u, "qaT", turn_blocks(ps, [oqa[:, t, k * P:(k + 1) * P] for k in range(2) for t in range(TT)]))
            emptied(pe, u, "qaT")
            slot = landed2("o_qb")
            for t in range(TT):
                for c in range(3):
                    ps = begin(u, f"oqb{t}{c}")
                    for k in range(2):
                        mm = pe.matmul(ps[:, :], qaT[:, k, t * P:(t + 1) * P],
                                       ring[:, slot, k * 1536 + c * 512:k * 1536 + c * 512 + 512],
                                       start=(k == 0), stop=(k == 1))
                    done(u, f"oqb{t}{c}", mm)
            slot = landed2("o_g1")
            for t in range(TT):
                project2(u, f"o_g1{t}", slot, t, 512)
            pe.wait_ge(event("oq_rot"), 1)
            for j in range(8):
                ps = begin(u, f"oqT{j}")
                done(u, f"oqT{j}", turn_blocks(ps, [q2[:, t, h * MLA_QK:(h + 1) * MLA_QK] for h in (2 * j, 2 * j + 1)
                                                    for t in range(TT)]))
            for j in range(8):
                emptied(pe, u, f"oqT{j}")
            for h in range(MLA_HEADS):
                emptied(pe, u, f"on{h}")
            for t in range(NT):
                for h in range(2):
                    emptied(pe, u, f"ov{t}{h}")
            pe.wait_ge(event("okT_ready"), 1)
            for p in range(16 + 2):
                if p < 16:
                    for i in (2 * p, 2 * p + 1):
                        t, h = O_UNITS[i]
                        ps = begin(u, f"ml{i}")
                        done(u, f"ml{i}", pe.matmul(ps[:, :], oqT[:, h, t * P:(t + 1) * P], okT[:, h, :], start=True, stop=True))
                if 1 <= p < 17:
                    for i in (2 * p - 2, 2 * p - 1):
                        emptied(pe, u, f"ml{i}")
                        ps = begin(u, f"mp{i}")
                        done(u, f"mp{i}", turn_blocks(ps, [L2[:, i % 4, b * P:(b + 1) * P] for b in range(4)]))
                if p >= 2:
                    for i in (2 * p - 4, 2 * p - 3):
                        t, h = O_UNITS[i]
                        emptied(pe, u, f"mp{i}")
                        if i % 8 == 0:
                            begin(u, f"mo{i // 8}")
                        o = bank[u.at[f"mo{i // 8}"][0]]
                        for b in range(NT):
                            mm = pe.matmul(o[:, (h % 8) * 64:(h % 8) * 64 + 64], PT2[:, i % 4, b * P:(b + 1) * P],
                                           ova[:, b, h * 64:(h + 1) * 64], start=(b == 0), stop=(b == NT - 1))
                        if i % 8 == 7:
                            done(u, f"mo{i // 8}", mm)
            for t in range(TT):
                pe.wait_ge(event("om_ready"), t + 1)
                for h in range(2):
                    ps = begin(u, f"oyT{t}{h}")
                    done(u, f"oyT{t}{h}", turn_blocks(ps, [og[:, t, (4 * h + i) * P:(4 * h + i + 1) * P] for i in range(4)]))
            slots = [landed2("o_o0"), landed2("o_o1")]
            for t in range(TT):
                for h in range(2):
                    emptied(pe, u, f"oyT{t}{h}")
                for h in range(2):
                    project2(u, f"oout{t}{h}", slots[h], t, 512)

        @block.scalar
        def _(act):
            steps = [0]
            base = [0]

            def step(ins):
                steps[0] += 1
                ins.then_inc(event("act_step"), 1)

            def settle():
                act.wait_ge(event("act_step"), base[0] + steps[0])

            act.dma_start(col[:], cols).then_inc(loaded, 16)
            act.dma_start(ident[:], ident_in).then_inc(loaded, 16)
            act.dma_start(X[:, 0:TT, :], x.rearrange("(t p) d -> p t d", p=P)).then_inc(loaded, 16)
            act.dma_start(posi[:], pos).then_inc(loaded, 16)
            act.dma_start(kc[:], k1).then_inc(loaded, 16)
            act.dma_start(gmf, gmask).then_inc(loaded, 16)
            act.dma_start(wl_all[:], wlr).then_inc(loaded, 16)
            act.wait_ge(loaded, LOADS)
            act.activation(cact[:].rearrange("p k v -> p (k v)"), col[:, C_CT:C_CT + 24], ACT.Silu).then_inc(event("c_ready"), 1)
            act.wait_ge(event("sin_in"), 2)
            act.activation(sinT[:], sinT[:], ACT.Sin).then_inc(event("sin_out"), 1)
            act.activation(cosT[:], cosT[:], ACT.Sin).then_inc(event("sin_out"), 1)

            def copy_out(u, name, dst, rep, func=ACT.Copy, scale=1.0):
                ps = filled(act, u, name, rep)
                n = int(np.prod(dst.shape[1:]))
                act.activation(dst, shape_like(ps[0:dst.shape[0], 0:n], dst), func, scale=scale).then_inc(free(u, name), 1)

            with act.Fori(0, DEPTH) as l:
                u = lay1
                base[0], steps[0] = l * ACT_STEPS, 0
                act.wait_ge(event("x_ready"), l * TT + 1)
                for t in range(TT):
                    act.activation(Y[:, t, :], X[:, t, :], ACT.Square, accum_out=st[:, t:t + 1]).then_inc(event("x_ssq"), 1)
                act.wait_ge(event("x_var"), l + 1)
                for t in range(TT):
                    act.activation(st[:, 4 + t:5 + t], st[:, 2 + t:3 + t], ACT.Sqrt).then_inc(event("x_std"), 1)
                act.wait_ge(event("hmod_ready"), l + 1)
                for t in range(TT):
                    ps = filled(act, u, f"xT{t}0", l)
                    for k in range(4):
                        ins = act.activation(hT[:, k, t * P:(t + 1) * P], ps[:, k * P:(k + 1) * P], ACT.Identity,
                                             bias=hsh[:, k:k + 1], scale=hsc[:, k:k + 1])
                        if k < 3:
                            step(ins)
                    ins.then_inc(free(u, f"xT{t}0"), 1)
                for h in range(2):
                    copy_out(u, f"gb{h}", gpb[:, h * 512:(h + 1) * 512], l)
                for t in range(TT):
                    copy_out(u, f"idx{t}", idx[:, t, :], l)
                copy_out(u, "aT", aT[:, :], l)
                for t in range(TT):
                    copy_out(u, f"dsa_q{t}", dsaqkv[:, t, 0:512], l)
                copy_out(u, "qiT", qiT[:], l)
                copy_out(u, "kiT", kiT[:], l)
                copy_out(u, "gq", gqT[:], l, scale=0.125)
                copy_out(u, "gk", gkT[:], l)
                for t in range(TT):
                    for r in range(2):
                        ps = filled(act, u, f"s{t}{r}", l)
                        n = P * (t + 1)
                        at = (0, 2 * P)[r] if t == 0 else 512 + 512 * r
                        act.activation(RI[:, at:at + 2 * n], ps[:, 0:2 * n], ACT.Relu, scale=1.0 / 16).then_inc(free(u, f"s{t}{r}"), 1)
                for t in range(TT):
                    copy_out(u, f"dsa_kv{t}", dsaqkv[:, t, 512:768], l)
                for t in range(TT):
                    copy_out(u, f"ret_qk{t}", retqkv[:, t, 0:512], l)
                act.wait_ge(event("z_ready"), l + 1)
                step(act.activation(AZ[:], AZ[:], ACT.Exp, scale=-1.0))
                settle()
                act.activation(LG[:], AZ[:], ACT.Ln, bias=1.0).then_inc(event("lg_ready"), 1)
                copy_out(u, "dqT0", qdT[:, 0:2, :], l)
                copy_out(u, "dqT1", qdT[:, 2:4, :], l)
                copy_out(u, "dkT", kdT[:], l)
                for t in range(TT):
                    copy_out(u, f"ret_v{t}", retqkv[:, t, 512:1024], l)
                for t in range(TT):
                    copy_out(u, f"gla_v{t}", glav[:, t, :], l)
                copy_out(u, "rqT", qrT[:], l)
                copy_out(u, "rkT", krT[:], l)

                def gla_exp(i):
                    if i < len(LEVELS):
                        act.wait_ge(event("gsub"), l * 8 + i)
                        act.activation(E[i % 2], E[i % 2], ACT.Exp, scale=1.0 / 16).then_inc(event("gexp"), 1)

                gla_exp(1)

                def dsa_exp(i):
                    t, heads = DSA_UNITS[i]
                    act.wait_ge(event("dmax"), l * 6 + (i + 1))
                    n = P * (t + 1)
                    for a, h in enumerate(heads):
                        ins = act.activation(L[:, i % 2, a * n:(a + 1) * n], L[:, i % 2, a * n:(a + 1) * n], ACT.Exp,
                                             bias=mx[:, t, a + PARTS[i]:a + PARTS[i] + 1], accum_out=sm[:, t, h:h + 1])
                        if a < len(heads) - 1:
                            step(ins)
                    ins.then_inc(event("dexp"), 1)

                def head_sums(kind, o, at):
                    for t in range(TT):
                        ps = filled(act, u, f"{o}{t}", l)
                        for h in range(4):
                            settle()
                            ins = act.activation(junk[:], ps[:, h * P:(h + 1) * P], ACT.Square,
                                                 accum_out=st[:, at + 4 * t + h:at + 4 * t + h + 1])
                            if t < TT - 1 or h < 3:
                                step(ins)
                    ins.then_inc(event(kind + "_ssq"), 1)

                def head_roots(kind, at):
                    act.wait_ge(event(kind + "_var"), l + 1)
                    act.activation(st[:, at + 16:at + 24], st[:, at + 8:at + 16], ACT.Sqrt).then_inc(event(kind + "_std"), 1)

                def branch_out(name, dst):
                    for t in range(TT):
                        copy_out(u, f"{name}{t}", dst[:, :, t * P:(t + 1) * P], l)

                g = 0
                for name in ("ret_g", "dsa_g", "gla_g") + tuple(f"merge{m}" for m in range(MERGES)):
                    for t in range(TT):
                        if name[0] == "m":
                            m = int(name[5])
                            if g == 6:
                                act.wait_ge(event("sel_ready"), l * TT + TT)
                            dst = G[:, t, m * 512:(m + 1) * 512]
                            copy_out(u, f"{name}{t}", dst, l, func=ACT.Copy if g < 13 else ACT.Sigmoid)
                        else:
                            dst = {"ret_g": retg, "dsa_g": dsag, "gla_g": glag}[name][:, t, :]
                            copy_out(u, f"{name}{t}", dst, l)
                        gla_exp(g + 2)
                        if 6 <= g <= 11:
                            copy_out(u, f"dp{g - 6}", PT[:, g % 2, :], l)
                        if 5 <= g <= 10:
                            dsa_exp(g - 5)
                        if g == 5:
                            head_sums("r", "ro", 8)
                            head_roots("r", 8)
                            for dst in (retg, dsag, glag):
                                emptied(act, u, "gla_g1", l)
                                act.activation(dst[:], dst[:], ACT.Silu).then_inc(event("silu_ready"), 1)
                        if g == 9:
                            head_sums("g", "go", 40)
                        if g == 10:
                            head_roots("g", 40)
                        if g == 11:
                            branch_out("retT", retT)
                        if g == 12:
                            branch_out("glaT", glaT)
                            emptied(act, u, "merge30", l)
                            act.activation(G[:, 0, 0:2048], G[:, 0, 0:2048], ACT.Sigmoid).then_inc(event("g_sig"), 1)
                            act.activation(G[:, 1, 0:1536], G[:, 1, 0:1536], ACT.Sigmoid).then_inc(event("g_sig"), 1)
                        if g == 13:
                            branch_out("dsaT", dsaT)
                        g += 1
                for t in range(TT):
                    copy_out(u, f"yT{t}0", hT[:, 0:4, t * P:(t + 1) * P], l)
                for t in range(TT):
                    for h in range(2):
                        ps = filled(act, u, f"out{t}{h}", l)
                        settle()
                        step(act.activation(L[:, 0, :], ps[:, :], ACT.Square, accum_out=st[:, 72 + 2 * t + h:73 + 2 * t + h]))
                        act.activation(Y[:, t, h * 512:(h + 1) * 512], ps[:, :], ACT.Copy).then_inc(free(u, f"out{t}{h}"), 1)
                    act.wait_ge(event("o_var"), l * TT + (t + 1))
                    act.activation(st[:, 78 + t:79 + t], st[:, 76 + t:77 + t], ACT.Sqrt).then_inc(event("o_std"), 1)
                counted("ACT_STEPS", steps[0], ACT_STEPS)

            base[0], steps[0] = DEPTH * ACT_STEPS, 0

            def copy_rows(u, name, dst, ps, func=ACT.Copy, **more):
                act.activation(dst, ps, func, **more).then_inc(free(u, name), 1)

            def norm_x2(u, first):
                for t in range(NT):
                    act.activation(Y2[:, t, :], X[:, t, :], ACT.Square, accum_out=st2[:, t:t + 1]).then_inc(event("h2_ssq"), 1)
                act.wait_ge(event("h2_var"), first + 1)
                act.activation(st2[:, 8:12], st2[:, 4:8], ACT.Sqrt).then_inc(event("h2_std"), 1)
                act.wait_ge(event("hmod2"), first + 1)
                for t in range(NT):
                    v = t // TT
                    ps = filled(act, u, f"xT{t}0")
                    for k in range(4):
                        ins = act.activation(hT2[:, k, t * P:(t + 1) * P], ps[:, k * P:(k + 1) * P], ACT.Identity,
                                             bias=hsh2[:, v, k:k + 1], scale=hsc2[:, v, k:k + 1])
                        if k < 3:
                            step(ins)
                    ins.then_inc(free(u, f"xT{t}0"), 1)

            u = le
            act.wait_ge(event("x_ready"), DEPTH * TT + 1)
            act.wait_ge(event("ctx_in"), 32)
            norm_x2(u, 0)
            for v in range(2):
                for h in range(2):
                    copy_out(u, f"gb{v}{h}", gbr[:, v, h * 512:(h + 1) * 512], 0)
            for t in range(NT):
                ps = filled(act, u, f"e_kv{t}")
                step(act.activation(eqk[:, t, 512:640], ps[:, 0:P], ACT.Copy))
                copy_rows(u, f"e_kv{t}", ev[:, t, :], ps[:, P:2 * P])
            for t in range(NT):
                copy_out(u, f"e_q{t}", eqk[:, t, 0:512], 0)
            for t in range(NT):
                copy_out(u, f"e_u{t}", eu[:, t, :], 0, func=ACT.Gelu)
            for t in range(NT):
                ps = filled(act, u, f"e_vv{t}")
                copy_rows(u, f"e_vv{t}", evv[:, t, :], ps[:, :], ACT.Gelu, accum_out=st2[:, 12 + t:13 + t])
            for j in range(2):
                copy_out(u, f"ekT{j}", ekT[:, j, :], 0)
            for j in range(4):
                copy_out(u, f"eqT{j}", eqT[:, j, :], 0)
            for t in range(NT):
                act.wait_ge(event("ln_c"), t + 1)
                act.activation(PT2[:, t, :], evv[:, t, :], ACT.Square, accum_out=st2[:, 16 + t:17 + t]).then_inc(event("ln_ssq"), 1)
            act.wait_ge(event("ln_var"), 1)
            act.activation(st2[:, 24:28], st2[:, 20:24], ACT.Sqrt).then_inc(event("ln_std"), 1)
            for g in range(14):
                if g < 8:
                    copy_out(u, f"e_g{g // 4}{g % 4}", eg[:, g % 4, (g // 4) * 512:(g // 4) * 512 + 512], 0)
                if g == 8:
                    for t in range(NT):
                        emptied(act, u, f"e_g1{t}")
                    act.activation(eg[:], eg[:], ACT.Silu).then_inc(event("esilu"), 1)
                if 1 <= g < 13:
                    for i in (2 * g - 2, 2 * g - 1):
                        copy_out(u, f"ep{i}", PT2[:, i % 4, :], 0)
                if g < 12:
                    for i in (2 * g, 2 * g + 1):
                        t, heads = E_UNITS[i]
                        act.wait_ge(event("e_max"), i + 1)
                        if t < TT:
                            h = heads[0]
                            act.activation(L2[:, i % 4, :], L2[:, i % 4, :], ACT.Exp, bias=mx2[:, t, h:h + 1],
                                           accum_out=sm2[:, t, h:h + 1]).then_inc(event("e_exp"), 1)
                        else:
                            ps = filled(act, u, f"el{i}")
                            for a, h in enumerate(heads):
                                ins = act.activation(L2[:, i % 4, a * 256:(a + 1) * 256], ps[:, a * 256:(a + 1) * 256], ACT.Exp,
                                                     bias=mx2[:, t, h:h + 1], scale=0.125, accum_out=sm2[:, t, h:h + 1])
                                if a == 0:
                                    step(ins)
                            ins.then_inc(free(u, f"el{i}"), 1)
                for t in range(NT):
                    if g == E_LAST[t] // 2 + 1:
                        act.wait_ge(event("e_arg"), t + 1)
                        act.activation(es2[:, t, :], es2[:, t, :], ACT.Exp).then_inc(event("e_es"), 1)
            for t in range(NT):
                copy_out(u, f"eyT{t}0", hT2[:, 0:4, t * P:(t + 1) * P], 0)

            u = lo
            act.wait_ge(event("x2_ready"), NT)
            norm_x2(u, 1)
            for h in range(2):
                copy_out(u, f"gb0{h}", gbr[:, 0, h * 512:(h + 1) * 512], 0)
            for t in range(NT):
                copy_out(u, f"o_kv{t}", okv[:, t, :], 0)
            for t in range(TT):
                copy_out(u, f"o_q{t}", oqa[:, t, :], 0)
            for t in range(NT):
                emptied(act, u, f"o_kv{t}")
                act.activation(PT2[:, t, 0:P], okv[:, t, 0:P], ACT.Square, accum_out=st2[:, 32 + t:33 + t]).then_inc(event("o_ssq2"), 1)
            for t in range(TT):
                emptied(act, u, f"o_q{t}")
                act.activation(PT2[:, t, 256:512], oqa[:, t, :], ACT.Square, accum_out=st2[:, 36 + t:37 + t]).then_inc(event("o_ssq2"), 1)
            act.wait_ge(event("o_var2"), 1)
            act.activation(st2[:, 48:54], st2[:, 40:46], ACT.Sqrt).then_inc(event("o_std2"), 1)
            for t in range(TT):
                copy_out(u, f"o_g0{t}", og[:, t, 0:512], 0)
            ps = filled(act, u, "kvT")
            copy_rows(u, "kvT", kvT, ps[:, :], ACT.Copy, scale=col[:, C_KVN:C_KVN + 1])
            ps = filled(act, u, "kpT")
            copy_rows(u, "kpT", kpe[64:96, :], ps[64:96, :])
            for h in range(0, MLA_HEADS, 2):
                ps = filled(act, u, f"on{h}")
                copy_rows(u, f"on{h}", okT[0:MLA_NOPE, h, :], ps[0:MLA_NOPE, :])
            for t in range(NT):
                copy_out(u, f"ov{t}0", ova[:, t, 0:512], 0)
            ps = filled(act, u, "qaT")
            step(act.activation(qaT[:, 0, :], ps[:, 0:S], ACT.Copy, scale=col[:, C_QN:C_QN + 1]))
            copy_rows(u, "qaT", qaT[:, 1, :], ps[:, S:2 * S], ACT.Copy, scale=col[:, C_QN + 1:C_QN + 2])
            for t in range(TT):
                for c in (0, 2):
                    copy_out(u, f"oqb{t}{c}", q2[:, t, c * 512:(c + 1) * 512], 0)
            for t in range(TT):
                copy_out(u, f"o_g1{t}", og[:, t, 512:1024], 0)
            for t in range(TT):
                emptied(act, u, f"o_g0{t}")
                emptied(act, u, f"o_g1{t}")
            act.activation(og[:], og[:], ACT.Silu).then_inc(event("osilu"), 1)
            for j in range(0, 8, 2):
                ps = filled(act, u, f"oqT{j}")
                copy_rows(u, f"oqT{j}", oqT[:, 2 * j:2 * j + 2, :], ps[0:MLA_QK, :].rearrange("p (a b) -> p a b", a=2))
            for p in range(17):
                if p >= 1:
                    i = 2 * p - 2
                    copy_out(u, f"mp{i}", PT2[:, i % 4, :], 0)
                if p < 16:
                    for i in (2 * p, 2 * p + 1):
                        t, h = O_UNITS[i]
                        act.wait_ge(event("o_max"), i + 1)
                        ps = filled(act, u, f"ml{i}")
                        copy_rows(u, f"ml{i}", L2[:, i % 4, :], ps[:, :], ACT.Exp, bias=mx2[:, t, h:h + 1], scale=MLA_SCALE,
                                  accum_out=sm2[:, t, h:h + 1])
            for t in range(TT):
                copy_out(u, f"oyT{t}0", hT2[:, 0:4, t * P:(t + 1) * P], 0)
            for t in range(TT):
                act.wait_ge(event("x3_ready"), t + 1)
                act.activation(Y2[:, TT + t, :], X[:, t, :], ACT.Square, accum_out=st2[:, t:t + 1]).then_inc(event("f_ssq"), 1)
                act.wait_ge(event("f_var"), t + 1)
                act.activation(st2[:, 8 + t:9 + t], st2[:, 4 + t:5 + t], ACT.Sqrt).then_inc(event("f_std"), 1)

        @block.gpsimd
        def _(pool):
            steps, base = [0], [0]

            def step(ins):
                steps[0] += 1
                ins.then_inc(event("pool_step"), 1)

            def settle():
                pool.wait_ge(event("pool_step"), base[0] + steps[0])

            pool.wait_ge(event("sin_out"), 2)
            with pool.Fori(0, DEPTH) as l:
                u = lay1
                base[0], steps[0] = l * POOL_STEPS, 0

                def rotate(v, half, f0, heads):
                    x1, x2 = v[:, :, :, 0:half], v[:, :, :, half:2 * half]
                    c = cosT[:, :, f0:f0 + half].unsqueeze(2).broadcast_to([P, TT, heads, half])
                    s = sinT[:, :, f0:f0 + half].unsqueeze(2).broadcast_to([P, TT, heads, half])
                    T = [rt[:, q, 0:TT * heads * half].rearrange("p (t h d) -> p t h d", t=TT, h=heads) for q in range(4)]
                    for q, (a, b) in enumerate(((x1, c), (x2, s), (x2, c), (x1, s))):
                        step(pool.tensor_tensor(T[q], a, b, ALU.mult))
                    settle()
                    step(pool.tensor_tensor(x1, T[0], T[1], ALU.subtract))
                    return pool.tensor_tensor(x2, T[2], T[3], ALU.add)

                for t in range(TT):
                    for h in range(2):
                        emptied(pool, u, f"xT{t}{h}", l)
                for name in ("dsa_q", "dsa_kv"):
                    for t in range(TT):
                        emptied(pool, u, f"{name}{t}", l)
                step(rotate(dsaqkv[:, :, 0:640].rearrange("p t (h d) -> p t h d", h=10), 8, 32, 10))
                settle()
                step(pool.tensor_tensor(pw[:, 0:1], ident[:, 0:1], ident[:, 0:1], ALU.mult))
                for t in range(TT):
                    ins = pool.tensor_copy(kdd[:, t, :, :, :],
                                           dsaqkv[:, t, 512:640].rearrange("p (h d) -> p h d", h=2).unsqueeze(2).broadcast_to([P, 2, 2, 64]))
                    if t == 0:
                        step(ins)
                ins.then_inc(event("dsa_rot"), 1)
                for t in range(TT):
                    emptied(pool, u, f"ret_qk{t}", l)
                rotate(retqkv[:, :, 0:512].rearrange("p t (h d) -> p t h d", h=8), 32, 0, 8).then_inc(event("ret_rot"), 1)

                emptied(pool, u, "gk", l)
                for i in range(1, len(LEVELS)):
                    pool.wait_ge(event("gexp"), l * 8 + i)
                    if i >= 3:
                        for r in range(2):
                            filled(pool, u, f"g{i - 2}_{r}", l)
                    pool.tensor_tensor(KL[:, i % 2], gkT[:], E[i % 2], ALU.mult).then_inc(event("gkl"), 1)
                counted("POOL_STEPS", steps[0], POOL_STEPS)

            base[0], steps[0] = DEPTH * POOL_STEPS, 0

            def rotate2(x1, x2, y1, y2, c, s, T):
                for q, (a, b) in enumerate(((x1, c), (x2, s), (x2, c), (x1, s))):
                    step(pool.tensor_tensor(T[q], a, b, ALU.mult))
                settle()
                step(pool.tensor_tensor(y1, T[0], T[1], ALU.subtract))
                step(pool.tensor_tensor(y2, T[2], T[3], ALU.add))

            u = le
            pool.wait_ge(event("ctx_in"), 32)
            for name in ("e_kv", "e_q"):
                for t in range(TT):
                    emptied(pool, u, f"{name}{t}")
            for t in range(TT):
                v = eqk[:, t, :].rearrange("p (h a b d) -> p h a b d", h=10, a=2, b=2)
                x1, x2 = v[:, :, :, 0, :], v[:, :, :, 1, :]
                c, s = (e_rot[:, q, t, :].rearrange("p (a d) -> p a d", a=2).unsqueeze(1).broadcast_to([P, 10, 2, 16]) for q in range(2))
                T = [ert[:, q, :].rearrange("p (h a d) -> p h a d", h=10, a=2) for q in range(4)]
                rotate2(x1, x2, x1, x2, c, s, T)
                settle()
            for t in range(NT):
                emptied(pool, u, f"e_kv{t}")
                ins = pool.tensor_copy(ekd[:, t], eqk[:, t, 512:640].rearrange("p (h d) -> p h d", h=2).unsqueeze(2).broadcast_to([P, 2, 2, 64]))
                if t < NT - 1:
                    step(ins)
            ins.then_inc(event("e_rot"), 1)

            u = lo
            pool.wait_ge(event("x2_ready"), NT)
            step(pool.memset(okp[:, :, 0:64], 0.0))
            for t in range(NT):
                emptied(pool, u, f"o_kv{t}")
            step(pool.tensor_copy(okp[:, TT:NT, 64:96], okv[:, TT:NT, 128:160]))
            v = okv[:, 0:TT, 128:160].rearrange("p t (a b d) -> p t a b d", a=2, b=2)
            w = okp[:, 0:TT, 64:96].rearrange("p t (a b d) -> p t a b d", a=2, b=2)
            c, s = (o_rot[:, q].rearrange("p t (a d) -> p t a d", a=2) for q in range(2))
            T = [ort[:, q, 0:32 * TT // 2].rearrange("p (t a d) -> p t a d", t=TT, a=2) for q in range(4)]
            rotate2(v[:, :, :, 0, :], v[:, :, :, 1, :], w[:, :, :, 0, :], w[:, :, :, 1, :], c, s, T)
            settle()
            pool.tensor_tensor(pw[:, 0:1], ident[:, 0:1], ident[:, 0:1], ALU.mult).then_inc(event("okp_ready"), 1)
            emptied(pool, u, "kpT")
            pool.tensor_copy(okT[64:96], kpe[64:96, :].unsqueeze(1).broadcast_to([32, MLA_HEADS, NT * P])).then_inc(event("okT_ready"), 1)
            pool.wait_ge(event("okT_ready"), 1)
            for t in range(TT):
                for k in range(3):
                    emptied(pool, u, f"oqb{t}{k}")
            qv = q2.rearrange("p t (h c) -> p t h c", h=MLA_HEADS)
            for a in range(2):
                x1, x2 = qv[:, :, :, 64 + 16 * a:72 + 16 * a], qv[:, :, :, 72 + 16 * a:80 + 16 * a]
                c, s = (o_rot[:, q, :, 8 * a:8 * a + 8].unsqueeze(2).broadcast_to([P, TT, MLA_HEADS, 8]) for q in range(2))
                T = [ort[:, q, :].rearrange("p (t h d) -> p t h d", t=TT, h=MLA_HEADS) for q in range(4)]
                rotate2(x1, x2, x1, x2, c, s, T)
                settle()
            pool.tensor_tensor(pw[:, 1:2], ident[:, 0:1], ident[:, 0:1], ALU.mult).then_inc(event("oq_rot"), 1)

        @block.vector
        def _(dve):
            steps, base = [0], [0]

            def step(ins):
                steps[0] += 1
                ins.then_inc(event("dve_step"), 1)

            def settle():
                dve.wait_ge(event("dve_step"), base[0] + steps[0])

            def carry():
                carried[0] = (carried[0] + 1) % 64
                step(dve.tensor_copy(cw[:, carried[0]:carried[0] + 1], ident[:, 0:1]))

            carried = [0]
            adab = col[:, C_ADAB:C_ADAB + 96].rearrange("p (a f) -> p a f", a=4)
            condv = cact[:].rearrange("p k v -> p v k")
            layv = col[:, C_LAY:C_LAY + DEPTH * LAYC].rearrange("p (l c) -> p l c", l=DEPTH)

            def mod_out(u, name, m, which, vectors, rep=0):
                ps = filled(dve, u, name, rep)
                w = 64 * vectors
                dve.tensor_tensor(mod[:, 4 * m:4 * m + 4, 0:vectors],
                                  ps[:, 0:4 * w].rearrange("p (j v c) -> p j v c", j=4, v=vectors)[:, :, :, 0],
                                  adab[:, which, 4 * m:4 * m + 4].unsqueeze(2).broadcast_to([P, 4, vectors]),
                                  ALU.add).then_inc(free(u, name), 1)

            def mod_sum(chunks, c, chunks_before, sums, vectors, cond, rep=0):
                arrived(dve, chunks, c, chunks_before, rep)
                slot = ring[:, c % RING, :]
                for k in range(KD):
                    for v in range(vectors):
                        w = slot[:, k * 512:(k + 1) * 512]
                        if k == 0:
                            ins = dve.tensor_scalar(sums[:, v, :], w, cond[:, k, v:v + 1], None, ALU.mult)
                        else:
                            dve.wait_ge(event("dve_step"), base[0] + (steps[0] - vectors + 1))
                            ins = dve.scalar_tensor_tensor(sums[:, v, :], w, cond[:, k, v:v + 1], sums[:, v, :],
                                                           ALU.mult, ALU.add)
                        if k == KD - 1 and v == vectors - 1:
                            ins.then_inc(event("ada_sum"), 1)
                        else:
                            step(ins)

            for b in range(8):
                dve.memset(bank[b][:, :], 0.0).then_inc(bank_free[b], 1)
            step(dve.memset(ones[:], 1.0))
            dve.wait_ge(loaded, LOADS)
            step(dve.tensor_copy(gm[:], gmf))
            step(dve.tensor_copy(posf[:], posi[:]))
            settle()
            for t in range(TT):
                step(dve.tensor_scalar(ang[:, t, :], freq, posf[:, t:t + 1], None, ALU.mult))
            settle()
            for dst, quarter in ((sinT, 0.0), (cosT, 0.25)):
                step(dve.tensor_scalar(turn[:], ang[:], 1.0 / (2 * np.pi), quarter, ALU.mult, ALU.add))
                settle()
                step(dve.tensor_scalar(turn[:], turn[:], ROUND, None, ALU.add))
                settle()
                step(dve.tensor_scalar(turn[:], turn[:], -ROUND, None, ALU.add))
                settle()
                step(dve.scalar_tensor_tensor(dst[:], turn[:], -TWO_PI[0], ang[:], ALU.mult, ALU.add))
                for part in TWO_PI[1:]:
                    settle()
                    step(dve.scalar_tensor_tensor(dst[:], turn[:], -part, dst[:], ALU.mult, ALU.add))
                settle()
                step(dve.tensor_scalar(dst[:], dst[:], quarter * 2 * np.pi, PI_BELOW, ALU.add, ALU.min))
                settle()
                dve.tensor_scalar(dst[:], dst[:], -PI_BELOW, None, ALU.max).then_inc(event("sin_in"), 1)
            dve.wait_ge(event("c_ready"), 1)
            for m in range(MERGES):
                mod_sum(CH0, m, 0, msum[:, m % 2], 1, cact)
                if m > 0:
                    mod_out(pro, f"ada{m - 1}", m - 1, 0, 1)
            mod_out(pro, f"ada{MERGES - 1}", MERGES - 1, 0, 1)
            dve.tensor_copy(posf[:], posi[:]).then_inc(event("x_ready"), 1)
            before = steps[0]
            emptied(dve, pro, "ada4")
            emptied(dve, pro, "ada5")
            dve.wait_ge(event("sin_out"), 2)

            with dve.Fori(0, DEPTH) as l:
                u = lay1
                base[0], steps[0] = l * DVE_STEPS + before, 0
                step(dve.tensor_copy(lay[:], layv[:, l, :]))
                for v in range(2):
                    step(dve.tensor_copy(cnow[:, :, v], condv[:, l + v, :]))
                dve.tensor_copy(wl[:], wl_all[:, l, :]).then_inc(event("wl_ready"), 1)
                settle()
                step(dve.scalar_tensor_tensor(hsc[:], mod[:, 8:16, 0], 1.0, lay[:, 0:8], ALU.add, ALU.mult))
                step(dve.tensor_tensor(gpo[:], mod[:, 16:24, 0], lay[:, 8:16], ALU.mult))
                dve.tensor_copy(hsh[:], mod[:, 0:8, 0]).then_inc(event("hmod_ready"), 1)
                settle()
                dve.tensor_tensor(DG, ident[:].unsqueeze(1).broadcast_to([P, KD, P]),
                                  gpo[:].unsqueeze(2).broadcast_to([P, KD, P]), ALU.mult).then_inc(event("diag_ready"), 1)
                dve.wait_ge(event("x_ssq"), l * TT + TT)
                dve.tensor_scalar(st[:, 2:4], st[:, 0:2], 1.0 / D, EPS, ALU.mult, ALU.add).then_inc(event("x_var"), 1)
                dve.wait_ge(event("x_std"), l * TT + TT)
                step(dve.reciprocal(st[:, 6:8], st[:, 4:6]))
                settle()
                for t in range(TT):
                    dve.tensor_scalar(Y[:, t, :], X[:, t, :], st[:, 6 + t:7 + t], None, ALU.mult).then_inc(event("xn_ready"), 1)
                dve.wait_ge(event("hmod_ready"), l + 1)
                for t in range(TT):
                    ps = filled(dve, u, f"xT{t}1", l)
                    for k in range(4):
                        ins = dve.tensor_scalar(hT[:, 4 + k, t * P:(t + 1) * P], ps[:, k * P:(k + 1) * P],
                                                hsc[:, 4 + k:5 + k], hsh[:, 4 + k:5 + k], ALU.mult, ALU.add)
                        if k < 3:
                            step(ins)
                    ins.then_inc(free(u, f"xT{t}1"), 1)

                for t in range(TT):
                    emptied(dve, u, f"idx{t}", l)
                v = idx[:, :, 0:320].rearrange("p t (h d) -> p t h d", h=5)
                x1, x2 = v[:, :, :, 0:8], v[:, :, :, 8:16]
                c = cosT[:, :, 32:40].unsqueeze(2).broadcast_to([P, TT, 5, 8])
                s = sinT[:, :, 32:40].unsqueeze(2).broadcast_to([P, TT, 5, 8])
                T = [ti[:, q, :].rearrange("p (t h d) -> p t h d", t=TT, h=5) for q in range(4)]
                for q, (a, b) in enumerate(((x1, c), (x2, s), (x2, c), (x1, s))):
                    step(dve.tensor_tensor(T[q], a, b, ALU.mult))
                settle()
                step(dve.tensor_tensor(x1, T[0], T[1], ALU.subtract))
                step(dve.tensor_tensor(x2, T[2], T[3], ALU.add))
                settle()
                dve.tensor_copy(kdi[:], v[:, :, 4, :].unsqueeze(2).broadcast_to([P, TT, 2, 64])).then_inc(event("idx_rot"), 1)

                def scores(t):
                    n = P * (t + 1)
                    first = 0 if t == 0 else P
                    s_, w_, mask = sc[:, first:first + n], wk[:, first:first + n], cm[:, 256 - n:256]
                    for r in range(2):
                        emptied(dve, u, f"s{t}{r}", l)
                    for h in range(4):
                        r, j = h % 2, h // 2
                        at = ((0, 2 * P)[r] if t == 0 else 512 + 512 * r) + j * n
                        step(dve.scalar_tensor_tensor(s_, RI[:, at:at + n], idx[:, t, 320 + h:321 + h],
                                                      mask if h == 0 else s_, ALU.mult, ALU.add))
                        if h < 3:
                            settle()
                    for i in range(TOPK // 8):
                        src = s_ if i == 0 else w_
                        settle()
                        carry()
                        step(dve.max(m8[:], src))
                        settle()
                        carry()
                        step(dve.match_replace(w_, m8[:], src, TAKEN))
                    settle()
                    step(dve.tensor_tensor(w_, w_, s_, ALU.is_equal))
                    settle()
                    dve.scalar_tensor_tensor(s_, w_, NEG, mask, ALU.mult, ALU.add).then_inc(event("sel_ready"), 1)

                scores(0)
                ps = filled(dve, u, "z", l)
                step(dve.tensor_scalar(Z[:, 0, :], ps[:, 0:S], lay[:, 16:17], None, ALU.add))
                dve.tensor_scalar(Z[:, 1, :], ps[:, S:2 * S], lay[:, 17:18], None, ALU.add).then_inc(free(u, "z"), 1)
                emptied(dve, u, "z", l)
                dve.scalar_tensor_tensor(AZ, Z, -1.0, Z, ALU.mult, ALU.max).then_inc(event("z_ready"), 1)
                dve.wait_ge(event("z_ready"), l + 1)
                step(dve.tensor_scalar(Z, Z, 0.0, None, ALU.min))
                scores(1)
                dve.wait_ge(event("lg_ready"), l + 1)
                step(dve.tensor_tensor(LG, Z, LG, ALU.subtract))
                settle()
                for f in range(2):
                    step(dve.tensor_tensor_scan(bcum[:, f, :], reset, LG[:, f, :], 0.0, ALU.mult, ALU.add))
                settle()

                bf = bcum[:].rearrange("p f s -> p (f s)")

                def gla_sub(i):
                    if i >= len(LEVELS):
                        return
                    if i >= 3:
                        dve.wait_ge(event("gkl"), l * 8 + (i - 2))
                        dve.wait_ge(event("gql"), l * 8 + (i - 2))
                    e = E[i % 2]
                    if LEVELS[i] == "cross":
                        b = lambda a: bcum[:, :, a:a + 1].broadcast_to([P, 2, 64])
                        step(dve.tensor_copy(e[:, :, 128:192], bcum[:, :, 128:192]))
                        step(dve.tensor_tensor(e[:, :, 192:256], bcum[:, :, 192:256], b(191), ALU.add))
                        step(dve.tensor_tensor(e[:, :, 64:128], b(127), bcum[:, :, 64:128], ALU.subtract))
                        step(dve.tensor_tensor(e[:, :, 0:64], b(63), bcum[:, :, 0:64], ALU.subtract))
                        settle()
                        ins = dve.tensor_tensor(e[:, :, 0:64], e[:, :, 0:64], b(127), ALU.add)
                    else:
                        h = LEVELS[i]
                        v = bf.rearrange("p (n c) -> p n c", c=2 * h)
                        ev = e.rearrange("p f s -> p (f s)").rearrange("p (n c) -> p n c", c=2 * h)
                        n = 512 // (2 * h)
                        mid = v[:, :, h - 1:h].broadcast_to([P, n, h])
                        if h == GLA_CHUNK:
                            step(dve.tensor_copy(ev[:, :, h:2 * h], v[:, :, h:2 * h]))
                        else:
                            step(dve.tensor_tensor(ev[:, :, h:2 * h], v[:, :, h:2 * h], mid, ALU.subtract))
                        ins = dve.tensor_tensor(ev[:, :, 0:h], mid, v[:, :, 0:h], ALU.subtract)
                    ins.then_inc(event("gsub"), 1)

                def gla_mul(i):
                    if i < len(LEVELS):
                        dve.wait_ge(event("gexp"), l * 8 + i)
                        dve.tensor_tensor(QL[i % 2], gqT[:], E[i % 2], ALU.mult).then_inc(event("gql"), 1)

                def gla_take(i):
                    kind = LEVELS[i]
                    for r in range(2):
                        ps = filled(dve, u, f"g{i}_{r}", l)
                        if kind == "cross":
                            dve.tensor_copy(AT[:, r, 2], ps[:, 0:2 * P].rearrange("p (j c) -> p j c", j=2)).then_inc(free(u, f"g{i}_{r}"), 1)
                            continue
                        dst = AT[:, r, 0:2].rearrange("p t j c -> p (t j) c")
                        src = ps[:, :].rearrange("p (b c) -> p b c", b=4)
                        if kind == "diag":
                            ins = dve.tensor_tensor(dst, src, ident[:].unsqueeze(1).broadcast_to([P, 4, P]), ALU.mult)
                        else:
                            emptied(dve, u, f"g{i - 1}_{r}", l)
                            carry()
                            ins = dve.copy_predicated(dst, gm[:, i - 1, :].unsqueeze(1).broadcast_to([P, 4, P]), src)
                        ins.then_inc(free(u, f"g{i}_{r}"), 1)

                dve.wait_ge(event("ret_rot"), l + 1)
                emptied(dve, u, "gq", l)
                gla_sub(1)

                def head_norm(kind, o, at, gate, ready, silu):
                    dve.wait_ge(event(kind + "_ssq"), l + 1)
                    dve.tensor_scalar(st[:, at + 8:at + 16], st[:, at:at + 8], 1.0 / P, EPS, ALU.mult,
                                      ALU.add).then_inc(event(kind + "_var"), 1)
                    dve.wait_ge(event(kind + "_std"), l + 1)
                    step(dve.reciprocal(st[:, at + 24:at + 32], st[:, at + 16:at + 24]))
                    gated(o, st[:, at + 24:at + 32], 4, gate, ready, silu)

                def gated(o, factor, heads, gate, ready, silu):
                    dve.wait_ge(event("silu_ready"), l * 3 + silu)
                    for t in range(TT):
                        settle()
                        ps = filled(dve, u, f"{o}{t}", l)
                        w = 512 // heads
                        tmp = RS[:].rearrange("p a b -> p (a b)")[:, 0:512]
                        dve.tensor_tensor(tmp.rearrange("p (h d) -> p h d", h=heads),
                                          ps[:, :].rearrange("p (h d) -> p h d", h=heads),
                                          factor[:, t * heads:(t + 1) * heads].unsqueeze(2).broadcast_to([P, heads, w]),
                                          ALU.mult).then_inc(free(u, f"{o}{t}"), 1)
                        emptied(dve, u, f"{o}{t}", l)
                        dve.tensor_tensor(gate[:, t, :], tmp, gate[:, t, :], ALU.mult).then_inc(event(ready), 1)
                        dve.wait_ge(event(ready), l * TT + (t + 1))

                g = 0
                for name in ("ret_g", "dsa_g", "gla_g") + tuple(f"merge{m}" for m in range(MERGES)):
                    for t in range(TT):
                        gla_sub(g + 2)
                        gla_mul(g + 1)
                        if g < 4:
                            ps = filled(dve, u, f"rs{g}", l)
                            dve.tensor_tensor(RS[:, g % 2, :], ps[:, 0:384], decay[:, g, :], ALU.mult).then_inc(free(u, f"rs{g}"), 1)
                        if 5 <= g <= 10:
                            i = g - 5
                            tq, heads = DSA_UNITS[i]
                            n, nh = P * (tq + 1), len(heads)
                            first = 0 if tq == 0 else P
                            if i in (0, 2):
                                dve.wait_ge(event("sel_ready"), l * TT + (tq + 1))
                            ps = filled(dve, u, f"dl{i}", l)
                            lv = L[:, i % 2, :].rearrange("p (h n) -> p h n", h=nh)
                            dve.scalar_tensor_tensor(lv, ps[:, :].rearrange("p (h n) -> p h n", h=nh), 0.125,
                                                     sc[:, first:first + n].unsqueeze(1).broadcast_to([P, nh, n]),
                                                     ALU.mult, ALU.add).then_inc(free(u, f"dl{i}"), 1)
                            emptied(dve, u, f"dl{i}", l)
                            dve.tensor_reduce(mx[:, tq, PARTS[i]:PARTS[i] + nh], lv, AX, ALU.max,
                                              negate=True).then_inc(event("dmax"), 1)
                        if g < len(LEVELS):
                            gla_take(g)
                        if g == 8:
                            emptied(dve, u, "g8_0", l)
                            emptied(dve, u, "g8_1", l)
                            dve.tensor_copy(st[:, 95:96], AT[:, 1, 2, 1, 127:128]).then_inc(event("at_ready"), 1)
                        if g == 5:
                            head_norm("r", "ro", 8, retg, "ret_ready", 1)
                        if g == 10:
                            head_norm("g", "go", 40, glag, "gla_ready", 3)
                        if g == 12:
                            filled(dve, u, "do1", l)
                            dve.wait_ge(event("dexp"), l * 6 + 6)
                            step(dve.reciprocal(st[:, 80:96], sm[:].rearrange("p t h -> p (t h)")))
                            gated("do", st[:, 80:96], 8, dsag, "dsa_ready", 2)
                        g += 1
                    if name.startswith("merge"):
                        m = int(name[5])
                        mod_sum(CH1, [n for n, _ in CH1].index(f"ada{m}"), len(CH0), msum[:, m % 2], 2, cnow, l)
                        if m > 0:
                            mod_out(u, f"ada{m - 1}", m - 1, l + 1, 2, l)

                dve.wait_ge(event("g_sig"), l * 2 + 2)
                emptied(dve, u, f"merge{MERGES - 1}0", l)
                emptied(dve, u, f"merge{MERGES - 1}1", l)
                for b in range(3):
                    for t in range(TT):
                        for h in range(2):
                            name = f"br{b}{t}{h}"
                            ps = filled(dve, u, name, l)
                            gv = G[:, t, b * D + h * 512:b * D + h * 512 + 512]
                            yv = Y[:, t, h * 512:(h + 1) * 512]
                            dve.tensor_tensor(yv if b == 0 else gv, ps[:, :], gv, ALU.mult).then_inc(free(u, name), 1)
                            if b == 0:
                                continue
                            emptied(dve, u, name, l)
                            emptied(dve, u, f"br{b - 1}{t}{h}", l)
                            settle()
                            ins = dve.tensor_tensor(yv, yv, gv, ALU.add)
                            if b == 2 and h == 1:
                                ins.then_inc(event("y_ready"), 1)
                            else:
                                step(ins)
                    if b == 0:
                        mod_out(u, f"ada{MERGES - 1}", MERGES - 1, l + 1, 2, l)
                for t in range(TT):
                    ps = filled(dve, u, f"yT{t}1", l)
                    dve.tensor_copy(hT[:, 4:8, t * P:(t + 1) * P], ps[:, :].rearrange("p (k c) -> p k c", k=4)).then_inc(free(u, f"yT{t}1"), 1)
                for t in range(TT):
                    for h in range(2):
                        emptied(dve, u, f"out{t}{h}", l)
                    step(dve.tensor_tensor(st[:, 72 + 2 * t:73 + 2 * t], st[:, 72 + 2 * t:73 + 2 * t],
                                           st[:, 73 + 2 * t:74 + 2 * t], ALU.add))
                    settle()
                    dve.tensor_scalar(st[:, 76 + t:77 + t], st[:, 72 + 2 * t:73 + 2 * t], 1.0 / D, EPS, ALU.mult,
                                      ALU.add).then_inc(event("o_var"), 1)
                    dve.wait_ge(event("o_std"), l * TT + (t + 1))
                    step(dve.reciprocal(st[:, 8 + t:9 + t], st[:, 78 + t:79 + t]))
                    settle()
                    step(dve.scalar_tensor_tensor(Y[:, t, :], Y[:, t, :], st[:, 8 + t:9 + t], gpb[:], ALU.mult, ALU.mult))
                    settle()
                    dve.tensor_tensor(X[:, t, :], X[:, t, :], Y[:, t, :], ALU.add).then_inc(event("x_ready"), 1)
                counted("DVE_STEPS", steps[0], DVE_STEPS)

            base[0], steps[0] = before + DEPTH * DVE_STEPS, 0
            sink = col[:, C_SINK:C_SINK + 8]

            def modulate2(n):
                for v in range(2):
                    step(dve.scalar_tensor_tensor(hsc2[:, v, :], mod[:, 8:16, v], 1.0,
                                                  col[:, C_NG + 8 * n:C_NG + 8 * n + 8], ALU.add, ALU.mult))
                    ins = dve.tensor_copy(hsh2[:, v, :], mod[:, 0:8, v])
                    if v == 0:
                        step(ins)
                ins.then_inc(event("hmod2"), 1)

            def diagonal(dst, v):
                dve.tensor_tensor(dst, ident[:].unsqueeze(1).broadcast_to([P, KD, P]),
                                  mod[:, 16:24, v].unsqueeze(2).broadcast_to([P, KD, P]), ALU.mult).then_inc(event("diag_ready"), 1)

            def norm_x2(u, n):
                dve.wait_ge(event("h2_ssq"), NT * (n + 1))
                dve.tensor_scalar(st2[:, 4:8], st2[:, 0:4], 1.0 / D, EPS, ALU.mult, ALU.add).then_inc(event("h2_var"), 1)
                dve.wait_ge(event("h2_std"), n + 1)
                step(dve.reciprocal(st2[:, 28:32], st2[:, 8:12]))
                settle()
                for t in range(NT):
                    dve.tensor_scalar(Y2[:, t, :], X[:, t, :], st2[:, 28 + t:29 + t], None, ALU.mult).then_inc(event("h2_ready"), 1)
                dve.wait_ge(event("hmod2"), n + 1)
                for t in range(NT):
                    v = t // TT
                    ps = filled(dve, u, f"xT{t}1")
                    for k in range(4):
                        ins = dve.tensor_scalar(hT2[:, 4 + k, t * P:(t + 1) * P], ps[:, k * P:(k + 1) * P],
                                                hsc2[:, v, 4 + k:5 + k], hsh2[:, v, 4 + k:5 + k], ALU.mult, ALU.add)
                        if k < 3:
                            step(ins)
                    ins.then_inc(free(u, f"xT{t}1"), 1)

            def add_out(u, name, t, v, ready):
                for h in range(2):
                    ps = filled(dve, u, f"{name}{t}{h}")
                    c = slice(h * 512, (h + 1) * 512)
                    dve.tensor_tensor(Y2[:, t, c], ps[:, :], gbr[:, v, c], ALU.mult).then_inc(free(u, f"{name}{t}{h}"), 1)
                    emptied(dve, u, f"{name}{t}{h}")
                    ins = dve.tensor_tensor(X[:, t, c], X[:, t, c], Y2[:, t, c], ALU.add)
                    if h == 0:
                        step(ins)
                ins.then_inc(event(ready), 1)

            u = le
            dve.wait_ge(event("x_ready"), DEPTH * TT + 1)
            dve.wait_ge(event("ctx_in"), 32)
            emptied(dve, lay1, "ada4", DEPTH - 1)
            emptied(dve, lay1, "ada5", DEPTH - 1)
            step(dve.tensor_scalar(nsink[:], sink, -1.0, None, ALU.mult))
            modulate2(0)
            for v in range(2):
                diagonal(DG2[v], v)
            norm_x2(u, 0)
            for t in range(NT):
                emptied(dve, u, f"e_vv{t}")
                step(dve.tensor_scalar(st2[:, 12 + t:13 + t], st2[:, 12 + t:13 + t], 1.0 / 512, None, ALU.mult))
                settle()
                dve.tensor_scalar(evv[:, t, :], evv[:, t, :], st2[:, 12 + t:13 + t], None, ALU.subtract).then_inc(event("ln_c"), 1)
            dve.wait_ge(event("ln_ssq"), NT)
            dve.tensor_scalar(st2[:, 20:24], st2[:, 16:20], 1.0 / 512, EPS, ALU.mult, ALU.add).then_inc(event("ln_var"), 1)
            dve.wait_ge(event("ln_std"), 1)
            step(dve.reciprocal(st2[:, 54:58], st2[:, 24:28]))
            settle()
            for t in range(NT):
                step(dve.scalar_tensor_tensor(evv[:, t, :], evv[:, t, :], st2[:, 54 + t:55 + t], lng, ALU.mult, ALU.mult))
                settle()
                dve.tensor_tensor(evv[:, t, :], evv[:, t, :], lnb, ALU.add).then_inc(event("ln_ready"), 1)

            def e_gated(t):
                dve.wait_ge(event("e_es"), t + 1)
                if t < TT:
                    dve.wait_ge(event("e_exp"), E_LAST[t] + 1)
                else:
                    emptied(dve, u, f"el{E_LAST[t]}")
                step(dve.tensor_tensor(r2[:, t, 0:8], sm2[:, t, 0:8], es2[:, t, :], ALU.add))
                settle()
                step(dve.reciprocal(r2[:, t, 0:8], r2[:, t, 0:8]))
                settle()
                ps = filled(dve, u, f"eo{t}")
                dve.tensor_tensor(etmp.rearrange("p (h d) -> p h d", h=8), ps[:, :].rearrange("p (h d) -> p h d", h=8),
                                  r2[:, t, 0:8].unsqueeze(2).broadcast_to([P, 8, 64]), ALU.mult).then_inc(free(u, f"eo{t}"), 1)
                emptied(dve, u, f"eo{t}")
                dve.tensor_tensor(eg[:, t, 0:512], etmp, eg[:, t, 0:512], ALU.mult).then_inc(event("em_ready"), 1)
                dve.wait_ge(event("em_ready"), t + 1)

            for g in range(14):
                if g < 12:
                    for i in (2 * g, 2 * g + 1):
                        t, heads = E_UNITS[i]
                        nh = len(heads)
                        ps = filled(dve, u, f"el{i}")
                        m = mx2[:, t, heads[0]:heads[-1] + 1:2] if nh > 1 else mx2[:, t, heads[0]:heads[0] + 1]
                        ns = nsink[:, heads[0]:heads[-1] + 1:2] if nh > 1 else nsink[:, heads[0]:heads[0] + 1]
                        if t < TT:
                            dve.scalar_tensor_tensor(L2[:, i % 4, :], ps[:, :], 0.125, near[:, t, :], ALU.mult,
                                                     ALU.add).then_inc(free(u, f"el{i}"), 1)
                            emptied(dve, u, f"el{i}")
                            step(dve.tensor_reduce(m, L2[:, i % 4, :], AX, ALU.max, negate=True))
                            settle()
                            dve.tensor_tensor(m, m, ns, ALU.min).then_inc(event("e_max"), 1)
                        else:
                            step(dve.tensor_reduce(m, ps[:, :].rearrange("p (h n) -> p h n", h=nh), AX, ALU.max, negate=True))
                            settle()
                            dve.scalar_tensor_tensor(m, m, 0.125, ns, ALU.mult, ALU.min).then_inc(event("e_max"), 1)
                for t in range(NT):
                    if g == E_LAST[t] // 2:
                        dve.wait_ge(event("e_max"), E_LAST[t] + 1)
                        dve.tensor_tensor(es2[:, t, :], mx2[:, t, 0:8], sink, ALU.add).then_inc(event("e_arg"), 1)
                if g in E_ADA:
                    mod_out(u, f"ada{E_ADA[g]}", E_ADA[g], 3, 2)
                if g + 1 in E_ADA:
                    m = E_ADA[g + 1]
                    mod_sum(CH2, [n for n, _ in CH2].index(f"ada{m}"), BASE2, msum2[m % 2], 2, cnow)
                if g == 7:
                    for j in range(4):
                        ps = filled(dve, u, f"gs{j}")
                        for a in range(2):
                            q = 2 * j + a
                            uv = eu[:, :, q * 64:(q + 1) * 64]
                            ins = dve.scalar_tensor_tensor(uv, ps[:, a * 256:(a + 1) * 256].rearrange("p (t c) -> p t c", t=NT),
                                                           col[:, C_BS + q:C_BS + q + 1], uv, ALU.add, ALU.mult)
                            if a == 0:
                                step(ins)
                        ins.then_inc(free(u, f"gs{j}"), 1)
                if g == 9:
                    for j in range(4):
                        emptied(dve, u, f"gs{j}")
                    dve.wait_ge(event("esilu"), 1)
                    step(dve.tensor_tensor(eg[:, :, 512:1024], eu[:], eg[:, :, 512:1024], ALU.mult))
                    e_gated(0)
                if g == 10:
                    e_gated(1)
                if g == 12:
                    e_gated(2)
            e_gated(3)
            for t in range(NT):
                ps = filled(dve, u, f"eyT{t}1")
                dve.tensor_copy(hT2[:, 4:8, t * P:(t + 1) * P], ps[:, :].rearrange("p (k c) -> p k c", k=4)).then_inc(free(u, f"eyT{t}1"), 1)
            for t in range(NT):
                add_out(u, "eout", t, t // TT, "x2_ready")

            u = lo
            for m in range(4, 6):
                emptied(dve, le, f"ada{m}")
            dve.wait_ge(event("x2_ready"), NT)
            modulate2(1)
            diagonal(DG3, 0)
            norm_x2(u, 1)
            dve.wait_ge(event("o_ssq2"), NT + TT)
            step(dve.tensor_scalar(st2[:, 40:44], st2[:, 32:36], 1.0 / 128, EPS, ALU.mult, ALU.add))
            dve.tensor_scalar(st2[:, 44:46], st2[:, 36:38], 1.0 / 256, EPS, ALU.mult, ALU.add).then_inc(event("o_var2"), 1)
            dve.wait_ge(event("o_std2"), 1)
            step(dve.reciprocal(st2[:, 58:64], st2[:, 48:54]))
            settle()
            for t in range(NT):
                ins = dve.tensor_scalar(okv[:, t, 0:P], okv[:, t, 0:P], st2[:, 58 + t:59 + t], None, ALU.mult)
                if t < NT - 1:
                    step(ins)
            ins.then_inc(event("okv_ready"), 1)
            for t in range(TT):
                ins = dve.tensor_scalar(oqa[:, t, :], oqa[:, t, :], st2[:, 62 + t:63 + t], None, ALU.mult)
                if t < TT - 1:
                    step(ins)
            ins.then_inc(event("oqa_ready"), 1)
            for h in range(1, MLA_HEADS, 2):
                ps = filled(dve, u, f"on{h}")
                dve.tensor_copy(okT[0:MLA_NOPE, h, :], ps[0:MLA_NOPE, :]).then_inc(free(u, f"on{h}"), 1)
            for t in range(NT):
                ps = filled(dve, u, f"ov{t}1")
                dve.tensor_copy(ova[:, t, 512:1024], ps[:, :]).then_inc(free(u, f"ov{t}1"), 1)
            for t in range(TT):
                ps = filled(dve, u, f"oqb{t}1")
                dve.tensor_copy(q2[:, t, 512:1024], ps[:, :]).then_inc(free(u, f"oqb{t}1"), 1)
            for j in range(1, 8, 2):
                ps = filled(dve, u, f"oqT{j}")
                dve.tensor_copy(oqT[:, 2 * j:2 * j + 2, :], ps[0:MLA_QK, :].rearrange("p (a b) -> p a b", a=2)).then_inc(free(u, f"oqT{j}"), 1)

            def o_gated(q):
                t, h0 = q // 2, 8 * (q % 2)
                emptied(dve, u, f"ml{8 * q + 7}")
                step(dve.reciprocal(r2[:, t, h0:h0 + 8], sm2[:, t, h0:h0 + 8]))
                settle()
                ps = filled(dve, u, f"mo{q}")
                dve.tensor_tensor(otmp.rearrange("p (h d) -> p h d", h=8), ps[:, :].rearrange("p (h d) -> p h d", h=8),
                                  r2[:, t, h0:h0 + 8].unsqueeze(2).broadcast_to([P, 8, 64]), ALU.mult).then_inc(free(u, f"mo{q}"), 1)
                emptied(dve, u, f"mo{q}")
                dve.wait_ge(event("osilu"), 1)
                gv = og[:, t, h0 * 64:h0 * 64 + 512]
                ins = dve.tensor_tensor(gv, otmp, gv, ALU.mult)
                if q % 2:
                    ins.then_inc(event("om_ready"), 1)
                    dve.wait_ge(event("om_ready"), t + 1)
                else:
                    step(ins)
                    settle()

            for p in range(19):
                if p < 16:
                    for i in (2 * p, 2 * p + 1):
                        t, h = O_UNITS[i]
                        ps = filled(dve, u, f"ml{i}")
                        step(dve.tensor_reduce(mx2[:, t, h:h + 1], ps[:, :], AX, ALU.max, negate=True))
                        settle()
                        dve.tensor_scalar(mx2[:, t, h:h + 1], mx2[:, t, h:h + 1], MLA_SCALE, None, ALU.mult).then_inc(event("o_max"), 1)
                if 1 <= p < 17:
                    i = 2 * p - 1
                    ps = filled(dve, u, f"mp{i}")
                    dve.tensor_copy(PT2[:, i % 4, :], ps[:, :]).then_inc(free(u, f"mp{i}"), 1)
                if p >= 6 and (p - 6) % 4 == 0:
                    o_gated((p - 6) // 4)
            for t in range(TT):
                ps = filled(dve, u, f"oyT{t}1")
                dve.tensor_copy(hT2[:, 4:8, t * P:(t + 1) * P], ps[:, :].rearrange("p (k c) -> p k c", k=4)).then_inc(free(u, f"oyT{t}1"), 1)
            for t in range(TT):
                add_out(u, "oout", t, 0, "x3_ready")
                if t == 0:
                    dve.wait_ge(event("fing_in"), 16)
                dve.wait_ge(event("f_ssq"), t + 1)
                dve.tensor_scalar(st2[:, 4 + t:5 + t], st2[:, t:t + 1], 1.0 / D, EPS, ALU.mult, ALU.add).then_inc(event("f_var"), 1)
                dve.wait_ge(event("f_std"), t + 1)
                step(dve.reciprocal(st2[:, 28 + t:29 + t], st2[:, 8 + t:9 + t]))
                settle()
                dve.scalar_tensor_tensor(Y2[:, t, :], X[:, t, :], st2[:, 28 + t:29 + t], fing, ALU.mult,
                                         ALU.mult).then_inc(event("out_ready"), 1)

def chunk_of(w, k):
    return w.reshape(k, P, w.shape[1]).transpose(1, 0, 2).reshape(P, -1)


def lay_out(i):
    w = []
    cols1 = lambda l, n: i["w_in"][l][:, IN1[n][0]:IN1[n][0] + IN1[n][1]]
    ada = [i["ada_w"][0], i["ada_w"][1], i["w_ada_2"][0], i["w_ada_2"][1]]

    def ada_part(a, m):
        return chunk_of(ada[a][:, m * 512:(m + 1) * 512], KD)

    for m in range(MERGES):
        w.append(ada_part(0, m))
    for l in range(DEPTH):
        for name, width in CH1:
            if name == "idx":
                a = np.concatenate([cols1(l, n) for n in ("idx_q", "idx_k", "idx_w", "gla_a")], 1)
            elif name == "gla_qk":
                a = np.concatenate([cols1(l, n) for n in ("gla_q", "gla_k")], 1)
            elif name == "dsa_kv":
                a = np.concatenate([cols1(l, n) for n in ("dsa_k", "dsa_v")], 1)
            elif name == "ret_qk":
                a = np.concatenate([cols1(l, n) for n in ("ret_q", "ret_k")], 1)
            elif name.startswith("merge"):
                m = int(name[5])
                a = cols1(l, "merge")[:, m * 512:(m + 1) * 512]
            elif name.startswith("ada"):
                w.append(ada_part(l + 1, int(name[3])))
                continue
            elif name.startswith("br"):
                w.append(chunk_of(i[("w_br_ret", "w_br_dsa", "w_br_gla")[int(name[2])]][l], 4))
                continue
            elif name.startswith("out"):
                h = int(name[3])
                a = i["w_out"][l][:, h * 512:(h + 1) * 512]
            else:
                a = cols1(l, name)
            w.append(chunk_of(a, KD))
            assert w[-1].shape[1] == width, name
    we, wo = i["w_in0_2"][0], i["w_in1_2"][0]
    heads = i["w_kvb_2"][0].reshape(P, MLA_HEADS, MLA_NOPE + MLA_V)
    more = {
        "e_kv": we[:, 512:768], "e_q": we[:, 0:512], "e_u": we[:, 768:1280], "e_vv": we[:, 1280:1792],
        "e_g0": we[:, 1792:2304], "e_g1": we[:, 2304:2816],
        "e_o0": i["w_out0_2"][0][:, 0:512], "e_o1": i["w_out0_2"][0][:, 512:1024],
        "o_kv": wo[:, 256:416], "o_q": wo[:, 0:256], "o_g0": wo[:, 416:928], "o_g1": wo[:, 928:1440],
        "o_kvb": np.concatenate([heads[:, :, 0:MLA_NOPE].reshape(P, -1), heads[:, :, MLA_NOPE:].reshape(P, -1)], 1),
        "o_qb": i["w_qb_2"][0], "o_o0": i["w_out1_2"][0][:, 0:512], "o_o1": i["w_out1_2"][0][:, 512:1024],
    }
    for name, width in CH2:
        if name == "e_ws":
            w.append(i["gm_ws_2"][0].transpose(2, 0, 1).reshape(P, -1))
        elif name.startswith("ada"):
            w.append(ada_part(3, int(name[3])))
        else:
            w.append(chunk_of(more[name], more[name].shape[0] // P))
        assert w[-1].shape[1] == width, name
    weights = np.zeros((len(w), P, SLOT), np.float32)
    for n, a in enumerate(w):
        weights[n, :, 0:a.shape[1]] = a

    def column(v):
        return np.asarray(v).reshape(-1, P).T

    cols = np.zeros((P, N_COLS), np.float32)
    for v, name in enumerate((i["c"][0], i["c_2"][0], i["c_ctx_2"])):
        cols[:, C_CT + v:C_CT + 24:3] = column(name)
    for a, b in enumerate((i["ada_b"][0], i["ada_b"][1], i["b_ada_2"][0], i["b_ada_2"][1])):
        cols[:, C_ADAB + 24 * a:C_ADAB + 24 * a + 24] = column(b)
    for l in range(DEPTH):
        at = C_LAY + l * LAYC
        cols[:, at:at + 8] = column(i["pre_norm"][l])
        cols[:, at + 8:at + 16] = column(i["post_norm"][l])
        cols[:, at + 16:at + 18] = column(i["gla_b_lr"][l])
        cols[:, C_NG + 8 * l:C_NG + 8 * l + 8] = column(i["norm_g_2"][l])
    cols[:, C_QN:C_QN + 2] = column(i["q_norm_2"][0])
    cols[:, C_KVN:C_KVN + 1] = column(i["kv_norm_2"][0])
    cols[:, C_BS:C_BS + 8] = i["gm_bs_2"][0].T
    cols[:, C_SINK:C_SINK + 8] = i["sink0_2"][0][None, :]

    a = np.arange(P)
    k1 = np.zeros((P, N_K1), np.float32)
    for h in range(4):
        lg = np.log1p(-np.exp2(-5.0 - h))
        rel = np.arange(S)[None, :] - a[:, None]
        full = np.where(rel >= 0, np.exp(lg * np.maximum(rel, 0)), 0.0) * 0.125
        k1[:, K_DECAY + 384 * h:K_DECAY + 384 * h + 256] = full
        k1[:, K_DECAY + 384 * h + 256:K_DECAY + 384 * h + 384] = full[:, 0:P]
    k1[:, K_CM + P:K_CM + 2 * P] = np.where(a[None, :] > a[:, None], NEG, 0.0)
    k1[:, K_RESET:K_RESET + S] = (np.arange(S) % GLA_CHUNK != 0)[None, :]
    f = np.float32
    k1[:, K_FREQ:K_FREQ + 32] = f(10000.0) ** (-np.arange(32, dtype=f) * f(2.0) / f(64))
    k1[:, K_FREQ + 32:K_FREQ + 40] = f(500000.0) ** (-np.arange(8, dtype=f) * f(2.0) / f(16))
    gmask = np.zeros((P, len(HALVES), P), np.float32)
    key, query = a[:, None], a[None, :]
    for n, h in enumerate(HALVES):
        gmask[:, n, :] = (key // (2 * h) == query // (2 * h)) & (key % (2 * h) < h) & (query % (2 * h) >= h)
    k2 = np.zeros((P, N_K2 + D), np.float32)
    for at, half in ((K_EROT, 16), (K_OROT, 8)):
        inv = f(10000.0) ** (-np.arange(half, dtype=f) / f(half))
        for t in range(TT):
            tok = t * P + a
            for rc, p in enumerate((tok // 64, tok % 64)):
                ang = p.astype(f)[:, None] * inv[None, :]
                for q, v in enumerate((np.cos(ang), np.sin(ang))):
                    c0 = at + (q * TT + t) * 2 * half + rc * half
                    k2[:, c0:c0 + half] = v
    k2[:, K_NEAR + P:K_NEAR + 2 * P] = np.where(a[None, :] <= a[:, None], 0.0, NEG)
    k2[:, K_NEAR + 512:K_NEAR + 512 + P] = np.where(a[:, None] <= a[None, :], 0.0, NEG)
    k2[:, K_LNG:K_LNG + 512] = i["gm_ln_g_2"][0][None, :]
    k2[:, K_LNB:K_LNB + 512] = i["gm_ln_b_2"][0][None, :]
    k2[:, N_K2:] = i["final_g_2"][None, :]
    return {
        "x": i["x"][0], "pos": np.ascontiguousarray(i["positions"][0].reshape(TT, P).T), "weights": weights,
        "cols": cols, "k1": k1, "gmask": gmask, "ident": np.eye(P, dtype=np.float32),
        "wlr": np.ascontiguousarray(i["gla_w_lr"].transpose(1, 0, 2)), "context": i["ctx_2"][0], "k2": k2,
    }


def kernel(**inputs):
    import concourse.bacc as _bacc
    from concourse.bass_utils import run_bass_kernel_spmd as _run

    arrays = {"in_" + k: np.ascontiguousarray(v) for k, v in lay_out({k: np.asarray(v) for k, v in inputs.items()}).items()}
    nc = _bacc.Bacc("TRN2", target_bir_lowering=False, num_devices=1)
    args = [nc.dram_tensor(k, v.shape, mybir.dt.from_np(v.dtype), kind="ExternalInput").ap() for k, v in arrays.items()]
    out = nc.dram_tensor("out", (1, S, D), F32, kind="ExternalOutput").ap()
    build(nc, *args, out)
    return _run(nc, [arrays], core_ids=[0]).results[0]["out"]
```

```python
from contextlib import ExitStack

import numpy as np
import concourse.bass as bass
from concourse import mybir
from concourse.alu_op_type import AluOpType as ALU

F32 = mybir.dt.float32
F32R = mybir.dt.float32r
I32 = mybir.dt.int32
U8 = mybir.dt.uint8
ACT = mybir.ActivationFunctionType
AX = mybir.AxisListType.X

P = 128
D = 1024
KD = D // P
S = 256
TT = S // P
CT = 256 // P
DEPTH = 2
EPS = 1e-6
NEG = -1e30
TAKEN = -3e38
TOPK = 64
RING = 3
SLOT = 4096

IN1 = {}
_at = 0
for _n, _w in (("ret_q", 256), ("ret_k", 256), ("ret_v", 512), ("ret_g", 512), ("dsa_q", 512),
               ("dsa_k", 128), ("dsa_v", 128), ("dsa_g", 512), ("idx_q", 256), ("idx_k", 64),
               ("idx_w", 4), ("gla_q", 256), ("gla_k", 256), ("gla_v", 512), ("gla_g", 512),
               ("gla_a", 16), ("merge", 3072)):
    IN1[_n] = (_at, _w)
    _at += _w
RANK = 16

MERGES = 6
CH1 = [("idx", KD * 340), ("dsa_q", KD * 512), ("gla_qk", KD * 512), ("dsa_kv", KD * 256),
       ("ret_qk", KD * 512), ("ret_v", KD * 512), ("gla_v", KD * 512), ("ret_g", KD * 512),
       ("dsa_g", KD * 512), ("gla_g", KD * 512)]
for _m in range(MERGES):
    CH1 += [(f"merge{_m}", KD * 512), (f"ada{_m}", KD * 512)]
CH1 += [("br0", 4 * D), ("br1", 4 * D), ("br2", 4 * D), ("out0", KD * 512), ("out1", KD * 512)]
SHIFTS = 4
CH0 = [(f"ada{_m}", KD * 512) for _m in range(SHIFTS)]
CHE = [("e_kv", KD * 256), ("e_q", KD * 512), ("e_u", KD * 512), ("e_vv", KD * 512),
       ("e_g0", KD * 512), ("adag4", KD * 512), ("e_g1", KD * 512), ("adag5", KD * 512), ("ada0", KD * 512),
       ("e_ws", KD * P), ("ada1", KD * 512), ("e_o0", KD * 512), ("ada2", KD * 512),
       ("e_o1", KD * 512), ("ada3", KD * 512)]
CHO = [("o_kv", KD * 160), ("o_q", KD * 256), ("adah4", KD * 512), ("o_g0", KD * 512), ("o_kvb", 2048),
       ("o_qb", 2 * 1536), ("o_g1", KD * 512), ("adah5", KD * 512), ("o_o0", KD * 512), ("o_o1", KD * 512)]
CH2 = CHE + CHO
NT = TT + CT
E_UNITS = [(t, (h,)) for t in range(TT) for h in (0, 2, 4, 6, 1, 3, 5, 7)]
E_UNITS += [(t, hs) for t in range(TT, NT) for hs in ((0, 2), (4, 6), (1, 3), (5, 7))]
E_SUM = {0: ("adag4", range(KD)), 5: ("adag5", range(KD)), 6: ("ada0", range(KD))}
E_SUM.update({9 + _n: ("ada1", range(2 * _n, 2 * _n + 2)) for _n in range(4)})
E_ADA = {2: "adag4", 7: "adag5", 8: "ada0", 13: "ada1"}
E_ORDER, O_ORDER = (2, 3, 0, 1), (0, 1, 2, 3)
BUFFERS, PIECE = 4, 512
PIECES1 = [(_n, _i, _w) for _n, _w in (("dsa_q", 512), ("dsa_kv", 256), ("ret_qk", 512), ("ret_v", 512), ("gla_v", 512),
                                     ("ret_g", 512), ("dsa_g", 512), ("gla_g", 512))
           for _i in range(KD * _w // PIECE)]
assert len(PIECES1) % BUFFERS == 0
E_SPLIT = ("e_q", "e_u", "e_vv")
SPLIT_PIECES = 4
E_LAST = {t: max(i for i, (a, _) in enumerate(E_UNITS) if a == t) for t in range(NT)}
MLA_HEADS, MLA_QK, MLA_NOPE, MLA_V = 16, 96, 64, 64
O_UNITS = [(t, h) for t in range(TT) for h in range(MLA_HEADS)]
MLA_SCALE = MLA_QK ** -0.5
assert len(CH1) % RING == 0 and len(CH0) > RING

HALVES = [1, 2, 4, 8, 16, 32, 64]
LEVELS = ["diag"] + HALVES + ["cross"]
GLA_CHUNK = 64

DSA_UNITS = [(0, (0, 2, 4, 6)), (0, (1, 3, 5, 7)), (1, (0, 2)), (1, (4, 6)), (1, (1, 3)), (1, (5, 7))]
PARTS = [0, 4, 0, 2, 4, 6]

ACT_STEPS = 35
DVE_STEPS = 212
POOL_STEPS = 13
LOADS = 3 * 16
TWO_PI = (6.28125, 0.0019350051879882812, 3.0199159819567e-07)
ROUND = 12582912.0
PI_BELOW = 3.1415925

C_CT, C_ADAB, C_LAY, C_NG, C_QN, C_KVN, C_BS, C_SINK = 0, 24, 120, 156, 172, 174, 175, 183
N_COLS = 191
LAYC = 18
K_DECAY, K_CM, K_RESET, K_FREQ = 0, 1536, 1792, 2048
N_K1 = 2088
K_EROT, K_OROT, K_NEAR, K_LNG, K_LNB = 0, 128, 192, 1216, 1728
N_K2 = 2240


class Units:

    def __init__(self, units, before=None):
        self.start = dict(before.end) if before else {b: 0 for b in range(8)}
        self.at, self.per = {}, {b: 0 for b in range(8)}
        for name, bank in units:
            assert name not in self.at, name
            self.at[name] = (bank, self.per[bank])
            self.per[bank] += 1
        self.end = {b: self.start[b] + self.per[b] for b in range(8)}

    def repeated(self, times):
        self.end = {b: self.start[b] + times * self.per[b] for b in range(8)}
        return self

    def count(self, name, rep=0):
        bank, n = self.at[name]
        return bank, rep * self.per[bank] + (self.start[bank] + n)


def units_of_layer1():
    u = [(f"xT{t}{h}", 2 + 2 * t + h) for t in range(TT) for h in range(2)]
    u += [("idx0", 0), ("idx1", 1), ("aT", 5), ("dsa_q0", 6), ("dsa_q1", 7)]
    u += [("qiT", 2), ("kiT", 3), ("gq", 0), ("gk", 1)]
    u += [("s00", 2), ("s01", 3), ("s10", 4), ("s11", 5), ("z", 2)]
    u += [("dsa_kv0", 6), ("dsa_kv1", 7), ("ret_qk0", 0), ("ret_qk1", 1)]
    u += [("dqT0", 2), ("dqT1", 3), ("dkT", 4)]
    u += [("ret_v0", 6), ("ret_v1", 7), ("gla_v0", 0), ("gla_v1", 1), ("rqT", 2), ("rkT", 3)]
    gap = [[("rs0", 4), ("ro0", 6), ("ro1", 7), ("g0_0", 2), ("g0_1", 3)]]
    gap += [[(f"rs{g}", 4), (f"g{g}_0", 2), (f"g{g}_1", 3)] for g in (1, 2, 3)]
    gap += [[("g4_0", 2), ("g4_1", 3)]]
    gap += [[("dl0", 4), ("g5_0", 2), ("g5_1", 3)]]
    gap += [[("dl1", 4), ("dp0", 5), ("g6_0", 2), ("g6_1", 3)]]
    gap += [[("dl2", 4), ("dp1", 5), ("do0", 6), ("g7_0", 2), ("g7_1", 3)]]
    gap += [[("dl3", 4), ("dp2", 5), ("g8_0", 2), ("g8_1", 3)]]
    gap += [[("dl4", 4), ("dp3", 5), ("do1", 7), ("go0", 2), ("go1", 3)]]
    gap += [[("dl5", 4), ("dp4", 5)]]
    gap += [[("dp5", 5), ("retT0", 2), ("retT1", 3)]]
    gap += [[("glaT0", 2), ("glaT1", 3)]]
    gap += [[("dsaT0", 4), ("dsaT1", 5)]]
    proj = ["ret_g0", "ret_g1", "dsa_g0", "dsa_g1", "gla_g0", "gla_g1"]
    for m in range(MERGES):
        proj += [f"merge{m}0", f"merge{m}1"]
    n = 0
    for g, name in enumerate(proj):
        u.append((name, n % 2))
        n += 1
        if g < len(gap):
            u += gap[g]
        if name.startswith("merge") and name.endswith("1") and name[5] != "0":
            u.append((f"ada{int(name[5]) - 1}", n % 2))
            n += 1
    n = 3
    for b in range(3):
        for t in range(TT):
            for h in range(2):
                u.append((f"br{b}{t}{h}", n % 8))
                n += 1
        if b == 0:
            u.append((f"ada{MERGES - 1}", n % 8))
            n += 1
    u += [(f"yT{t}{h}", 4 + 2 * t + h) for t in range(TT) for h in range(2)]
    u += [("out00", 0), ("out01", 1), ("gb0", 6), ("gb1", 7), ("out10", 2), ("out11", 3)]
    return u


def units_of_layer_e():
    n = [0, 0]

    def turn():
        n[0] += 1
        return 2 + (n[0] - 1) % 6

    def proj():
        n[1] += 1
        return (n[1] - 1) % 2

    u = [(f"xT{t}{h}", turn()) for t in E_ORDER for h in range(2)]
    u += [(f"e_kv{t}", i) for i, t in enumerate(E_ORDER)]
    for i, name in enumerate(E_SPLIT):
        u += [(f"{name}{t}", 4 * ((i + 1) % 2) + t) for t in range(NT)]
    u += [(f"ekT{j}", turn()) for j in range(2)] + [(f"eqT{j}", turn()) for j in range(4)]
    for g in range(14):
        if g < 8:
            u.append((f"e_g{g // 4}{g % 4}", proj()))
        if g in E_ADA:
            u.append((E_ADA[g], proj()))
        if g in (9, 11):
            u += [(f"gb{(g - 9) // 2}{h}", proj()) for h in range(2)]
        if g < 12:
            u += [(f"el{2 * g}", 4), (f"el{2 * g + 1}", 5)]
        if 1 <= g < 13:
            u += [(f"ep{2 * g - 2}", 6), (f"ep{2 * g - 1}", 7)]
        if g >= 2:
            for i in (2 * g - 4, 2 * g - 3):
                t = E_UNITS[i][0]
                if E_UNITS[i - 1][0] != t or i == 0:
                    u.append((f"eo{t}", 2 + t % 2))
        if g == 7:
            u += [(f"gs{j}", proj()) for j in range(4)]
    u += [(f"eyT{t}{h}", turn()) for t in range(NT) for h in range(2)]
    u += [(f"eout{t}0", turn()) for t in range(NT)] + [("ada2", proj())]
    u += [(f"eout{t}1", turn()) for t in range(NT - 1)] + [("ada3", proj()), (f"eout{NT - 1}1", turn())]
    return u


def units_of_layer_o():
    n = [0, 0]

    def turn():
        n[0] += 1
        return 2 + (n[0] - 1) % 6

    def proj():
        n[1] += 1
        return (n[1] - 1) % 2

    u = [(f"xT{t}{h}", turn()) for t in range(NT) for h in range(2)]
    u += [(f"o_kv{t}", proj()) for t in range(NT)] + [(f"o_q{t}", proj()) for t in range(TT)]
    u += [("adah4", proj())]
    u += [(f"o_g0{t}", proj()) for t in range(TT)]
    u += [("kvT", turn()), ("kpT", turn())]
    u += [(f"on{h}", turn()) for h in range(MLA_HEADS)]
    u += [(f"ov{t}{h}", turn()) for t in range(NT) for h in range(2)]
    u += [("qaT", turn())]
    u += [(f"oqb{t}{c}", turn()) for t in range(TT) for c in range(3)]
    u += [(f"o_g1{t}", proj()) for t in range(TT)]
    u += [(f"oqT{j}", turn()) for j in range(8)] + [("adah5", proj())]
    for p in range(16 + 2):
        if p < 16:
            b = (4, 0)[p % 2]
            u += [(f"ml{2 * p}", b), (f"ml{2 * p + 1}", b + 1)]
        if p == 0:
            u += [(f"gb0{h}", proj()) for h in range(2)]
        if 1 <= p < 17:
            u += [(f"mp{2 * p - 2}", 6), (f"mp{2 * p - 1}", 7)]
        if p >= 2:
            i = 2 * p - 4
            if i % 8 == 0:
                u.append((f"mo{i // 8}", 2 + (i // 8) % 2))
    u += [(f"oyT{t}{h}", turn()) for t in range(TT) for h in range(2)]
    u += [(f"oout{t}{h}", turn()) for t in range(TT) for h in range(2)]
    return u


def build(nc, x, pos, weights, cols, k1, gmask, ident_in, wlr, context, k2, out):
    ctx = ExitStack()
    with ctx:
        def sem(name):
            return ctx.enter_context(nc.semaphore(name))

        def pool_of(stack):
            return lambda name, shape, dt=F32: stack.enter_context(nc.sbuf_tensor(name, shape, dt))

        def first_of(name, shape):
            with ExitStack() as own:
                return own.enter_context(nc.sbuf_tensor(name, shape, F32))

        sb = pool_of(ctx)
        bank = [ctx.enter_context(nc.psum_tensor(f"bank{b}", [P, 512], F32)) for b in range(8)]
        ring = sb("ring", [P, RING, SLOT])
        X = first_of("X", [P, TT + CT, D])
        sb("x_rows", [P, TT, D])
        xhi1 = sb("xhi1", [P, KD, S], F32R)
        ident = sb("ident", [P, P])
        ones = sb("ones", [P, P])
        col = sb("col", [P, N_COLS])
        cact = sb("cact", [P, KD, 3])
        mod = sb("mod", [P, 24, 2])
        cnow = sb("cnow", [P, KD, 2])
        pw = sb("pw", [P, 2])

        one = ExitStack()
        sb1 = pool_of(one)
        Y = sb1("Y", [P, TT, D])
        hT = sb1("hT", [P, KD, S])
        retqkv = sb1("retqkv", [P, TT, D])
        retg = sb1("retg", [P, TT, 512])
        dsaqkv = sb1("dsaqkv", [P, TT, 768])
        dsag = sb1("dsag", [P, TT, 512])
        idx = sb1("idx", [P, TT, 324])
        glav = sb1("glav", [P, TT, 512])
        glag = sb1("glag", [P, TT, 512])
        with ExitStack() as shared:
            G = pool_of(shared)("G", [P, TT, 3 * D])
            L = pool_of(shared)("L", [P, 2, 512])
            PT = pool_of(shared)("PT", [P, 2, 512])
        sb1("g_rows", [P, 3 * D])
        xlo1 = sb1("xlo1", [P, KD, S], F32R)
        whi1 = sb1("whi1", [P, BUFFERS, PIECE], F32R)
        wlo1 = sb1("wlo1", [P, BUFFERS, PIECE], F32R)
        with ExitStack() as shared:
            ti = pool_of(shared)("ti", [P, 4, TT * 40])
            kdi = pool_of(shared)("kdi", [P, TT, 2, 64])
            kdd = pool_of(shared)("kdd", [P, TT, 2, 2, 64])
        RS = sb1("RS", [P, 2, 384])
        sb1("k_rest", [P, 320])
        kc = sb1("kc", [P, N_K1])
        gm = sb1("gm", [P, len(HALVES), P], U8)
        wl_all = sb1("wl_all", [RANK, DEPTH, 256])
        wl = sb1("wl", [RANK, 256])
        lay = sb1("lay", [P, LAYC])
        hsc = sb1("hsc", [P, KD])
        hsh = sb1("hsh", [P, KD])
        gpo = sb1("gpo", [P, KD])
        gpb = sb1("gpb", [P, D])
        posi = sb1("posi", [P, TT], I32)
        posf = sb1("posf", [P, TT])
        ang = sb1("ang", [P, TT, 40])
        turn = sb1("turn", [P, TT, 40])
        cosT = sb1("cosT", [P, TT, 40])
        sinT = sb1("sinT", [P, TT, 40])
        st = sb1("st", [P, 96])
        junk = sb1("junk", [P, P])
        cw = sb1("cw", [P, 64])
        qiT = sb1("qiT", [P, 2, S])
        kiT = sb1("kiT", [P, S])
        qdT = sb1("qdT", [P, 4, S])
        kdT = sb1("kdT", [P, 2, S])
        qrT = sb1("qrT", [P, 2, S])
        krT = sb1("krT", [P, 2, S])
        gqT = sb1("gqT", [P, 2, S])
        gkT = sb1("gkT", [P, 2, S])
        bcum = sb1("bcum", [P, 2, S])
        KL = sb1("KL", [P, 2, 2, S])
        AT = sb1("AT", [P, 2, 3, 2, P])
        sc = sb1("sc", [P, 384])
        wk = sb1("wk", [P, 384])
        m8 = sb1("m8", [P, 8])
        mx = sb1("mx", [P, TT, 8])
        sm = sb1("sm", [P, TT, 8])
        aT = sb1("aT", [RANK, S])
        retT = X[:, 2, :].rearrange("p (k s) -> p k s", k=4)
        dsaT = X[:, 3, :].rearrange("p (k s) -> p k s", k=4)
        glaT = dsaqkv[:].rearrange("p t c -> p (t c)")[:, 0:1024].rearrange("p (k s) -> p k s", k=4)
        branchT = [retT, dsaT, glaT]
        DG = G[:, 0, 0:D].rearrange("p (k s) -> p k s", k=KD)
        RI = G[:, 0, 0:1536]
        Z = G[:, 0, 1536:2048].rearrange("p (f s) -> p f s", f=2)
        AZ = G[:, 0, 2048:2560].rearrange("p (f s) -> p f s", f=2)
        LG = G[:, 0, 2560:3072].rearrange("p (f s) -> p f s", f=2)
        Yf = Y[:].rearrange("p t d -> p (t d)")
        msum = retqkv[:].rearrange("p b (v c) -> p b v c", v=2)
        rt = Yf.rearrange("p (q n) -> p q n", q=4)
        gmf = G[:, 0, 0:len(HALVES) * P].rearrange("p (n c) -> p n c", n=len(HALVES))
        E = [Yf[:, 512 * i:512 * i + 512].rearrange("p (f s) -> p f s", f=2) for i in range(2)]
        QL = [Yf[:, 1024 + 512 * i:1536 + 512 * i].rearrange("p (f s) -> p f s", f=2) for i in range(2)]
        decay = kc[:, K_DECAY:K_DECAY + 1536].rearrange("p (h c) -> p h c", h=4)
        cm = kc[:, K_CM:K_CM + 256]
        reset = kc[:, K_RESET:K_RESET + 256]
        freq = kc[:, K_FREQ:K_FREQ + 40]
        one.close()

        two = ExitStack()
        sb2 = pool_of(two)
        Y2 = first_of("Y2", [P, NT, D])
        whi = sb2("whi", [P, 2, 1024], F32R)
        wlo = sb2("wlo", [P, 2, 1024], F32R)
        hT2 = sb2("hT2", [P, KD, NT * P])
        LP = first_of("LP", [P, 8, 512])
        L2 = LP[:, 0:4, :]
        PT2 = LP[:, 4:8, :]
        xhi = sb2("xhi", [P, KD, NT * P], F32R)
        gbr = sb2("gbr", [P, 2, D])
        hsc2 = sb2("hsc2", [P, 2, KD])
        hsh2 = sb2("hsh2", [P, 2, KD])
        st2 = sb2("st2", [P, 64])
        mx2 = sb2("mx2", [P, NT, 16])
        sm2 = sb2("sm2", [P, NT, 16])
        es2 = sb2("es2", [P, NT, 8])
        r2 = sb2("r2", [P, NT, 16])
        nsink = sb2("nsink", [P, 8])
        kk = sb2("kk", [P, N_K2])
        lay_e, lay_o = ExitStack(), ExitStack()
        sbe = pool_of(lay_e)
        eqk = sbe("eqk", [P, NT, 640])
        ev = sbe("ev", [P, NT, P])
        eu = sbe("eu", [P, NT, 512])
        evv = sbe("evv", [P, NT, 512])
        eg = first_of("eg", [P, NT, D])
        xlo = sbe("xlo", [P, KD, NT * P], F32R)
        eqT = sbe("eqT", [P, 4, NT * P])
        ekT = sbe("ekT", [P, 2, NT * P])
        ekd = sbe("ekd", [P, NT, 2, 2, 64])
        ert = sbe("ert", [P, 4, 320])
        lay_e.close()
        sbo = pool_of(lay_o)
        okT = sbo("okT", [MLA_QK, MLA_HEADS, NT * P])
        oqT = sbo("oqT", [MLA_QK, MLA_HEADS, S])
        ova = sbo("ova", [P, NT, D])
        og = sbo("og", [P, TT, D])
        lay_o.close()
        two.close()
        q2 = Y2[:].rearrange("p t d -> p (t d)")[:, 0:TT * 1536].rearrange("p (t c) -> p t c", t=TT)
        DG2 = evv[:, 2:4, :].rearrange("p t (k c) -> p (t k) c", k=KD // 2)
        DG3 = Y2[:, NT - 1, :].rearrange("p (k c) -> p k c", k=KD)
        msum3 = [L2[:, m:m + 1, :] for m in range(2)]
        e_rot = kk[:, K_EROT:K_EROT + 128].rearrange("p (q t c) -> p q t c", q=2, t=TT)
        o_rot = kk[:, K_OROT:K_OROT + 64].rearrange("p (q t c) -> p q t c", q=2, t=TT)
        near = kk[:, K_NEAR:K_NEAR + 1024].rearrange("p (t c) -> p t c", t=TT)
        lng, lnb = kk[:, K_LNG:K_LNG + 512], kk[:, K_LNB:K_LNB + 512]
        fing = gbr[:, 1, :]
        etmp = evv[:, 0, :]
        msum2 = [ekd[:].rearrange("p t a b c -> p (t a b c)").rearrange("p (v c) -> p v c", v=2),
                 ert[:].rearrange("p q c -> p (q c)")[:, 0:D].rearrange("p (v c) -> p v c", v=2)]
        otmp = Y2[:].rearrange("p t d -> p (t d)")[:, TT * 1536:TT * 1536 + 512]
        ort = near.rearrange("p t c -> p (t c)").rearrange("p (q c) -> p q c", q=4)
        okv = kk[:, K_LNG:K_LNG + NT * 160].rearrange("p (t c) -> p t c", t=NT)
        okp = kk[:, K_LNG + NT * 160:K_LNG + NT * (160 + MLA_QK)].rearrange("p (t c) -> p t c", t=NT)
        kvT, kpe = X[:, TT, 0:NT * P], X[0:MLA_QK, TT, NT * P:2 * NT * P]
        oqa = X[:, TT + 1, 0:TT * 256].rearrange("p (t c) -> p t c", t=TT)
        qaT = X[:, TT + 1, 512:512 + 2 * S].rearrange("p (k s) -> p k s", k=2)

        bank_full = [sem(f"bank_full{b}") for b in range(8)]
        bank_free = [sem(f"bank_free{b}") for b in range(8)]
        slot_full = [sem(f"slot_full{s}") for s in range(RING)]
        loaded = sem("loaded")
        stored = sem("stored")
        E_ = {}

        def event(name):
            if name not in E_:
                E_[name] = sem(name)
            return E_[name]

        pro = Units([(f"ada{m}", m % 2) for m in range(SHIFTS)])
        lay1 = Units(units_of_layer1(), pro).repeated(DEPTH)
        le = Units(units_of_layer_e(), lay1)
        lo = Units(units_of_layer_o(), le)
        BASE2 = len(CH0) + DEPTH * len(CH1)

        def sum_number(c):
            return SHIFTS + DEPTH * MERGES + sum(name.startswith("ada") for name, _ in CH2[:c + 1])

        def chunk2(name):
            return [n for n, _ in CH2].index(name)

        SPLIT1 = {name: q + 1 for q, (name, _, _) in enumerate(PIECES1)}
        ENDS1 = sorted(SPLIT1.values())
        INNER1 = len(PIECES1) - len(ENDS1)

        def piece1(q):
            name, i, _ = PIECES1[q]
            c = [n for n, _ in CH1].index(name)
            return c, i, ring[:, (len(CH0) + c) % RING, i * PIECE:(i + 1) * PIECE]

        def piece1_used(eng, q, l):
            if q + 1 in ENDS1:
                filled(eng, lay1, f"{PIECES1[q][0]}1", l)
            else:
                eng.wait_ge(event("piece1_used"), l * INNER1 + (q + 1 - sum(e <= q for e in ENDS1)))

        def piece(q):
            c, i = chunk2(E_SPLIT[q // SPLIT_PIECES]), q % SPLIT_PIECES
            return c, i, ring[:, (BASE2 + c) % RING, i * 1024:(i + 1) * 1024]

        def piece_used(eng, q):
            if q % SPLIT_PIECES == SPLIT_PIECES - 1:
                filled(eng, le, f"{E_SPLIT[q // SPLIT_PIECES]}{NT - 1}")
            else:
                eng.wait_ge(event("piece_used"), q - q // SPLIT_PIECES + 1)

        def last1(c):
            name = CH1[c][0]
            if name == "idx":
                return "aT"
            if name == "gla_qk":
                return "gk"
            if name.startswith("br"):
                return name + "11"
            if name.startswith("out"):
                return "out1" + name[3]
            return name + "1"

        def filled(eng, u, name, rep=0):
            b, n = u.count(name, rep)
            eng.wait_ge(bank_full[b], n + 1)
            return bank[b]

        def emptied(eng, u, name, rep=0):
            b, n = u.count(name, rep)
            eng.wait_ge(bank_free[b], n + 2)

        def free(u, name):
            return bank_free[u.at[name][0]]

        def shape_like(ps, dst):
            return ps if len(dst.shape) == 2 else ps.rearrange("p (a b) -> p a b", a=dst.shape[1])

        def counted(name, got, want):
            assert got == want, f"{name} has to be {got}"

        block = ctx.enter_context(nc.Block())

        @block.sync
        def _(sp):
            def load(n, slot, width):
                sp.dma_start(ring[:, slot, 0:width], weights[n][:, 0:width]).then_inc(slot_full[slot], 16)

            for c in range(RING):
                load(c, c, CH0[c][1])
            for c in range(RING, len(CH0)):
                sp.wait_ge(event("ada_sum"), c - RING + 1)
                load(c, c % RING, CH0[c][1])
            with sp.Fori(0, DEPTH) as l:
                for c, (name, width) in enumerate(CH1):
                    if c < RING:
                        sp.wait_ge(event("ada_sum"), len(CH0) - RING + c + 1)
                        b, n = lay1.count(("out00", "out10", "out11")[c])
                        assert n + 1 - lay1.per[b] == lay1.start[b]
                        sp.wait_ge(bank_full[b], l * lay1.per[b] + lay1.start[b])
                    elif CH1[c - RING][0].startswith("ada"):
                        sp.wait_ge(event("ada_sum"), l * MERGES + (SHIFTS + int(CH1[c - RING][0][3]) + 1))
                    elif CH1[c - RING][0] in SPLIT1:
                        sp.wait_ge(event("lo1_ready"), l * len(PIECES1) + SPLIT1[CH1[c - RING][0]])
                    else:
                        filled(sp, lay1, last1(c - RING), l)
                    slot = (len(CH0) + c) % RING
                    sp.dma_start(ring[:, slot, 0:width],
                                 weights[l * len(CH1) + (len(CH0) + c)][:, 0:width]).then_inc(slot_full[slot], 16)

            last2 = []
            for name, _ in CHE:
                last2.append((le, "gs3" if name == "e_ws" else name if name[0] == "a" else
                              f"eout{NT - 1}{name[3]}" if name[2] == "o" else
                              f"e_kv{E_ORDER[-1]}" if name == "e_kv" else f"{name}{NT - 1}"))
            for name, _ in CHO:
                last2.append((lo, {"o_kv": f"o_kv{NT - 1}", "o_q": "o_q1", "o_kvb": f"ov{NT - 1}1", "o_qb": "oqb12",
                                   "o_g0": "o_g01", "o_g1": "o_g11", "o_o0": "oout10", "o_o1": "oout11"}.get(name)))
            for c, (name, width) in enumerate(CH2):
                if c < RING:
                    filled(sp, lay1, ("out00", "out10", "out11")[c], DEPTH - 1)
                elif CH2[c - RING][0] in E_SPLIT:
                    sp.wait_ge(event("lo_ready"), SPLIT_PIECES * (E_SPLIT.index(CH2[c - RING][0]) + 1))
                elif CH2[c - RING][0].startswith("ada"):
                    sp.wait_ge(event("ada_sum"), sum_number(c - RING))
                else:
                    filled(sp, last2[c - RING][0], last2[c - RING][1])
                load(BASE2 + c, (BASE2 + c) % RING, width)
                if c == 0:
                    sp.dma_start(X[:, TT:NT, :], context.rearrange("(t p) d -> p t d", p=P)).then_inc(event("ctx_in"), 16)
                if c == RING - 1:
                    sp.wait_ge(event("x_ready"), (DEPTH + 1) * TT)
                    sp.dma_start(kk[:], k2[:, 0:N_K2]).then_inc(event("kk_in"), 16)
            sp.wait_ge(event("x2_ready"), NT)
            sp.dma_start(fing, k2[:, N_K2:N_K2 + D]).then_inc(event("fing_in"), 16)
            for t in range(TT):
                sp.wait_ge(event("out_ready"), t + 1)
                sp.dma_start(out[0, t * P:(t + 1) * P, :], Y2[:, t, :]).then_inc(stored, 16)
            sp.wait_ge(stored, 16 * TT)

        def arrived(eng, chunks, c, base, rep=0):
            eng.wait_ge(slot_full[(base + c) % RING], rep * (16 * len(chunks) // RING) + 16 * ((base + c) // RING + 1))

        @block.tensor
        def _(pe):
            def begin(u, name, rep=0):
                b, n = u.count(name, rep)
                pe.wait_ge(bank_free[b], n + 1)
                return bank[b]

            def done(u, name, ins):
                ins.then_inc(bank_full[u.at[name][0]], 1)

            def ada(u, name, sums, vectors, count, rep=0):
                pe.wait_ge(event("ada_sum"), count)
                ps = begin(u, name, rep)
                for j in range(4):
                    for v in range(vectors):
                        at = 64 * (vectors * j + v)
                        mm = pe.matmul(ps[:, at:at + 64], sums[:, v, j * P:(j + 1) * P], ones[:, 0:64],
                                       start=True, stop=True)
                done(u, name, mm)

            def turn_blocks(ps, blocks):
                for i, blk in enumerate(blocks):
                    n = blk.shape[1]
                    mm = pe.transpose(ps[0:n, i * P:(i + 1) * P], blk, ident[:])
                return mm

            def project(u, name, slot, t, width, rep, stride=None, w0=0):
                stride = stride or width
                ps = begin(u, name, rep)
                for k in range(KD):
                    mm = pe.matmul(ps[:, 0:width], hT[:, k, t * P:(t + 1) * P],
                                   ring[:, slot, k * stride + w0:k * stride + w0 + width],
                                   start=(k == 0), stop=(k == KD - 1))
                done(u, name, mm)

            def project_split(name, l, part=None):
                for q, (n, i, width) in enumerate(PIECES1):
                    if n != name or (part is not None and part != i // (KD // 2)):
                        continue
                    if i == 0:
                        for t in range(TT):
                            begin(lay1, f"{name}{t}", l)
                    pe.wait_ge(event("lo1_ready"), l * len(PIECES1) + (q + 1))
                    rows = PIECE // width
                    for t in range(TT):
                        o = bank[lay1.at[f"{name}{t}"][0]]
                        for j in range(rows):
                            k = i * rows + j
                            hi, low = xhi1[:, k, t * P:(t + 1) * P], xlo1[:, k, t * P:(t + 1) * P]
                            at = slice(j * width, (j + 1) * width)
                            for m, (a, b) in enumerate(((hi, whi1), (hi, wlo1), (low, whi1))):
                                mm = pe.matmul(o[:, 0:width], a, b[:, q % BUFFERS, at], start=(k == 0 and m == 0),
                                               stop=(k == KD - 1 and m == 2))
                        if q + 1 in ENDS1:
                            done(lay1, f"{name}{t}", mm)
                    if q + 1 not in ENDS1:
                        mm.then_inc(event("piece1_used"), 1)

            for m in range(SHIFTS):
                ada(pro, f"ada{m}", msum[:, m % 2], 1, m + 1)

            with pe.Fori(0, DEPTH) as l:
                u = lay1
                chunk = {n: c for c, (n, _) in enumerate(CH1)}

                def landed(name):
                    arrived(pe, CH1, chunk[name], len(CH0), l)
                    return (len(CH0) + chunk[name]) % RING

                for t in range(TT):
                    pe.wait_ge(event("xn_ready"), l * TT + (t + 1))
                    for h in range(2):
                        ps = begin(u, f"xT{t}{h}", l)
                        done(u, f"xT{t}{h}", turn_blocks(ps, [Y[:, t, (4 * h + i) * P:(4 * h + i + 1) * P] for i in range(4)]))

                slot = landed("idx")
                for t in range(TT):
                    for h in range(2):
                        emptied(pe, u, f"xT{t}{h}", l)
                    project(u, f"idx{t}", slot, t, 324, l, stride=340)
                ps = begin(u, "aT", l)
                for k in range(KD):
                    mm = pe.matmul(ps[0:RANK, 0:S], ring[:, slot, k * 340 + 324:k * 340 + 340], hT[:, k, :],
                                   start=(k == 0), stop=(k == KD - 1))
                done(u, "aT", mm)
                project_split("dsa_q", l)

                pe.wait_ge(event("idx_rot"), l + 1)
                ps = begin(u, "qiT", l)
                done(u, "qiT", turn_blocks(ps, [idx[:, t, j * P:(j + 1) * P] for j in range(2) for t in range(TT)]))
                ps = begin(u, "kiT", l)
                done(u, "kiT", turn_blocks(ps, [kdi[:, t, :, :].rearrange("p a b -> p (a b)") for t in range(TT)]))

                slot = landed("gla_qk")
                for i, name in enumerate(("gq", "gk")):
                    ps = begin(u, name, l)
                    for f in range(2):
                        for k in range(KD):
                            at = k * 512 + (2 * i + f) * P
                            mm = pe.matmul(ps[:, f * S:(f + 1) * S], ring[:, slot, at:at + P], hT[:, k, :],
                                           start=(k == 0), stop=(k == KD - 1))
                    done(u, name, mm)

                emptied(pe, u, "qiT", l)
                emptied(pe, u, "kiT", l)
                for t in range(TT):
                    for r in range(2):
                        ps = begin(u, f"s{t}{r}", l)
                        n = P * (t + 1)
                        for j in range(2):
                            mm = pe.matmul(ps[:, j * n:(j + 1) * n], qiT[64 * r:64 * r + 64, j, t * P:(t + 1) * P],
                                           kiT[64 * r:64 * r + 64, 0:n], start=True, stop=True)
                        done(u, f"s{t}{r}", mm)
                emptied(pe, u, "aT", l)
                pe.wait_ge(event("wl_ready"), l + 1)
                ps = begin(u, "z", l)
                for f in range(2):
                    mm = pe.matmul(ps[:, f * S:(f + 1) * S], wl[:, f * P:(f + 1) * P], aT[:, :], start=True, stop=True)
                done(u, "z", mm)

                project_split("dsa_kv", l)
                project_split("ret_qk", l)
                pe.wait_ge(event("dsa_rot"), l + 1)
                for i in range(2):
                    ps = begin(u, f"dqT{i}", l)
                    done(u, f"dqT{i}", turn_blocks(ps, [dsaqkv[:, t, (2 * i + j) * P:(2 * i + j + 1) * P]
                                                        for j in range(2) for t in range(TT)]))
                ps = begin(u, "dkT", l)
                done(u, "dkT", turn_blocks(ps, [kdd[:, t, j, :, :].rearrange("p a b -> p (a b)")
                                                for j in range(2) for t in range(TT)]))
                project_split("ret_v", l)
                project_split("gla_v", l)
                pe.wait_ge(event("ret_rot"), l + 1)
                for name, at in (("rqT", 0), ("rkT", 256)):
                    ps = begin(u, name, l)
                    done(u, name, turn_blocks(ps, [retqkv[:, t, at + j * P:at + (j + 1) * P]
                                                   for j in range(2) for t in range(TT)]))

                def ret_scores(h):
                    if h == 0:
                        emptied(pe, u, "rqT", l)
                        emptied(pe, u, "rkT", l)
                    r, j = h % 2, h // 2
                    ps = begin(u, f"rs{h}", l)
                    pe.matmul(ps[:, 0:S], krT[64 * r:64 * r + 64, j, 0:P], qrT[64 * r:64 * r + 64, j, 0:S],
                              start=True, stop=True)
                    done(u, f"rs{h}", pe.matmul(ps[:, S:S + P], krT[64 * r:64 * r + 64, j, P:S],
                                                qrT[64 * r:64 * r + 64, j, P:S], start=True, stop=True))

                def ret_values(h):
                    emptied(pe, u, f"rs{h}", l)
                    if h == 0:
                        begin(u, "ro0", l)
                        begin(u, "ro1", l)
                    v = [retqkv[:, t, 512 + h * P:512 + (h + 1) * P] for t in range(TT)]
                    o = [bank[u.at[f"ro{t}"][0]][:, h * P:(h + 1) * P] for t in range(TT)]
                    m0 = pe.matmul(o[0], RS[:, h % 2, 0:P], v[0], start=True, stop=True)
                    pe.matmul(o[1], RS[:, h % 2, P:2 * P], v[0], start=True, stop=False)
                    m1 = pe.matmul(o[1], RS[:, h % 2, 2 * P:3 * P], v[1], start=False, stop=True)
                    if h == 3:
                        done(u, "ro0", m0)
                        done(u, "ro1", m1)

                def gla_scores(i):
                    if i:
                        pe.wait_ge(event("gql"), l * 8 + i)
                        pe.wait_ge(event("gkl"), l * 8 + i)
                    else:
                        emptied(pe, u, "gq", l)
                        emptied(pe, u, "gk", l)
                    q, k = (QL[i % 2], KL[:, i % 2]) if i else (gqT, gkT)
                    pairs = [(1, 0)] if LEVELS[i] == "cross" else [(t, t) for t in range(TT)]
                    for r in range(2):
                        ps = begin(u, f"g{i}_{r}", l)
                        n = 0
                        for tq, tk in pairs:
                            for j in range(2):
                                mm = pe.matmul(ps[:, n:n + P], k[64 * r:64 * r + 64, j, tk * P:(tk + 1) * P],
                                               q[64 * r:64 * r + 64, j, tq * P:(tq + 1) * P], start=True, stop=True)
                                n += P
                        done(u, f"g{i}_{r}", mm)

                def gla_values():
                    pe.wait_ge(event("at_ready"), l + 1)
                    ps0, ps1 = begin(u, "go0", l), begin(u, "go1", l)
                    for h in range(4):
                        r, j = h % 2, h // 2
                        v = [glav[:, t, h * P:(h + 1) * P] for t in range(TT)]
                        c = slice(h * P, (h + 1) * P)
                        m0 = pe.matmul(ps0[:, c], AT[:, r, 0, j, :], v[0], start=True, stop=True)
                        if h == 3:
                            done(u, "go0", m0)
                        pe.matmul(ps1[:, c], AT[:, r, 2, j, :], v[0], start=True, stop=False)
                        m1 = pe.matmul(ps1[:, c], AT[:, r, 1, j, :], v[1], start=False, stop=True)
                    done(u, "go1", m1)

                def dsa_logits(i):
                    if i == 0:
                        for name in ("dqT0", "dqT1", "dkT"):
                            emptied(pe, u, name, l)
                    t, heads = DSA_UNITS[i]
                    ps = begin(u, f"dl{i}", l)
                    n = P * (t + 1)
                    for a, h in enumerate(heads):
                        r = 64 * (h % 2)
                        mm = pe.matmul(ps[:, a * n:(a + 1) * n], qdT[r:r + 64, h // 2, t * P:(t + 1) * P],
                                       kdT[r:r + 64, h // 4, 0:n], start=True, stop=True)
                    done(u, f"dl{i}", mm)

                def dsa_turn(i):
                    pe.wait_ge(event("dexp"), l * 6 + (i + 1))
                    ps = begin(u, f"dp{i}", l)
                    done(u, f"dp{i}", turn_blocks(ps, [L[:, i % 2, b * P:(b + 1) * P] for b in range(4)]))

                def dsa_values(i):
                    emptied(pe, u, f"dp{i}", l)
                    t, heads = DSA_UNITS[i]
                    if i in (0, 2):
                        begin(u, f"do{t}", l)
                    o = bank[u.at[f"do{t}"][0]]
                    for a, h in enumerate(heads):
                        for b in range(t + 1):
                            at = (a * (t + 1) + b) * P
                            mm = pe.matmul(o[:, h * 64:(h + 1) * 64], PT[:, i % 2, at:at + P],
                                           dsaqkv[:, b, 640 + (h // 4) * 64:704 + (h // 4) * 64],
                                           start=(b == 0), stop=(b == t))
                    if i in (1, 5):
                        done(u, f"do{t}", mm)

                def turn_branch(name, src, ready):
                    for t in range(TT):
                        pe.wait_ge(event(ready), l * TT + (t + 1))
                        ps = begin(u, f"{name}{t}", l)
                        done(u, f"{name}{t}", turn_blocks(ps, [src[:, t, j * P:(j + 1) * P] for j in range(4)]))

                def gap(g):
                    if g < 4:
                        ret_scores(g)
                    if 1 <= g <= 4:
                        ret_values(g - 1)
                    if 5 <= g <= 10:
                        dsa_logits(g - 5)
                    if 6 <= g <= 11:
                        dsa_turn(g - 6)
                    if 7 <= g <= 12:
                        dsa_values(g - 7)
                    if g < len(LEVELS):
                        gla_scores(g)
                    if g == 9:
                        gla_values()
                    if g == 11:
                        turn_branch("retT", retg, "ret_ready")
                    if g == 12:
                        turn_branch("glaT", glag, "gla_ready")
                    if g == 13:
                        turn_branch("dsaT", dsag, "dsa_ready")

                g = 0
                for name in ("ret_g", "dsa_g", "gla_g") + tuple(f"merge{m}" for m in range(MERGES)):
                    slot = None if name in SPLIT1 else landed(name)
                    for t in range(TT):
                        if name in SPLIT1:
                            project_split(name, l, t)
                        else:
                            project(u, f"{name}{t}", slot, t, 512, l)
                        gap(g)
                        g += 1
                    if name.startswith("merge") and name != "merge0":
                        m = int(name[5]) - 1
                        ada(u, f"ada{m}", msum[:, m % 2], 2 if m < SHIFTS else 1, l * MERGES + (SHIFTS + m + 1), l)

                for b, name in enumerate(("retT", "dsaT", "glaT")):
                    slot = landed(f"br{b}")
                    for t in range(TT):
                        emptied(pe, u, f"{name}{t}", l)
                        for h in range(2):
                            ps = begin(u, f"br{b}{t}{h}", l)
                            for k in range(4):
                                mm = pe.matmul(ps[:, :], branchT[b][:, k, t * P:(t + 1) * P],
                                               ring[:, slot, k * D + h * 512:k * D + h * 512 + 512],
                                               start=(k == 0), stop=(k == 3))
                            done(u, f"br{b}{t}{h}", mm)
                    if b == 0:
                        m = MERGES - 1
                        ada(u, f"ada{m}", msum[:, m % 2], 2 if m < SHIFTS else 1, l * MERGES + (SHIFTS + m + 1), l)
                for t in range(TT):
                    pe.wait_ge(event("y_ready"), l * TT + (t + 1))
                    for h in range(2):
                        ps = begin(u, f"yT{t}{h}", l)
                        done(u, f"yT{t}{h}", turn_blocks(ps, [Y[:, t, (4 * h + i) * P:(4 * h + i + 1) * P] for i in range(4)]))
                slots = [landed("out0"), landed("out1")]
                for t in range(TT):
                    for h in range(2):
                        emptied(pe, u, f"yT{t}{h}", l)
                    for h in range(2):
                        project(u, f"out{t}{h}", slots[h], t, 512, l)
                    if t == 0:
                        pe.wait_ge(event("diag_ready"), l + 1)
                        for h in range(2):
                            ps = begin(u, f"gb{h}", l)
                            done(u, f"gb{h}", pe.matmul(ps[:, :], ones[:], DG[:, 4 * h:4 * h + 4, :], start=True, stop=True))

            def landed2(name):
                c = chunk2(name)
                arrived(pe, CH2, c, BASE2)
                return (BASE2 + c) % RING

            def project2(u, name, slot, t, width):
                ps = begin(u, name)
                for k in range(KD):
                    mm = pe.matmul(ps[:, 0:width], hT2[:, k, t * P:(t + 1) * P],
                                   ring[:, slot, k * width:(k + 1) * width], start=(k == 0), stop=(k == KD - 1))
                done(u, name, mm)

            def turn_x2(u, first, order):
                for i, t in enumerate(order):
                    pe.wait_ge(event("h2_ready"), first + i + 1)
                    for h in range(2):
                        ps = begin(u, f"xT{t}{h}")
                        done(u, f"xT{t}{h}", turn_blocks(ps, [Y2[:, t, (4 * h + i) * P:(4 * h + i + 1) * P] for i in range(4)]))

            def turned_x2(u, t):
                for h in range(2):
                    emptied(pe, u, f"xT{t}{h}")

            def gate_rows(u, v, diag, count):
                pe.wait_ge(event("diag_ready"), count)
                for h in range(2):
                    ps = begin(u, f"gb{v}{h}")
                    done(u, f"gb{v}{h}", pe.matmul(ps[:, :], ones[:], diag[:, 4 * h:4 * h + 4, :], start=True, stop=True))

            u = le
            turn_x2(u, 0, E_ORDER)
            slot = landed2("e_kv")
            for t in E_ORDER:
                turned_x2(u, t)
                project2(u, f"e_kv{t}", slot, t, 256)
            pe.wait_ge(event("xlo_ready"), NT)
            for q in range(len(E_SPLIT) * SPLIT_PIECES):
                name, i = E_SPLIT[q // SPLIT_PIECES], q % SPLIT_PIECES
                pe.wait_ge(event("lo_ready"), q + 1)
                for t in range(NT):
                    if i == 0:
                        begin(u, f"{name}{t}")
                    o = bank[u.at[f"{name}{t}"][0]]
                    for k in range(2 * i, 2 * i + 2):
                        at = slice((k % 2) * 512, (k % 2) * 512 + 512)
                        hi, lo_ = xhi[:, k, t * P:(t + 1) * P], xlo[:, k, t * P:(t + 1) * P]
                        for n, (a, b) in enumerate(((hi, whi), (hi, wlo), (lo_, whi))):
                            mm = pe.matmul(o[:, :], a, b[:, q % 2, at], start=(k == 0 and n == 0), stop=(k == KD - 1 and n == 2))
                    if i == SPLIT_PIECES - 1:
                        done(u, f"{name}{t}", mm)
                if i < SPLIT_PIECES - 1:
                    mm.then_inc(event("piece_used"), 1)
            pe.wait_ge(event("e_rot"), 1)
            for t in range(NT):
                emptied(pe, u, f"e_q{t}")
                emptied(pe, u, f"e_kv{t}")
            for j in range(2):
                ps = begin(u, f"ekT{j}")
                done(u, f"ekT{j}", turn_blocks(ps, [ekd[:, t, j].rearrange("p a b -> p (a b)") for t in range(NT)]))
            for j in range(4):
                ps = begin(u, f"eqT{j}")
                done(u, f"eqT{j}", turn_blocks(ps, [eqk[:, t, j * P:(j + 1) * P] for t in range(NT)]))

            def e_logits(i):
                t, heads = E_UNITS[i]
                k0 = 0 if t < TT else TT * P
                n = NT * P - k0
                ps = begin(u, f"el{i}")
                for a, h in enumerate(heads):
                    r = 64 * (h % 2)
                    mm = pe.matmul(ps[:, a * n:(a + 1) * n], eqT[r:r + 64, h // 2, t * P:(t + 1) * P],
                                   ekT[r:r + 64, h // 4, k0:k0 + n], start=True, stop=True)
                done(u, f"el{i}", mm)

            def e_turn(i):
                if E_UNITS[i][0] < TT:
                    pe.wait_ge(event("e_exp"), i + 1)
                else:
                    emptied(pe, u, f"el{i}")
                ps = begin(u, f"ep{i}")
                done(u, f"ep{i}", turn_blocks(ps, [L2[:, i % 4, b * P:(b + 1) * P] for b in range(4)]))

            def e_values(i):
                emptied(pe, u, f"ep{i}")
                t, heads = E_UNITS[i]
                b0 = 0 if t < TT else TT
                nb = NT - b0
                if i == 0 or E_UNITS[i - 1][0] != t:
                    begin(u, f"eo{t}")
                o = bank[u.at[f"eo{t}"][0]]
                for a, h in enumerate(heads):
                    for b in range(nb):
                        mm = pe.matmul(o[:, h * 64:(h + 1) * 64], PT2[:, i % 4, (a * nb + b) * P:(a * nb + b + 1) * P],
                                       ev[:, b0 + b, (h // 4) * 64:(h // 4) * 64 + 64], start=(b == 0), stop=(b == nb - 1))
                if i == E_LAST[t]:
                    done(u, f"eo{t}", mm)

            for j in range(2):
                emptied(pe, u, f"ekT{j}")
            for j in range(4):
                emptied(pe, u, f"eqT{j}")
            for g in range(14):
                if g < 8:
                    name = f"e_g{g // 4}"
                    slot = landed2(name)
                    project2(u, f"{name}{g % 4}", slot, g % 4, 512)
                if g in E_ADA:
                    n = sum_number(chunk2(E_ADA[g]))
                    ada(u, E_ADA[g], msum2[n % 2], 2, n)
                if g in (9, 11):
                    gate_rows(u, (g - 9) // 2, DG2, DEPTH + (g - 9) // 2 + 1)
                if g < 12:
                    e_logits(2 * g)
                    e_logits(2 * g + 1)
                if 1 <= g < 13:
                    e_turn(2 * g - 2)
                    e_turn(2 * g - 1)
                if g >= 2:
                    e_values(2 * g - 4)
                    e_values(2 * g - 3)
                if g == 7:
                    slot = landed2("e_ws")
                    pe.wait_ge(event("ln_ready"), NT)
                    for j in range(4):
                        ps = begin(u, f"gs{j}")
                        for a in range(2):
                            q = 2 * j + a
                            mm = pe.matmul(ps[:, a * 256:(a + 1) * 256].rearrange("p (t c) -> p t c", t=NT),
                                           ring[:, slot, q * P:(q + 1) * P], evv[:, :, q * 64:(q + 1) * 64],
                                           start=True, stop=True)
                        done(u, f"gs{j}", mm)
            for t in range(NT):
                pe.wait_ge(event("em_ready"), t + 1)
                for h in range(2):
                    ps = begin(u, f"eyT{t}{h}")
                    done(u, f"eyT{t}{h}", turn_blocks(ps, [eg[:, t, (4 * h + i) * P:(4 * h + i + 1) * P] for i in range(4)]))
            slots = [landed2("e_o0"), landed2("e_o1")]
            for h in range(2):
                for t in range(NT):
                    if h == 0:
                        emptied(pe, u, f"eyT{t}0")
                        emptied(pe, u, f"eyT{t}1")
                    if (h, t) == (1, NT - 1):
                        ada(u, "ada3", msum2[sum_number(chunk2("ada3")) % 2], 2, sum_number(chunk2("ada3")))
                    project2(u, f"eout{t}{h}", slots[h], t, 512)
                if h == 0:
                    ada(u, "ada2", msum2[sum_number(chunk2("ada2")) % 2], 2, sum_number(chunk2("ada2")))

            u = lo
            turn_x2(u, NT, O_ORDER)
            slot = landed2("o_kv")
            for t in range(NT):
                turned_x2(u, t)
                project2(u, f"o_kv{t}", slot, t, 160)
            slot = landed2("o_q")
            for t in range(TT):
                project2(u, f"o_q{t}", slot, t, 256)
            ada(u, "adah4", msum3[0], 1, sum_number(chunk2("adah4")))
            slot = landed2("o_g0")
            for t in range(TT):
                project2(u, f"o_g0{t}", slot, t, 512)
            pe.wait_ge(event("okv_ready"), 1)
            ps = begin(u, "kvT")
            done(u, "kvT", turn_blocks(ps, [okv[:, t, 0:P] for t in range(NT)]))
            pe.wait_ge(event("okp_ready"), 1)
            ps = begin(u, "kpT")
            done(u, "kpT", turn_blocks(ps, [okp[:, t, :] for t in range(NT)]))
            emptied(pe, u, "kvT")
            slot = landed2("o_kvb")
            for h in range(MLA_HEADS):
                ps = begin(u, f"on{h}")
                done(u, f"on{h}", pe.matmul(ps[0:MLA_NOPE, :], ring[:, slot, h * MLA_NOPE:(h + 1) * MLA_NOPE],
                                            kvT[:, :], start=True, stop=True))
            for t in range(NT):
                for h in range(2):
                    ps = begin(u, f"ov{t}{h}")
                    done(u, f"ov{t}{h}", pe.matmul(ps[:, :], kvT[:, t * P:(t + 1) * P],
                                                   ring[:, slot, D + h * 512:D + h * 512 + 512], start=True, stop=True))
            pe.wait_ge(event("oqa_ready"), 1)
            ps = begin(u, "qaT")
            done(u, "qaT", turn_blocks(ps, [oqa[:, t, k * P:(k + 1) * P] for k in range(2) for t in range(TT)]))
            emptied(pe, u, "qaT")
            slot = landed2("o_qb")
            for t in range(TT):
                for c in range(3):
                    ps = begin(u, f"oqb{t}{c}")
                    for k in range(2):
                        mm = pe.matmul(ps[:, :], qaT[:, k, t * P:(t + 1) * P],
                                       ring[:, slot, k * 1536 + c * 512:k * 1536 + c * 512 + 512],
                                       start=(k == 0), stop=(k == 1))
                    done(u, f"oqb{t}{c}", mm)
            slot = landed2("o_g1")
            for t in range(TT):
                project2(u, f"o_g1{t}", slot, t, 512)
            pe.wait_ge(event("oq_rot"), 1)
            for j in range(8):
                ps = begin(u, f"oqT{j}")
                done(u, f"oqT{j}", turn_blocks(ps, [q2[:, t, h * MLA_QK:(h + 1) * MLA_QK] for h in (2 * j, 2 * j + 1)
                                                    for t in range(TT)]))
            ada(u, "adah5", msum3[1], 1, sum_number(chunk2("adah5")))
            for j in range(8):
                emptied(pe, u, f"oqT{j}")
            for h in range(MLA_HEADS):
                emptied(pe, u, f"on{h}")
            for t in range(NT):
                for h in range(2):
                    emptied(pe, u, f"ov{t}{h}")
            pe.wait_ge(event("okT_ready"), 1)
            for p in range(16 + 2):
                if p < 16:
                    for i in (2 * p, 2 * p + 1):
                        t, h = O_UNITS[i]
                        ps = begin(u, f"ml{i}")
                        done(u, f"ml{i}", pe.matmul(ps[:, :], oqT[:, h, t * P:(t + 1) * P], okT[:, h, :], start=True, stop=True))
                if p == 0:
                    gate_rows(u, 0, DG3, DEPTH + 3)
                if 1 <= p < 17:
                    for i in (2 * p - 2, 2 * p - 1):
                        emptied(pe, u, f"ml{i}")
                        ps = begin(u, f"mp{i}")
                        done(u, f"mp{i}", turn_blocks(ps, [L2[:, i % 4, b * P:(b + 1) * P] for b in range(4)]))
                if p >= 2:
                    for i in (2 * p - 4, 2 * p - 3):
                        t, h = O_UNITS[i]
                        emptied(pe, u, f"mp{i}")
                        if i % 8 == 0:
                            begin(u, f"mo{i // 8}")
                        o = bank[u.at[f"mo{i // 8}"][0]]
                        for b in range(NT):
                            mm = pe.matmul(o[:, (h % 8) * 64:(h % 8) * 64 + 64], PT2[:, i % 4, b * P:(b + 1) * P],
                                           ova[:, b, h * 64:(h + 1) * 64], start=(b == 0), stop=(b == NT - 1))
                        if i % 8 == 7:
                            done(u, f"mo{i // 8}", mm)
            for t in range(TT):
                pe.wait_ge(event("om_ready"), t + 1)
                for h in range(2):
                    ps = begin(u, f"oyT{t}{h}")
                    done(u, f"oyT{t}{h}", turn_blocks(ps, [og[:, t, (4 * h + i) * P:(4 * h + i + 1) * P] for i in range(4)]))
            slots = [landed2("o_o0"), landed2("o_o1")]
            for t in range(TT):
                for h in range(2):
                    emptied(pe, u, f"oyT{t}{h}")
                for h in range(2):
                    project2(u, f"oout{t}{h}", slots[h], t, 512)

        @block.scalar
        def _(act):
            steps = [0]
            base = [0]

            def step(ins):
                steps[0] += 1
                ins.then_inc(event("act_step"), 1)

            def settle():
                act.wait_ge(event("act_step"), base[0] + steps[0])

            act.dma_start(col[:], cols).then_inc(event("col_in"), 16)
            act.wait_ge(event("col_in"), 16)
            act.activation(cact[:].rearrange("p k v -> p (k v)"), col[:, C_CT:C_CT + 24], ACT.Silu).then_inc(event("c_ready"), 1)
            act.wait_ge(slot_full[0], 16)
            act.dma_start(posi[:], pos).then_inc(event("pos_in"), 16)
            act.dma_start(freq, k1[:, K_FREQ:K_FREQ + 40]).then_inc(event("pos_in"), 16)
            act.dma_start(ident[:], ident_in).then_inc(event("x_in"), 16)
            act.dma_start(X[:, 0:TT, :], x.rearrange("(t p) d -> p t d", p=P)).then_inc(event("x_in"), 16)
            act.wait_ge(event("sin_in"), 2)
            act.activation(sinT[:], sinT[:], ACT.Sin).then_inc(event("sin_out"), 1)
            act.activation(cosT[:], cosT[:], ACT.Sin).then_inc(event("sin_out"), 1)
            act.wait_ge(slot_full[SHIFTS - 1 - RING], 32)
            act.dma_start(kc[:, 0:K_FREQ], k1[:, 0:K_FREQ]).then_inc(loaded, 16)
            act.dma_start(wl_all[:], wlr).then_inc(loaded, 16)
            act.dma_start(gmf, gmask).then_inc(loaded, 16)

            def copy_out(u, name, dst, rep, func=ACT.Copy, scale=1.0):
                ps = filled(act, u, name, rep)
                n = int(np.prod(dst.shape[1:]))
                act.activation(dst, shape_like(ps[0:dst.shape[0], 0:n], dst), func, scale=scale).then_inc(free(u, name), 1)

            with act.Fori(0, DEPTH) as l:
                u = lay1
                base[0], steps[0] = l * ACT_STEPS, 0
                for t in range(TT):
                    act.wait_ge(event("x_ready"), l * TT + (t + 1))
                    act.activation(Y[:, t, :], X[:, t, :], ACT.Square, accum_out=st[:, t:t + 1]).then_inc(event("x_ssq"), 1)
                    act.wait_ge(event("x_var"), l * TT + (t + 1))
                    act.activation(st[:, 4 + t:5 + t], st[:, 2 + t:3 + t], ACT.Sqrt).then_inc(event("x_std"), 1)
                act.wait_ge(event("hmod_ready"), l + 1)
                for t in range(TT):
                    ps = filled(act, u, f"xT{t}0", l)
                    for k in range(4):
                        ins = act.activation(hT[:, k, t * P:(t + 1) * P], ps[:, k * P:(k + 1) * P], ACT.Identity,
                                             bias=hsh[:, k:k + 1], scale=hsc[:, k:k + 1])
                        if k < 3:
                            step(ins)
                    ins.then_inc(free(u, f"xT{t}0"), 1)

                def high(first, last):
                    for q in range(first, last):
                        c, i, w = piece1(q)
                        if i == 0:
                            arrived(act, CH1, c, len(CH0), l)
                        if q >= BUFFERS:
                            piece1_used(act, q - BUFFERS, l)
                        act.activation(whi1[:, q % BUFFERS, :], w, ACT.Copy).then_inc(event("hi1_ready"), 1)

                for t in range(TT):
                    emptied(act, u, f"xT{t}0", l)
                    emptied(act, u, f"xT{t}1", l)
                    c = slice(t * P, (t + 1) * P)
                    act.activation(xhi1[:, :, c], hT[:, :, c], ACT.Copy).then_inc(event("xhi1_ready"), 1)
                high(0, 4)
                for t in range(TT):
                    copy_out(u, f"idx{t}", idx[:, t, :], l)
                copy_out(u, "aT", aT[:, :], l)
                high(4, 12)
                for t in range(TT):
                    copy_out(u, f"dsa_q{t}", dsaqkv[:, t, 0:512], l)
                copy_out(u, "qiT", qiT[:], l)
                copy_out(u, "kiT", kiT[:], l)
                copy_out(u, "gq", gqT[:], l, scale=0.125)
                copy_out(u, "gk", gkT[:], l)
                act.wait_ge(event("gm_ready"), 1)
                for t in range(TT):
                    for r in range(2):
                        ps = filled(act, u, f"s{t}{r}", l)
                        n = P * (t + 1)
                        at = (0, 2 * P)[r] if t == 0 else 512 + 512 * r
                        act.activation(RI[:, at:at + 2 * n], ps[:, 0:2 * n], ACT.Relu, scale=1.0 / 16).then_inc(free(u, f"s{t}{r}"), 1)
                high(12, 16)
                for t in range(TT):
                    copy_out(u, f"dsa_kv{t}", dsaqkv[:, t, 512:768], l)
                high(16, 20)
                act.wait_ge(event("z_ready"), l + 1)
                step(act.activation(AZ[:], AZ[:], ACT.Exp, scale=-1.0))
                settle()
                act.activation(LG[:], AZ[:], ACT.Ln, bias=1.0).then_inc(event("lg_ready"), 1)
                high(20, 24)
                for t in range(TT):
                    copy_out(u, f"ret_qk{t}", retqkv[:, t, 0:512], l)
                copy_out(u, "dqT0", qdT[:, 0:2, :], l)
                copy_out(u, "dqT1", qdT[:, 2:4, :], l)
                copy_out(u, "dkT", kdT[:], l)
                high(24, 32)
                for t in range(TT):
                    copy_out(u, f"ret_v{t}", retqkv[:, t, 512:1024], l)
                high(32, 36)
                for t in range(TT):
                    copy_out(u, f"gla_v{t}", glav[:, t, :], l)
                high(36, 40)
                copy_out(u, "rqT", qrT[:], l)
                copy_out(u, "rkT", krT[:], l)

                def gla_exp(i):
                    if i < len(LEVELS):
                        act.wait_ge(event("gsub"), l * 8 + i)
                        act.activation(E[i % 2], E[i % 2], ACT.Exp, scale=1.0 / 16).then_inc(event("gexp"), 1)

                gla_exp(1)

                def dsa_exp(i):
                    t, heads = DSA_UNITS[i]
                    act.wait_ge(event("dmax"), l * 6 + (i + 1))
                    n = P * (t + 1)
                    for a, h in enumerate(heads):
                        ins = act.activation(L[:, i % 2, a * n:(a + 1) * n], L[:, i % 2, a * n:(a + 1) * n], ACT.Exp,
                                             bias=mx[:, t, a + PARTS[i]:a + PARTS[i] + 1], accum_out=sm[:, t, h:h + 1])
                        if a < len(heads) - 1:
                            step(ins)
                    ins.then_inc(event("dexp"), 1)

                def head_sums(kind, o, at):
                    for t in range(TT):
                        ps = filled(act, u, f"{o}{t}", l)
                        for h in range(4):
                            settle()
                            ins = act.activation(junk[:], ps[:, h * P:(h + 1) * P], ACT.Square,
                                                 accum_out=st[:, at + 4 * t + h:at + 4 * t + h + 1])
                            if t < TT - 1 or h < 3:
                                step(ins)
                    ins.then_inc(event(kind + "_ssq"), 1)

                def head_roots(kind, at):
                    act.wait_ge(event(kind + "_var"), l + 1)
                    act.activation(st[:, at + 16:at + 24], st[:, at + 8:at + 16], ACT.Sqrt).then_inc(event(kind + "_std"), 1)

                def branch_out(name, dst):
                    for t in range(TT):
                        copy_out(u, f"{name}{t}", dst[:, :, t * P:(t + 1) * P], l)

                g = 0
                for name in ("ret_g", "dsa_g", "gla_g") + tuple(f"merge{m}" for m in range(MERGES)):
                    for t in range(TT):
                        if name[0] == "m":
                            m = int(name[5])
                            if g == 6:
                                act.wait_ge(event("sel_ready"), l * TT + TT)
                            dst = G[:, t, m * 512:(m + 1) * 512]
                            copy_out(u, f"{name}{t}", dst, l, func=ACT.Copy if g < 13 else ACT.Sigmoid)
                        else:
                            dst = {"ret_g": retg, "dsa_g": dsag, "gla_g": glag}[name]
                            high(40 + 4 * g, min(44 + 4 * g, len(PIECES1)))
                            if t == TT - 1:
                                copy_out(u, f"{name}0", dst[:, 0, :], l)
                                copy_out(u, f"{name}1", dst[:, 1, :], l)
                        gla_exp(g + 2)
                        if 6 <= g <= 11:
                            copy_out(u, f"dp{g - 6}", PT[:, g % 2, :], l)
                        if 5 <= g <= 10:
                            dsa_exp(g - 5)
                        if g == 5:
                            head_sums("r", "ro", 8)
                            head_roots("r", 8)
                            for dst in (retg, dsag, glag):
                                emptied(act, u, "gla_g1", l)
                                act.activation(dst[:], dst[:], ACT.Silu).then_inc(event("silu_ready"), 1)
                        if g == 9:
                            head_sums("g", "go", 40)
                        if g == 10:
                            head_roots("g", 40)
                        if g == 11:
                            branch_out("retT", retT)
                        if g == 12:
                            branch_out("glaT", glaT)
                            emptied(act, u, "merge30", l)
                            act.activation(G[:, 0, 0:2048], G[:, 0, 0:2048], ACT.Sigmoid).then_inc(event("g_sig"), 1)
                            act.activation(G[:, 1, 0:1536], G[:, 1, 0:1536], ACT.Sigmoid).then_inc(event("g_sig"), 1)
                        if g == 13:
                            branch_out("dsaT", dsaT)
                        g += 1
                for t in range(TT):
                    copy_out(u, f"yT{t}0", hT[:, 0:4, t * P:(t + 1) * P], l)
                for t in range(TT):
                    for h in range(2):
                        ps = filled(act, u, f"out{t}{h}", l)
                        settle()
                        step(act.activation(L[:, 0, :], ps[:, :], ACT.Square, accum_out=st[:, 72 + 2 * t + h:73 + 2 * t + h]))
                        act.activation(Y[:, t, h * 512:(h + 1) * 512], ps[:, :], ACT.Copy).then_inc(free(u, f"out{t}{h}"), 1)
                    act.wait_ge(event("o_var"), l * TT + (t + 1))
                    act.activation(st[:, 78 + t:79 + t], st[:, 76 + t:77 + t], ACT.Sqrt).then_inc(event("o_std"), 1)
                    if t == 0:
                        for h in range(2):
                            copy_out(u, f"gb{h}", gpb[:, h * 512:(h + 1) * 512], l)
                counted("ACT_STEPS", steps[0], ACT_STEPS)

            base[0], steps[0] = DEPTH * ACT_STEPS, 0

            def copy_rows(u, name, dst, ps, func=ACT.Copy, **more):
                act.activation(dst, ps, func, **more).then_inc(free(u, name), 1)

            def norm_x2(u, first, order, signal, counts):
                for i, t in enumerate(order):
                    if counts[t] > 0:
                        act.wait_ge(event(signal), counts[t])
                    act.activation(Y2[:, t, :], X[:, t, :], ACT.Square, accum_out=st2[:, i:i + 1]).then_inc(event("h2_ssq"), 1)
                    if i >= NT - 2:
                        part = 0 if i == NT - 2 else 1
                        c = slice(0, NT - 1) if part == 0 else slice(NT - 1, NT)
                        act.wait_ge(event("h2_var"), 2 * first + part + 1)
                        act.activation(st2[:, 8:12][:, c], st2[:, 4:8][:, c], ACT.Sqrt).then_inc(event("h2_std"), 1)
                act.wait_ge(event("hmod2"), first + 1)
                for t in order:
                    v = t // TT
                    ps = filled(act, u, f"xT{t}0")
                    for k in range(4):
                        ins = act.activation(hT2[:, k, t * P:(t + 1) * P], ps[:, k * P:(k + 1) * P], ACT.Identity,
                                             bias=hsh2[:, v, k:k + 1], scale=hsc2[:, v, k:k + 1])
                        if k < 3:
                            step(ins)
                    ins.then_inc(free(u, f"xT{t}0"), 1)

            u = le
            act.wait_ge(event("ctx_in"), 16)
            norm_x2(u, 0, E_ORDER, "x_ready", [DEPTH * TT + 1, DEPTH * TT + 2, 0, 0])
            def split_high(q):
                c, i, w = piece(q)
                if i == 0:
                    arrived(act, CH2, c, BASE2)
                if q >= 2:
                    piece_used(act, q - 2)
                act.activation(whi[:, q % 2, :], w, ACT.Copy).then_inc(event("hi_ready"), 1)

            for t in E_ORDER:
                emptied(act, u, f"xT{t}0")
                emptied(act, u, f"xT{t}1")
                act.activation(xhi[:, :, t * P:(t + 1) * P], hT2[:, :, t * P:(t + 1) * P], ACT.Copy).then_inc(event("xhi_ready"), 1)
            split_high(0)
            split_high(1)
            for t in E_ORDER:
                ps = filled(act, u, f"e_kv{t}")
                step(act.activation(eqk[:, t, 512:640], ps[:, 0:P], ACT.Copy))
                copy_rows(u, f"e_kv{t}", ev[:, t, :], ps[:, P:2 * P])
            for q in range(2, 6):
                split_high(q)
            for t in range(NT):
                copy_out(u, f"e_q{t}", eqk[:, t, 0:512], 0)
            for q in range(6, 10):
                split_high(q)
            for t in range(NT):
                copy_out(u, f"e_u{t}", eu[:, t, :], 0, func=ACT.Gelu)
            for q in range(10, 12):
                split_high(q)
            for t in range(NT):
                ps = filled(act, u, f"e_vv{t}")
                copy_rows(u, f"e_vv{t}", evv[:, t, :], ps[:, :], ACT.Gelu, accum_out=st2[:, 12 + t:13 + t])
            for j in range(2):
                copy_out(u, f"ekT{j}", ekT[:, j, :], 0)
            for j in range(4):
                copy_out(u, f"eqT{j}", eqT[:, j, :], 0)
            for t in range(NT):
                act.wait_ge(event("ln_c"), t + 1)
                act.activation(PT2[:, t, :], evv[:, t, :], ACT.Square, accum_out=st2[:, 16 + t:17 + t]).then_inc(event("ln_ssq"), 1)
            act.wait_ge(event("ln_var"), 1)
            act.activation(st2[:, 24:28], st2[:, 20:24], ACT.Sqrt).then_inc(event("ln_std"), 1)
            for g in range(14):
                if g < 8:
                    copy_out(u, f"e_g{g // 4}{g % 4}", eg[:, g % 4, (g // 4) * 512:(g // 4) * 512 + 512], 0)
                if g == 8:
                    for t in range(NT):
                        emptied(act, u, f"e_g1{t}")
                    act.activation(eg[:], eg[:], ACT.Silu).then_inc(event("esilu"), 1)
                if 1 <= g < 13:
                    for i in (2 * g - 2, 2 * g - 1):
                        copy_out(u, f"ep{i}", PT2[:, i % 4, :], 0)
                if g < 12:
                    for i in (2 * g, 2 * g + 1):
                        t, heads = E_UNITS[i]
                        act.wait_ge(event("e_max"), i + 1)
                        if t < TT:
                            h = heads[0]
                            act.activation(L2[:, i % 4, :], L2[:, i % 4, :], ACT.Exp, bias=mx2[:, t, h:h + 1],
                                           accum_out=sm2[:, t, h:h + 1]).then_inc(event("e_exp"), 1)
                        else:
                            ps = filled(act, u, f"el{i}")
                            for a, h in enumerate(heads):
                                ins = act.activation(L2[:, i % 4, a * 256:(a + 1) * 256], ps[:, a * 256:(a + 1) * 256], ACT.Exp,
                                                     bias=mx2[:, t, h:h + 1], scale=0.125, accum_out=sm2[:, t, h:h + 1])
                                if a == 0:
                                    step(ins)
                            ins.then_inc(free(u, f"el{i}"), 1)
                if g in (9, 11):
                    v = (g - 9) // 2
                    for h in range(2):
                        copy_out(u, f"gb{v}{h}", gbr[:, v, h * 512:(h + 1) * 512], 0)
                for t in range(NT):
                    if g == E_LAST[t] // 2 + 1:
                        act.wait_ge(event("e_arg"), t + 1)
                        act.activation(es2[:, t, :], es2[:, t, :], ACT.Exp).then_inc(event("e_es"), 1)
            for t in range(NT):
                copy_out(u, f"eyT{t}0", hT2[:, 0:4, t * P:(t + 1) * P], 0)

            u = lo
            norm_x2(u, 1, O_ORDER, "x2_ready", [1, 2, 3, 4])
            for t in range(NT):
                copy_out(u, f"o_kv{t}", okv[:, t, :], 0)
            for t in range(TT):
                copy_out(u, f"o_q{t}", oqa[:, t, :], 0)
            for t in range(NT):
                emptied(act, u, f"o_kv{t}")
                act.activation(PT2[:, t, 0:P], okv[:, t, 0:P], ACT.Square, accum_out=st2[:, 32 + t:33 + t]).then_inc(event("o_ssq2"), 1)
            for t in range(TT):
                emptied(act, u, f"o_q{t}")
                act.activation(PT2[:, t, 256:512], oqa[:, t, :], ACT.Square, accum_out=st2[:, 36 + t:37 + t]).then_inc(event("o_ssq2"), 1)
            act.wait_ge(event("o_var2"), 1)
            act.activation(st2[:, 48:54], st2[:, 40:46], ACT.Sqrt).then_inc(event("o_std2"), 1)
            for t in range(TT):
                copy_out(u, f"o_g0{t}", og[:, t, 0:512], 0)
            ps = filled(act, u, "kvT")
            copy_rows(u, "kvT", kvT, ps[:, :], ACT.Copy, scale=col[:, C_KVN:C_KVN + 1])
            ps = filled(act, u, "kpT")
            copy_rows(u, "kpT", kpe[64:96, :], ps[64:96, :])
            for h in range(0, MLA_HEADS, 2):
                ps = filled(act, u, f"on{h}")
                copy_rows(u, f"on{h}", okT[0:MLA_NOPE, h, :], ps[0:MLA_NOPE, :])
            for t in range(NT):
                copy_out(u, f"ov{t}0", ova[:, t, 0:512], 0)
            ps = filled(act, u, "qaT")
            step(act.activation(qaT[:, 0, :], ps[:, 0:S], ACT.Copy, scale=col[:, C_QN:C_QN + 1]))
            copy_rows(u, "qaT", qaT[:, 1, :], ps[:, S:2 * S], ACT.Copy, scale=col[:, C_QN + 1:C_QN + 2])
            for t in range(TT):
                for c in (0, 2):
                    copy_out(u, f"oqb{t}{c}", q2[:, t, c * 512:(c + 1) * 512], 0)
            for t in range(TT):
                copy_out(u, f"o_g1{t}", og[:, t, 512:1024], 0)
            for t in range(TT):
                emptied(act, u, f"o_g0{t}")
                emptied(act, u, f"o_g1{t}")
            act.activation(og[:], og[:], ACT.Silu).then_inc(event("osilu"), 1)
            for j in range(0, 8, 2):
                ps = filled(act, u, f"oqT{j}")
                copy_rows(u, f"oqT{j}", oqT[:, 2 * j:2 * j + 2, :], ps[0:MLA_QK, :].rearrange("p (a b) -> p a b", a=2))
            for p in range(17):
                if p >= 1:
                    i = 2 * p - 2
                    copy_out(u, f"mp{i}", PT2[:, i % 4, :], 0)
                if p < 16:
                    for i in (2 * p, 2 * p + 1):
                        t, h = O_UNITS[i]
                        act.wait_ge(event("o_max"), i + 1)
                        ps = filled(act, u, f"ml{i}")
                        copy_rows(u, f"ml{i}", L2[:, i % 4, :], ps[:, :], ACT.Exp, bias=mx2[:, t, h:h + 1], scale=MLA_SCALE,
                                  accum_out=sm2[:, t, h:h + 1])
                if p == 0:
                    for h in range(2):
                        copy_out(u, f"gb0{h}", gbr[:, 0, h * 512:(h + 1) * 512], 0)
            for t in range(TT):
                copy_out(u, f"oyT{t}0", hT2[:, 0:4, t * P:(t + 1) * P], 0)
            for t in range(TT):
                act.wait_ge(event("x3_ready"), t + 1)
                act.activation(Y2[:, TT + t, :], X[:, t, :], ACT.Square, accum_out=st2[:, t:t + 1]).then_inc(event("f_ssq"), 1)
                act.wait_ge(event("f_var"), t + 1)
                act.activation(st2[:, 8 + t:9 + t], st2[:, 4 + t:5 + t], ACT.Sqrt).then_inc(event("f_std"), 1)

        @block.gpsimd
        def _(pool):
            steps, base = [0], [0]

            def step(ins):
                steps[0] += 1
                ins.then_inc(event("pool_step"), 1)

            def settle():
                pool.wait_ge(event("pool_step"), base[0] + steps[0])

            whole = ti[:, 0, :].rearrange("p (t c) -> p t c", t=TT)
            pool.wait_ge(event("pos_in"), 32)
            step(pool.tensor_copy(posf[:], posi[:]))
            settle()
            for t in range(TT):
                step(pool.tensor_scalar(ang[:, t, :], freq, posf[:, t:t + 1], None, ALU.mult))
            settle()
            for dst, quarter in ((sinT, 0.0), (cosT, 0.25)):
                step(pool.tensor_scalar(turn[:], ang[:], 1.0 / (2 * np.pi), quarter, ALU.mult, ALU.add))
                settle()
                step(pool.tensor_scalar(turn[:], turn[:], ROUND, None, ALU.add))
                settle()
                step(pool.tensor_scalar(turn[:], turn[:], -ROUND, None, ALU.add))
                settle()
                for n, part in enumerate(TWO_PI):
                    if n > 0:
                        settle()
                    step(pool.tensor_scalar(whole, turn[:], part, None, ALU.mult))
                    settle()
                    step(pool.tensor_tensor(dst[:], ang[:] if n == 0 else dst[:], whole, ALU.subtract))
                settle()
                step(pool.tensor_scalar(dst[:], dst[:], quarter * 2 * np.pi, PI_BELOW, ALU.add, ALU.min))
                settle()
                pool.tensor_scalar(dst[:], dst[:], -PI_BELOW, None, ALU.max).then_inc(event("sin_in"), 1)
            pool.wait_ge(loaded, LOADS)
            pool.tensor_copy(gm[:], gmf).then_inc(event("gm_ready"), 1)
            pool.wait_ge(event("sin_out"), 2)
            before = steps[0]
            with pool.Fori(0, DEPTH) as l:
                u = lay1
                base[0], steps[0] = l * POOL_STEPS + before, 0

                def rotate(v, half, f0, heads):
                    x1, x2 = v[:, :, :, 0:half], v[:, :, :, half:2 * half]
                    c = cosT[:, :, f0:f0 + half].unsqueeze(2).broadcast_to([P, TT, heads, half])
                    s = sinT[:, :, f0:f0 + half].unsqueeze(2).broadcast_to([P, TT, heads, half])
                    T = [rt[:, q, 0:TT * heads * half].rearrange("p (t h d) -> p t h d", t=TT, h=heads) for q in range(4)]
                    for q, (a, b) in enumerate(((x1, c), (x2, s), (x2, c), (x1, s))):
                        step(pool.tensor_tensor(T[q], a, b, ALU.mult))
                    settle()
                    step(pool.tensor_tensor(x1, T[0], T[1], ALU.subtract))
                    return pool.tensor_tensor(x2, T[2], T[3], ALU.add)

                for t in range(TT):
                    for h in range(2):
                        emptied(pool, u, f"xT{t}{h}", l)
                for name in ("dsa_q", "dsa_kv"):
                    for t in range(TT):
                        emptied(pool, u, f"{name}{t}", l)
                step(rotate(dsaqkv[:, :, 0:640].rearrange("p t (h d) -> p t h d", h=10), 8, 32, 10))
                settle()
                step(pool.tensor_tensor(pw[:, 0:1], ident[:, 0:1], ident[:, 0:1], ALU.mult))
                for t in range(TT):
                    ins = pool.tensor_copy(kdd[:, t, :, :, :],
                                           dsaqkv[:, t, 512:640].rearrange("p (h d) -> p h d", h=2).unsqueeze(2).broadcast_to([P, 2, 2, 64]))
                    if t == 0:
                        step(ins)
                ins.then_inc(event("dsa_rot"), 1)
                for t in range(TT):
                    emptied(pool, u, f"ret_qk{t}", l)
                rotate(retqkv[:, :, 0:512].rearrange("p t (h d) -> p t h d", h=8), 32, 0, 8).then_inc(event("ret_rot"), 1)

                emptied(pool, u, "gk", l)
                for i in range(1, len(LEVELS)):
                    pool.wait_ge(event("gexp"), l * 8 + i)
                    if i >= 3:
                        for r in range(2):
                            filled(pool, u, f"g{i - 2}_{r}", l)
                    pool.tensor_tensor(KL[:, i % 2], gkT[:], E[i % 2], ALU.mult).then_inc(event("gkl"), 1)
                counted("POOL_STEPS", steps[0], POOL_STEPS)

            base[0], steps[0] = before + DEPTH * POOL_STEPS, 0

            def rotate2(x1, x2, y1, y2, c, s, T):
                for q, (a, b) in enumerate(((x1, c), (x2, s), (x2, c), (x1, s))):
                    step(pool.tensor_tensor(T[q], a, b, ALU.mult))
                settle()
                step(pool.tensor_tensor(y1, T[0], T[1], ALU.subtract))
                step(pool.tensor_tensor(y2, T[2], T[3], ALU.add))

            u = le
            pool.wait_ge(event("kk_in"), 16)
            for name in ("e_kv", "e_q"):
                for t in range(TT):
                    emptied(pool, u, f"{name}{t}")
            for t in range(TT):
                v = eqk[:, t, :].rearrange("p (h a b d) -> p h a b d", h=10, a=2, b=2)
                x1, x2 = v[:, :, :, 0, :], v[:, :, :, 1, :]
                c, s = (e_rot[:, q, t, :].rearrange("p (a d) -> p a d", a=2).unsqueeze(1).broadcast_to([P, 10, 2, 16]) for q in range(2))
                T = [ert[:, q, :].rearrange("p (h a d) -> p h a d", h=10, a=2) for q in range(4)]
                rotate2(x1, x2, x1, x2, c, s, T)
                settle()
            for t in range(NT):
                emptied(pool, u, f"e_kv{t}")
                ins = pool.tensor_copy(ekd[:, t], eqk[:, t, 512:640].rearrange("p (h d) -> p h d", h=2).unsqueeze(2).broadcast_to([P, 2, 2, 64]))
                if t < NT - 1:
                    step(ins)
            ins.then_inc(event("e_rot"), 1)

            u = lo
            pool.wait_ge(event("x2_ready"), NT)
            step(pool.memset(okp[:, :, 0:64], 0.0))
            for t in range(NT):
                emptied(pool, u, f"o_kv{t}")
            step(pool.tensor_copy(okp[:, TT:NT, 64:96], okv[:, TT:NT, 128:160]))
            v = okv[:, 0:TT, 128:160].rearrange("p t (a b d) -> p t a b d", a=2, b=2)
            w = okp[:, 0:TT, 64:96].rearrange("p t (a b d) -> p t a b d", a=2, b=2)
            c, s = (o_rot[:, q].rearrange("p t (a d) -> p t a d", a=2) for q in range(2))
            T = [ort[:, q, 0:32 * TT // 2].rearrange("p (t a d) -> p t a d", t=TT, a=2) for q in range(4)]
            rotate2(v[:, :, :, 0, :], v[:, :, :, 1, :], w[:, :, :, 0, :], w[:, :, :, 1, :], c, s, T)
            settle()
            pool.tensor_tensor(pw[:, 0:1], ident[:, 0:1], ident[:, 0:1], ALU.mult).then_inc(event("okp_ready"), 1)
            emptied(pool, u, "kpT")
            pool.tensor_copy(okT[64:96], kpe[64:96, :].unsqueeze(1).broadcast_to([32, MLA_HEADS, NT * P])).then_inc(event("okT_ready"), 1)
            pool.wait_ge(event("okT_ready"), 1)
            for t in range(TT):
                for k in range(3):
                    emptied(pool, u, f"oqb{t}{k}")
            qv = q2.rearrange("p t (h c) -> p t h c", h=MLA_HEADS)
            for a in range(2):
                x1, x2 = qv[:, :, :, 64 + 16 * a:72 + 16 * a], qv[:, :, :, 72 + 16 * a:80 + 16 * a]
                c, s = (o_rot[:, q, :, 8 * a:8 * a + 8].unsqueeze(2).broadcast_to([P, TT, MLA_HEADS, 8]) for q in range(2))
                T = [ort[:, q, :].rearrange("p (t h d) -> p t h d", t=TT, h=MLA_HEADS) for q in range(4)]
                rotate2(x1, x2, x1, x2, c, s, T)
                settle()
            pool.tensor_tensor(pw[:, 1:2], ident[:, 0:1], ident[:, 0:1], ALU.mult).then_inc(event("oq_rot"), 1)

        @block.vector
        def _(dve):
            steps, base = [0], [0]

            def step(ins):
                steps[0] += 1
                ins.then_inc(event("dve_step"), 1)

            def settle():
                dve.wait_ge(event("dve_step"), base[0] + steps[0])

            def carry():
                carried[0] = (carried[0] + 1) % 64
                step(dve.tensor_copy(cw[:, carried[0]:carried[0] + 1], ident[:, 0:1]))

            carried = [0]
            adab = col[:, C_ADAB:C_ADAB + 96].rearrange("p (a f) -> p a f", a=4)
            condv = cact[:].rearrange("p k v -> p v k")
            layv = col[:, C_LAY:C_LAY + DEPTH * LAYC].rearrange("p (l c) -> p l c", l=DEPTH)

            def mod_out(u, name, m, which, vectors, rep=0):
                ps = filled(dve, u, name, rep)
                w = 64 * vectors
                dve.tensor_tensor(mod[:, 4 * m:4 * m + 4, 0:vectors],
                                  ps[:, 0:4 * w].rearrange("p (j v c) -> p j v c", j=4, v=vectors)[:, :, :, 0],
                                  adab[:, which, 4 * m:4 * m + 4].unsqueeze(2).broadcast_to([P, 4, vectors]),
                                  ALU.add).then_inc(free(u, name), 1)

            def mod_sum(chunks, c, chunks_before, sums, vectors, cond, rep=0, rows=range(KD)):
                if rows[0] == 0:
                    arrived(dve, chunks, c, chunks_before, rep)
                slot = ring[:, (chunks_before + c) % RING, :]
                for k in rows:
                    for v in range(vectors):
                        w = slot[:, k * 512:(k + 1) * 512]
                        if k == 0:
                            ins = dve.tensor_scalar(sums[:, v, :], w, cond[:, k, v:v + 1], None, ALU.mult)
                        else:
                            dve.wait_ge(event("dve_step"), base[0] + (steps[0] - vectors + 1))
                            ins = dve.scalar_tensor_tensor(sums[:, v, :], w, cond[:, k, v:v + 1], sums[:, v, :],
                                                           ALU.mult, ALU.add)
                        if k == KD - 1 and v == vectors - 1:
                            ins.then_inc(event("ada_sum"), 1)
                        else:
                            step(ins)

            for b in range(8):
                dve.memset(bank[b][:, :], 0.0).then_inc(bank_free[b], 1)
            step(dve.memset(ones[:], 1.0))
            dve.wait_ge(event("c_ready"), 1)
            for m in range(SHIFTS):
                mod_sum(CH0, m, 0, msum[:, m % 2], 1, cact)
                if m > 0:
                    mod_out(pro, f"ada{m - 1}", m - 1, 0, 1)
            mod_out(pro, f"ada{SHIFTS - 1}", SHIFTS - 1, 0, 1)
            dve.wait_ge(event("x_in"), 32)
            for t in range(TT):
                dve.tensor_copy(mod[:, 16:17, t], ident[:, 0:1]).then_inc(event("x_ready"), 1)
            before = steps[0]
            emptied(dve, pro, "ada2")
            emptied(dve, pro, "ada3")

            with dve.Fori(0, DEPTH) as l:
                u = lay1
                base[0], steps[0] = l * DVE_STEPS + before, 0
                step(dve.tensor_copy(lay[:], layv[:, l, :]))
                settle()
                step(dve.scalar_tensor_tensor(hsc[:], mod[:, 8:16, 0], 1.0, lay[:, 0:8], ALU.add, ALU.mult))
                dve.tensor_copy(hsh[:], mod[:, 0:8, 0]).then_inc(event("hmod_ready"), 1)
                for t in range(TT):
                    dve.wait_ge(event("x_ssq"), l * TT + (t + 1))
                    dve.tensor_scalar(st[:, 2 + t:3 + t], st[:, t:t + 1], 1.0 / D, EPS, ALU.mult, ALU.add).then_inc(event("x_var"), 1)
                    dve.wait_ge(event("x_std"), l * TT + (t + 1))
                    step(dve.reciprocal(st[:, 6 + t:7 + t], st[:, 4 + t:5 + t]))
                    settle()
                    dve.tensor_scalar(Y[:, t, :], X[:, t, :], st[:, 6 + t:7 + t], None, ALU.mult).then_inc(event("xn_ready"), 1)
                for v in range(2):
                    step(dve.tensor_copy(cnow[:, :, v], condv[:, l + v, :]))
                dve.wait_ge(event("hmod_ready"), l + 1)
                for t in range(TT):
                    ps = filled(dve, u, f"xT{t}1", l)
                    for k in range(4):
                        ins = dve.tensor_scalar(hT[:, 4 + k, t * P:(t + 1) * P], ps[:, k * P:(k + 1) * P],
                                                hsc[:, 4 + k:5 + k], hsh[:, 4 + k:5 + k], ALU.mult, ALU.add)
                        if k < 3:
                            step(ins)
                    ins.then_inc(free(u, f"xT{t}1"), 1)

                def low(first, last):
                    for q in range(first, last):
                        dve.wait_ge(event("hi1_ready"), l * len(PIECES1) + (q + 1))
                        dve.tensor_tensor(wlo1[:, q % BUFFERS, :], piece1(q)[2], whi1[:, q % BUFFERS, :],
                                          ALU.subtract).then_inc(event("lo1_ready"), 1)

                for t in range(TT):
                    dve.wait_ge(event("xhi1_ready"), l * TT + (t + 1))
                    c = slice(t * P, (t + 1) * P)
                    dve.tensor_tensor(xlo1[:, :, c], hT[:, :, c], xhi1[:, :, c], ALU.subtract).then_inc(event("xlo1_ready"), 1)
                low(0, 4)
                dve.wait_ge(event("sin_out"), 2)
                dve.wait_ge(loaded, LOADS)
                dve.tensor_copy(wl[:], wl_all[:, l, :]).then_inc(event("wl_ready"), 1)
                for t in range(TT):
                    emptied(dve, u, f"idx{t}", l)
                v = idx[:, :, 0:320].rearrange("p t (h d) -> p t h d", h=5)
                x1, x2 = v[:, :, :, 0:8], v[:, :, :, 8:16]
                c = cosT[:, :, 32:40].unsqueeze(2).broadcast_to([P, TT, 5, 8])
                s = sinT[:, :, 32:40].unsqueeze(2).broadcast_to([P, TT, 5, 8])
                T = [ti[:, q, :].rearrange("p (t h d) -> p t h d", t=TT, h=5) for q in range(4)]
                for q, (a, b) in enumerate(((x1, c), (x2, s), (x2, c), (x1, s))):
                    step(dve.tensor_tensor(T[q], a, b, ALU.mult))
                settle()
                step(dve.tensor_tensor(x1, T[0], T[1], ALU.subtract))
                step(dve.tensor_tensor(x2, T[2], T[3], ALU.add))
                settle()
                dve.tensor_copy(kdi[:], v[:, :, 4, :].unsqueeze(2).broadcast_to([P, TT, 2, 64])).then_inc(event("idx_rot"), 1)
                low(4, 12)

                def scores(t, pieces):
                    n = P * (t + 1)
                    first = 0 if t == 0 else P
                    s_, w_, mask = sc[:, first:first + n], wk[:, first:first + n], cm[:, 256 - n:256]
                    for r in range(2):
                        emptied(dve, u, f"s{t}{r}", l)
                    for h in range(4):
                        r, j = h % 2, h // 2
                        at = ((0, 2 * P)[r] if t == 0 else 512 + 512 * r) + j * n
                        step(dve.scalar_tensor_tensor(s_, RI[:, at:at + n], idx[:, t, 320 + h:321 + h],
                                                      mask if h == 0 else s_, ALU.mult, ALU.add))
                        if h < 3:
                            settle()
                    for i in range(TOPK // 8):
                        src = s_ if i == 0 else w_
                        settle()
                        carry()
                        step(dve.max(m8[:], src))
                        settle()
                        carry()
                        step(dve.match_replace(w_, m8[:], src, TAKEN))
                        n_ = len(pieces) // (TOPK // 8)
                        low(pieces[0] + i * n_, pieces[0] + (i + 1) * n_)
                    settle()
                    step(dve.tensor_tensor(w_, w_, s_, ALU.is_equal))
                    settle()
                    dve.scalar_tensor_tensor(s_, w_, NEG, mask, ALU.mult, ALU.add).then_inc(event("sel_ready"), 1)

                scores(0, range(12, 20))
                ps = filled(dve, u, "z", l)
                step(dve.tensor_scalar(Z[:, 0, :], ps[:, 0:S], lay[:, 16:17], None, ALU.add))
                dve.tensor_scalar(Z[:, 1, :], ps[:, S:2 * S], lay[:, 17:18], None, ALU.add).then_inc(free(u, "z"), 1)
                emptied(dve, u, "z", l)
                dve.scalar_tensor_tensor(AZ, Z, -1.0, Z, ALU.mult, ALU.max).then_inc(event("z_ready"), 1)
                dve.wait_ge(event("z_ready"), l + 1)
                step(dve.tensor_scalar(Z, Z, 0.0, None, ALU.min))
                scores(1, range(20, 36))
                low(36, 40)
                dve.wait_ge(event("lg_ready"), l + 1)
                step(dve.tensor_tensor(LG, Z, LG, ALU.subtract))
                settle()
                for f in range(2):
                    step(dve.tensor_tensor_scan(bcum[:, f, :], reset, LG[:, f, :], 0.0, ALU.mult, ALU.add))
                settle()

                bf = bcum[:].rearrange("p f s -> p (f s)")

                def gla_sub(i):
                    if i >= len(LEVELS):
                        return
                    if i >= 3:
                        dve.wait_ge(event("gkl"), l * 8 + (i - 2))
                        dve.wait_ge(event("gql"), l * 8 + (i - 2))
                    e = E[i % 2]
                    if LEVELS[i] == "cross":
                        b = lambda a: bcum[:, :, a:a + 1].broadcast_to([P, 2, 64])
                        step(dve.tensor_copy(e[:, :, 128:192], bcum[:, :, 128:192]))
                        step(dve.tensor_tensor(e[:, :, 192:256], bcum[:, :, 192:256], b(191), ALU.add))
                        step(dve.tensor_tensor(e[:, :, 64:128], b(127), bcum[:, :, 64:128], ALU.subtract))
                        step(dve.tensor_tensor(e[:, :, 0:64], b(63), bcum[:, :, 0:64], ALU.subtract))
                        settle()
                        ins = dve.tensor_tensor(e[:, :, 0:64], e[:, :, 0:64], b(127), ALU.add)
                    else:
                        h = LEVELS[i]
                        v = bf.rearrange("p (n c) -> p n c", c=2 * h)
                        ev = e.rearrange("p f s -> p (f s)").rearrange("p (n c) -> p n c", c=2 * h)
                        n = 512 // (2 * h)
                        mid = v[:, :, h - 1:h].broadcast_to([P, n, h])
                        if h == GLA_CHUNK:
                            step(dve.tensor_copy(ev[:, :, h:2 * h], v[:, :, h:2 * h]))
                        else:
                            step(dve.tensor_tensor(ev[:, :, h:2 * h], v[:, :, h:2 * h], mid, ALU.subtract))
                        ins = dve.tensor_tensor(ev[:, :, 0:h], mid, v[:, :, 0:h], ALU.subtract)
                    ins.then_inc(event("gsub"), 1)

                def gla_mul(i):
                    if i < len(LEVELS):
                        dve.wait_ge(event("gexp"), l * 8 + i)
                        dve.tensor_tensor(QL[i % 2], gqT[:], E[i % 2], ALU.mult).then_inc(event("gql"), 1)

                def gla_take(i):
                    kind = LEVELS[i]
                    for r in range(2):
                        ps = filled(dve, u, f"g{i}_{r}", l)
                        if kind == "cross":
                            dve.tensor_copy(AT[:, r, 2], ps[:, 0:2 * P].rearrange("p (j c) -> p j c", j=2)).then_inc(free(u, f"g{i}_{r}"), 1)
                            continue
                        dst = AT[:, r, 0:2].rearrange("p t j c -> p (t j) c")
                        src = ps[:, :].rearrange("p (b c) -> p b c", b=4)
                        if kind == "diag":
                            ins = dve.tensor_tensor(dst, src, ident[:].unsqueeze(1).broadcast_to([P, 4, P]), ALU.mult)
                        else:
                            emptied(dve, u, f"g{i - 1}_{r}", l)
                            carry()
                            ins = dve.copy_predicated(dst, gm[:, i - 1, :].unsqueeze(1).broadcast_to([P, 4, P]), src)
                        ins.then_inc(free(u, f"g{i}_{r}"), 1)

                dve.wait_ge(event("gm_ready"), 1)
                dve.wait_ge(event("ret_rot"), l + 1)
                emptied(dve, u, "gq", l)
                gla_sub(1)

                def head_norm(kind, o, at, gate, ready, silu):
                    dve.wait_ge(event(kind + "_ssq"), l + 1)
                    dve.tensor_scalar(st[:, at + 8:at + 16], st[:, at:at + 8], 1.0 / P, EPS, ALU.mult,
                                      ALU.add).then_inc(event(kind + "_var"), 1)
                    dve.wait_ge(event(kind + "_std"), l + 1)
                    step(dve.reciprocal(st[:, at + 24:at + 32], st[:, at + 16:at + 24]))
                    gated(o, st[:, at + 24:at + 32], 4, gate, ready, silu)

                def gated(o, factor, heads, gate, ready, silu):
                    dve.wait_ge(event("silu_ready"), l * 3 + silu)
                    for t in range(TT):
                        settle()
                        ps = filled(dve, u, f"{o}{t}", l)
                        w = 512 // heads
                        tmp = RS[:].rearrange("p a b -> p (a b)")[:, 0:512]
                        dve.tensor_tensor(tmp.rearrange("p (h d) -> p h d", h=heads),
                                          ps[:, :].rearrange("p (h d) -> p h d", h=heads),
                                          factor[:, t * heads:(t + 1) * heads].unsqueeze(2).broadcast_to([P, heads, w]),
                                          ALU.mult).then_inc(free(u, f"{o}{t}"), 1)
                        emptied(dve, u, f"{o}{t}", l)
                        dve.tensor_tensor(gate[:, t, :], tmp, gate[:, t, :], ALU.mult).then_inc(event(ready), 1)
                        dve.wait_ge(event(ready), l * TT + (t + 1))

                g = 0
                for name in ("ret_g", "dsa_g", "gla_g") + tuple(f"merge{m}" for m in range(MERGES)):
                    for t in range(TT):
                        if name in SPLIT1:
                            low(40 + 4 * g, min(44 + 4 * g, len(PIECES1)))
                        gla_sub(g + 2)
                        gla_mul(g + 1)
                        if g < 4:
                            ps = filled(dve, u, f"rs{g}", l)
                            dve.tensor_tensor(RS[:, g % 2, :], ps[:, 0:384], decay[:, g, :], ALU.mult).then_inc(free(u, f"rs{g}"), 1)
                        if 5 <= g <= 10:
                            i = g - 5
                            tq, heads = DSA_UNITS[i]
                            n, nh = P * (tq + 1), len(heads)
                            first = 0 if tq == 0 else P
                            if i in (0, 2):
                                dve.wait_ge(event("sel_ready"), l * TT + (tq + 1))
                            ps = filled(dve, u, f"dl{i}", l)
                            lv = L[:, i % 2, :].rearrange("p (h n) -> p h n", h=nh)
                            dve.scalar_tensor_tensor(lv, ps[:, :].rearrange("p (h n) -> p h n", h=nh), 0.125,
                                                     sc[:, first:first + n].unsqueeze(1).broadcast_to([P, nh, n]),
                                                     ALU.mult, ALU.add).then_inc(free(u, f"dl{i}"), 1)
                            emptied(dve, u, f"dl{i}", l)
                            dve.tensor_reduce(mx[:, tq, PARTS[i]:PARTS[i] + nh], lv, AX, ALU.max,
                                              negate=True).then_inc(event("dmax"), 1)
                        if g < len(LEVELS):
                            gla_take(g)
                        if g == 8:
                            emptied(dve, u, "g8_0", l)
                            emptied(dve, u, "g8_1", l)
                            dve.tensor_copy(st[:, 95:96], AT[:, 1, 2, 1, 127:128]).then_inc(event("at_ready"), 1)
                        if g == 5:
                            head_norm("r", "ro", 8, retg, "ret_ready", 1)
                        if g == 10:
                            head_norm("g", "go", 40, glag, "gla_ready", 3)
                        if g == 12:
                            filled(dve, u, "do1", l)
                            dve.wait_ge(event("dexp"), l * 6 + 6)
                            step(dve.reciprocal(st[:, 80:96], sm[:].rearrange("p t h -> p (t h)")))
                            gated("do", st[:, 80:96], 8, dsag, "dsa_ready", 2)
                        g += 1
                    if name.startswith("merge"):
                        m = int(name[5])
                        own = m >= SHIFTS
                        mod_sum(CH1, [n for n, _ in CH1].index(f"ada{m}"), len(CH0), msum[:, m % 2], 1 if own else 2,
                                cact if own else cnow, l)
                        if m > 0:
                            own = m - 1 >= SHIFTS
                            mod_out(u, f"ada{m - 1}", m - 1, l if own else l + 1, 1 if own else 2, l)

                dve.wait_ge(event("g_sig"), l * 2 + 2)
                emptied(dve, u, f"merge{MERGES - 1}0", l)
                emptied(dve, u, f"merge{MERGES - 1}1", l)
                for b in range(3):
                    for t in range(TT):
                        for h in range(2):
                            name = f"br{b}{t}{h}"
                            ps = filled(dve, u, name, l)
                            gv = G[:, t, b * D + h * 512:b * D + h * 512 + 512]
                            yv = Y[:, t, h * 512:(h + 1) * 512]
                            dve.tensor_tensor(yv if b == 0 else gv, ps[:, :], gv, ALU.mult).then_inc(free(u, name), 1)
                            if b == 0:
                                continue
                            emptied(dve, u, name, l)
                            emptied(dve, u, f"br{b - 1}{t}{h}", l)
                            settle()
                            ins = dve.tensor_tensor(yv, yv, gv, ALU.add)
                            if b == 2 and h == 1:
                                ins.then_inc(event("y_ready"), 1)
                            else:
                                step(ins)
                    if b == 0:
                        mod_out(u, f"ada{MERGES - 1}", MERGES - 1, l, 1, l)
                for t in range(TT):
                    ps = filled(dve, u, f"yT{t}1", l)
                    dve.tensor_copy(hT[:, 4:8, t * P:(t + 1) * P], ps[:, :].rearrange("p (k c) -> p k c", k=4)).then_inc(free(u, f"yT{t}1"), 1)
                emptied(dve, u, f"ada{MERGES - 2}", l)
                emptied(dve, u, f"ada{MERGES - 1}", l)
                step(dve.tensor_tensor(gpo[:], mod[:, 16:24, 0], lay[:, 8:16], ALU.mult))
                settle()
                dve.tensor_tensor(DG, ident[:].unsqueeze(1).broadcast_to([P, KD, P]),
                                  gpo[:].unsqueeze(2).broadcast_to([P, KD, P]), ALU.mult).then_inc(event("diag_ready"), 1)
                for t in range(TT):
                    for h in range(2):
                        emptied(dve, u, f"out{t}{h}", l)
                    step(dve.tensor_tensor(st[:, 72 + 2 * t:73 + 2 * t], st[:, 72 + 2 * t:73 + 2 * t],
                                           st[:, 73 + 2 * t:74 + 2 * t], ALU.add))
                    settle()
                    dve.tensor_scalar(st[:, 76 + t:77 + t], st[:, 72 + 2 * t:73 + 2 * t], 1.0 / D, EPS, ALU.mult,
                                      ALU.add).then_inc(event("o_var"), 1)
                    dve.wait_ge(event("o_std"), l * TT + (t + 1))
                    step(dve.reciprocal(st[:, 8 + t:9 + t], st[:, 78 + t:79 + t]))
                    if t == 0:
                        emptied(dve, u, "gb0", l)
                        emptied(dve, u, "gb1", l)
                    settle()
                    step(dve.scalar_tensor_tensor(Y[:, t, :], Y[:, t, :], st[:, 8 + t:9 + t], gpb[:], ALU.mult, ALU.mult))
                    settle()
                    dve.tensor_tensor(X[:, t, :], X[:, t, :], Y[:, t, :], ALU.add).then_inc(event("x_ready"), 1)
                counted("DVE_STEPS", steps[0], DVE_STEPS)

            base[0], steps[0] = before + DEPTH * DVE_STEPS, 0
            sink = col[:, C_SINK:C_SINK + 8]

            def modulate2(n):
                for v in range(2):
                    step(dve.scalar_tensor_tensor(hsc2[:, v, :], mod[:, 8:16, v], 1.0,
                                                  col[:, C_NG + 8 * n:C_NG + 8 * n + 8], ALU.add, ALU.mult))
                    ins = dve.tensor_copy(hsh2[:, v, :], mod[:, 0:8, v])
                    if v == 0:
                        step(ins)
                ins.then_inc(event("hmod2"), 1)

            def diagonal(dst, v):
                dve.tensor_tensor(dst, ident[:].unsqueeze(1).broadcast_to([P, KD, P]),
                                  mod[:, 16:24, v].unsqueeze(2).broadcast_to([P, KD, P]), ALU.mult).then_inc(event("diag_ready"), 1)

            def norm_x2(n, order, part):
                first, last = (0, NT - 1) if part == 0 else (NT - 1, NT)
                dve.wait_ge(event("h2_ssq"), NT * n + last)
                dve.tensor_scalar(st2[:, 4 + first:4 + last], st2[:, first:last], 1.0 / D, EPS, ALU.mult,
                                  ALU.add).then_inc(event("h2_var"), 1)
                dve.wait_ge(event("h2_std"), 2 * n + part + 1)
                step(dve.reciprocal(st2[:, 28 + first:28 + last], st2[:, 8 + first:8 + last]))
                settle()
                for i in range(first, last):
                    t = order[i]
                    dve.tensor_scalar(Y2[:, t, :], X[:, t, :], st2[:, 28 + i:29 + i], None, ALU.mult).then_inc(event("h2_ready"), 1)

            def scale_x2(u, n, order):
                dve.wait_ge(event("hmod2"), n + 1)
                for t in order:
                    v = t // TT
                    ps = filled(dve, u, f"xT{t}1")
                    for k in range(4):
                        ins = dve.tensor_scalar(hT2[:, 4 + k, t * P:(t + 1) * P], ps[:, k * P:(k + 1) * P],
                                                hsc2[:, v, 4 + k:5 + k], hsh2[:, v, 4 + k:5 + k], ALU.mult, ALU.add)
                        if k < 3:
                            step(ins)
                    ins.then_inc(free(u, f"xT{t}1"), 1)

            def add_half(u, name, t, h, v):
                ps = filled(dve, u, f"{name}{t}{h}")
                c = slice(h * 512, (h + 1) * 512)
                dve.tensor_tensor(Y2[:, t, c], ps[:, :], gbr[:, v, c], ALU.mult).then_inc(free(u, f"{name}{t}{h}"), 1)
                emptied(dve, u, f"{name}{t}{h}")
                return dve.tensor_tensor(X[:, t, c], X[:, t, c], Y2[:, t, c], ALU.add)

            u = le
            dve.wait_ge(event("x_ready"), (DEPTH + 1) * TT)
            dve.wait_ge(event("ctx_in"), 16)
            emptied(dve, lay1, "ada2", DEPTH - 1)
            emptied(dve, lay1, "ada3", DEPTH - 1)
            norm_x2(0, E_ORDER, 0)
            modulate2(0)
            norm_x2(0, E_ORDER, 1)
            scale_x2(u, 0, E_ORDER)
            for i, t in enumerate(E_ORDER):
                dve.wait_ge(event("xhi_ready"), i + 1)
                c = slice(t * P, (t + 1) * P)
                dve.tensor_tensor(xlo[:, :, c], hT2[:, :, c], xhi[:, :, c], ALU.subtract).then_inc(event("xlo_ready"), 1)
            for q in range(len(E_SPLIT) * SPLIT_PIECES):
                w = piece(q)[2]
                dve.wait_ge(event("hi_ready"), q + 1)
                dve.tensor_tensor(wlo[:, q % 2, :], w, whi[:, q % 2, :], ALU.subtract).then_inc(event("lo_ready"), 1)
            step(dve.tensor_scalar(nsink[:], sink, -1.0, None, ALU.mult))
            dve.wait_ge(event("kk_in"), 16)
            for t in range(NT):
                emptied(dve, u, f"e_vv{t}")
                step(dve.tensor_scalar(st2[:, 12 + t:13 + t], st2[:, 12 + t:13 + t], 1.0 / 512, None, ALU.mult))
                settle()
                dve.tensor_scalar(evv[:, t, :], evv[:, t, :], st2[:, 12 + t:13 + t], None, ALU.subtract).then_inc(event("ln_c"), 1)
            dve.wait_ge(event("ln_ssq"), NT)
            dve.tensor_scalar(st2[:, 20:24], st2[:, 16:20], 1.0 / 512, EPS, ALU.mult, ALU.add).then_inc(event("ln_var"), 1)
            dve.wait_ge(event("ln_std"), 1)
            step(dve.reciprocal(st2[:, 54:58], st2[:, 24:28]))
            settle()
            for t in range(NT):
                step(dve.scalar_tensor_tensor(evv[:, t, :], evv[:, t, :], st2[:, 54 + t:55 + t], lng, ALU.mult, ALU.mult))
                settle()
                dve.tensor_tensor(evv[:, t, :], evv[:, t, :], lnb, ALU.add).then_inc(event("ln_ready"), 1)

            def sum2(name, rows=range(KD)):
                mod_sum(CH2, chunk2(name), BASE2, msum2[sum_number(chunk2(name)) % 2], 2, cnow, rows=rows)

            def e_gated(t):
                dve.wait_ge(event("e_es"), t + 1)
                if t < TT:
                    dve.wait_ge(event("e_exp"), E_LAST[t] + 1)
                else:
                    emptied(dve, u, f"el{E_LAST[t]}")
                step(dve.tensor_tensor(r2[:, t, 0:8], sm2[:, t, 0:8], es2[:, t, :], ALU.add))
                settle()
                step(dve.reciprocal(r2[:, t, 0:8], r2[:, t, 0:8]))
                settle()
                ps = filled(dve, u, f"eo{t}")
                dve.tensor_tensor(etmp.rearrange("p (h d) -> p h d", h=8), ps[:, :].rearrange("p (h d) -> p h d", h=8),
                                  r2[:, t, 0:8].unsqueeze(2).broadcast_to([P, 8, 64]), ALU.mult).then_inc(free(u, f"eo{t}"), 1)
                emptied(dve, u, f"eo{t}")
                dve.tensor_tensor(eg[:, t, 0:512], etmp, eg[:, t, 0:512], ALU.mult).then_inc(event("em_ready"), 1)
                dve.wait_ge(event("em_ready"), t + 1)

            for g in range(14):
                if g < 12:
                    for i in (2 * g, 2 * g + 1):
                        t, heads = E_UNITS[i]
                        nh = len(heads)
                        ps = filled(dve, u, f"el{i}")
                        m = mx2[:, t, heads[0]:heads[-1] + 1:2] if nh > 1 else mx2[:, t, heads[0]:heads[0] + 1]
                        ns = nsink[:, heads[0]:heads[-1] + 1:2] if nh > 1 else nsink[:, heads[0]:heads[0] + 1]
                        if t < TT:
                            dve.scalar_tensor_tensor(L2[:, i % 4, :], ps[:, :], 0.125, near[:, t, :], ALU.mult,
                                                     ALU.add).then_inc(free(u, f"el{i}"), 1)
                            emptied(dve, u, f"el{i}")
                            step(dve.tensor_reduce(m, L2[:, i % 4, :], AX, ALU.max, negate=True))
                            settle()
                            dve.tensor_tensor(m, m, ns, ALU.min).then_inc(event("e_max"), 1)
                        else:
                            step(dve.tensor_reduce(m, ps[:, :].rearrange("p (h n) -> p h n", h=nh), AX, ALU.max, negate=True))
                            settle()
                            dve.scalar_tensor_tensor(m, m, 0.125, ns, ALU.mult, ALU.min).then_inc(event("e_max"), 1)
                for t in range(NT):
                    if g == E_LAST[t] // 2:
                        dve.wait_ge(event("e_max"), E_LAST[t] + 1)
                        dve.tensor_tensor(es2[:, t, :], mx2[:, t, 0:8], sink, ALU.add).then_inc(event("e_arg"), 1)
                if g in E_ADA:
                    mod_out(u, E_ADA[g], int(E_ADA[g][-1]), 2 if E_ADA[g][3] == "g" else 3, 2)
                if g in E_SUM:
                    sum2(*E_SUM[g])
                if g == 8:
                    emptied(dve, u, "adag4")
                    emptied(dve, u, "adag5")
                    diagonal(DG2, 0)
                if g == 9:
                    filled(dve, u, "gb01")
                    diagonal(DG2, 1)
                if g == 7:
                    for j in range(4):
                        ps = filled(dve, u, f"gs{j}")
                        for a in range(2):
                            q = 2 * j + a
                            uv = eu[:, :, q * 64:(q + 1) * 64]
                            ins = dve.scalar_tensor_tensor(uv, ps[:, a * 256:(a + 1) * 256].rearrange("p (t c) -> p t c", t=NT),
                                                           col[:, C_BS + q:C_BS + q + 1], uv, ALU.add, ALU.mult)
                            if a == 0:
                                step(ins)
                        ins.then_inc(free(u, f"gs{j}"), 1)
                if g == 9:
                    for j in range(4):
                        emptied(dve, u, f"gs{j}")
                    dve.wait_ge(event("esilu"), 1)
                    step(dve.tensor_tensor(eg[:, :, 512:1024], eu[:], eg[:, :, 512:1024], ALU.mult))
                    e_gated(0)
                if g == 10:
                    e_gated(1)
                if g == 12:
                    e_gated(2)
            e_gated(3)
            for t in range(NT):
                ps = filled(dve, u, f"eyT{t}1")
                dve.tensor_copy(hT2[:, 4:8, t * P:(t + 1) * P], ps[:, :].rearrange("p (k c) -> p k c", k=4)).then_inc(free(u, f"eyT{t}1"), 1)
            sum2("ada2")
            for t in range(NT):
                step(add_half(u, "eout", t, 0, t // TT))
            mod_out(u, "ada2", 2, 3, 2)
            sum2("ada3")
            for t in range(NT):
                if t == NT - 1:
                    norm_x2(1, O_ORDER, 0)
                    mod_out(u, "ada3", 3, 3, 2)
                add_half(u, "eout", t, 1, t // TT).then_inc(event("x2_ready"), 1)

            u = lo
            dve.wait_ge(event("x2_ready"), NT)
            norm_x2(1, O_ORDER, 1)
            modulate2(1)
            scale_x2(u, 1, O_ORDER)
            mod_sum(CH2, chunk2("adah4"), BASE2, msum3[0], 1, cnow)
            dve.wait_ge(event("o_ssq2"), NT + TT)
            step(dve.tensor_scalar(st2[:, 40:44], st2[:, 32:36], 1.0 / 128, EPS, ALU.mult, ALU.add))
            dve.tensor_scalar(st2[:, 44:46], st2[:, 36:38], 1.0 / 256, EPS, ALU.mult, ALU.add).then_inc(event("o_var2"), 1)
            dve.wait_ge(event("o_std2"), 1)
            step(dve.reciprocal(st2[:, 58:64], st2[:, 48:54]))
            settle()
            for t in range(NT):
                ins = dve.tensor_scalar(okv[:, t, 0:P], okv[:, t, 0:P], st2[:, 58 + t:59 + t], None, ALU.mult)
                if t < NT - 1:
                    step(ins)
            ins.then_inc(event("okv_ready"), 1)
            for t in range(TT):
                ins = dve.tensor_scalar(oqa[:, t, :], oqa[:, t, :], st2[:, 62 + t:63 + t], None, ALU.mult)
                if t < TT - 1:
                    step(ins)
            ins.then_inc(event("oqa_ready"), 1)
            mod_out(u, "adah4", 4, 3, 1)
            for h in range(1, MLA_HEADS, 2):
                ps = filled(dve, u, f"on{h}")
                dve.tensor_copy(okT[0:MLA_NOPE, h, :], ps[0:MLA_NOPE, :]).then_inc(free(u, f"on{h}"), 1)
            for t in range(NT):
                ps = filled(dve, u, f"ov{t}1")
                dve.tensor_copy(ova[:, t, 512:1024], ps[:, :]).then_inc(free(u, f"ov{t}1"), 1)
            for t in range(TT):
                ps = filled(dve, u, f"oqb{t}1")
                dve.tensor_copy(q2[:, t, 512:1024], ps[:, :]).then_inc(free(u, f"oqb{t}1"), 1)
            mod_sum(CH2, chunk2("adah5"), BASE2, msum3[1], 1, cnow)
            for j in range(1, 8, 2):
                ps = filled(dve, u, f"oqT{j}")
                dve.tensor_copy(oqT[:, 2 * j:2 * j + 2, :], ps[0:MLA_QK, :].rearrange("p (a b) -> p a b", a=2)).then_inc(free(u, f"oqT{j}"), 1)

            mod_out(u, "adah5", 5, 3, 1)
            emptied(dve, u, "adah4")
            emptied(dve, u, "adah5")
            diagonal(DG3, 0)

            def o_gated(q):
                t, h0 = q // 2, 8 * (q % 2)
                emptied(dve, u, f"ml{8 * q + 7}")
                step(dve.reciprocal(r2[:, t, h0:h0 + 8], sm2[:, t, h0:h0 + 8]))
                settle()
                ps = filled(dve, u, f"mo{q}")
                dve.tensor_tensor(otmp.rearrange("p (h d) -> p h d", h=8), ps[:, :].rearrange("p (h d) -> p h d", h=8),
                                  r2[:, t, h0:h0 + 8].unsqueeze(2).broadcast_to([P, 8, 64]), ALU.mult).then_inc(free(u, f"mo{q}"), 1)
                emptied(dve, u, f"mo{q}")
                dve.wait_ge(event("osilu"), 1)
                gv = og[:, t, h0 * 64:h0 * 64 + 512]
                ins = dve.tensor_tensor(gv, otmp, gv, ALU.mult)
                if q % 2:
                    ins.then_inc(event("om_ready"), 1)
                    dve.wait_ge(event("om_ready"), t + 1)
                else:
                    step(ins)
                    settle()

            for p in range(19):
                if p < 16:
                    for i in (2 * p, 2 * p + 1):
                        t, h = O_UNITS[i]
                        ps = filled(dve, u, f"ml{i}")
                        step(dve.tensor_reduce(mx2[:, t, h:h + 1], ps[:, :], AX, ALU.max, negate=True))
                        settle()
                        dve.tensor_scalar(mx2[:, t, h:h + 1], mx2[:, t, h:h + 1], MLA_SCALE, None, ALU.mult).then_inc(event("o_max"), 1)
                if 1 <= p < 17:
                    i = 2 * p - 1
                    ps = filled(dve, u, f"mp{i}")
                    dve.tensor_copy(PT2[:, i % 4, :], ps[:, :]).then_inc(free(u, f"mp{i}"), 1)
                if p >= 6 and (p - 6) % 4 == 0:
                    o_gated((p - 6) // 4)
            for t in range(TT):
                ps = filled(dve, u, f"oyT{t}1")
                dve.tensor_copy(hT2[:, 4:8, t * P:(t + 1) * P], ps[:, :].rearrange("p (k c) -> p k c", k=4)).then_inc(free(u, f"oyT{t}1"), 1)
            for t in range(TT):
                step(add_half(u, "oout", t, 0, 0))
                add_half(u, "oout", t, 1, 0).then_inc(event("x3_ready"), 1)
                if t == 0:
                    dve.wait_ge(event("fing_in"), 16)
                dve.wait_ge(event("f_ssq"), t + 1)
                dve.tensor_scalar(st2[:, 4 + t:5 + t], st2[:, t:t + 1], 1.0 / D, EPS, ALU.mult, ALU.add).then_inc(event("f_var"), 1)
                dve.wait_ge(event("f_std"), t + 1)
                step(dve.reciprocal(st2[:, 28 + t:29 + t], st2[:, 8 + t:9 + t]))
                settle()
                dve.scalar_tensor_tensor(Y2[:, t, :], X[:, t, :], st2[:, 28 + t:29 + t], fing, ALU.mult,
                                         ALU.mult).then_inc(event("out_ready"), 1)

def chunk_of(w, k):
    return w.reshape(k, P, w.shape[1]).transpose(1, 0, 2).reshape(P, -1)


def lay_out(i):
    w = []
    cols1 = lambda l, n: i["w_in"][l][:, IN1[n][0]:IN1[n][0] + IN1[n][1]]
    ada = [i["ada_w"][0], i["ada_w"][1], i["w_ada_2"][0], i["w_ada_2"][1]]

    def ada_part(a, m):
        return chunk_of(ada[a][:, m * 512:(m + 1) * 512], KD)

    for m in range(SHIFTS):
        w.append(ada_part(0, m))
    for l in range(DEPTH):
        for name, width in CH1:
            if name == "idx":
                a = np.concatenate([cols1(l, n) for n in ("idx_q", "idx_k", "idx_w", "gla_a")], 1)
            elif name == "gla_qk":
                a = np.concatenate([cols1(l, n) for n in ("gla_q", "gla_k")], 1)
            elif name == "dsa_kv":
                a = np.concatenate([cols1(l, n) for n in ("dsa_k", "dsa_v")], 1)
            elif name == "ret_qk":
                a = np.concatenate([cols1(l, n) for n in ("ret_q", "ret_k")], 1)
            elif name.startswith("merge"):
                m = int(name[5])
                a = cols1(l, "merge")[:, m * 512:(m + 1) * 512]
            elif name.startswith("ada"):
                w.append(ada_part(l + 1 if int(name[3]) < SHIFTS else l, int(name[3])))
                continue
            elif name.startswith("br"):
                w.append(chunk_of(i[("w_br_ret", "w_br_dsa", "w_br_gla")[int(name[2])]][l], 4))
                continue
            elif name.startswith("out"):
                h = int(name[3])
                a = i["w_out"][l][:, h * 512:(h + 1) * 512]
            else:
                a = cols1(l, name)
            w.append(chunk_of(a, KD))
            assert w[-1].shape[1] == width, name
    we, wo = i["w_in0_2"][0], i["w_in1_2"][0]
    heads = i["w_kvb_2"][0].reshape(P, MLA_HEADS, MLA_NOPE + MLA_V)
    more = {
        "e_kv": we[:, 512:768], "e_q": we[:, 0:512], "e_u": we[:, 768:1280], "e_vv": we[:, 1280:1792],
        "e_g0": we[:, 1792:2304], "e_g1": we[:, 2304:2816],
        "e_o0": i["w_out0_2"][0][:, 0:512], "e_o1": i["w_out0_2"][0][:, 512:1024],
        "o_kv": wo[:, 256:416], "o_q": wo[:, 0:256], "o_g0": wo[:, 416:928], "o_g1": wo[:, 928:1440],
        "o_kvb": np.concatenate([heads[:, :, 0:MLA_NOPE].reshape(P, -1), heads[:, :, MLA_NOPE:].reshape(P, -1)], 1),
        "o_qb": i["w_qb_2"][0], "o_o0": i["w_out1_2"][0][:, 0:512], "o_o1": i["w_out1_2"][0][:, 512:1024],
    }
    for name, width in CH2:
        if name == "e_ws":
            w.append(i["gm_ws_2"][0].transpose(2, 0, 1).reshape(P, -1))
        elif name.startswith("ada"):
            w.append(ada_part(2 if name[3] == "g" else 3, int(name[-1])))
        else:
            w.append(chunk_of(more[name], more[name].shape[0] // P))
        assert w[-1].shape[1] == width, name
    weights = np.zeros((len(w), P, SLOT), np.float32)
    for n, a in enumerate(w):
        weights[n, :, 0:a.shape[1]] = a

    def column(v):
        return np.asarray(v).reshape(-1, P).T

    cols = np.zeros((P, N_COLS), np.float32)
    for v, name in enumerate((i["c"][0], i["c_2"][0], i["c_ctx_2"])):
        cols[:, C_CT + v:C_CT + 24:3] = column(name)
    for a, b in enumerate((i["ada_b"][0], i["ada_b"][1], i["b_ada_2"][0], i["b_ada_2"][1])):
        cols[:, C_ADAB + 24 * a:C_ADAB + 24 * a + 24] = column(b)
    for l in range(DEPTH):
        at = C_LAY + l * LAYC
        cols[:, at:at + 8] = column(i["pre_norm"][l])
        cols[:, at + 8:at + 16] = column(i["post_norm"][l])
        cols[:, at + 16:at + 18] = column(i["gla_b_lr"][l])
        cols[:, C_NG + 8 * l:C_NG + 8 * l + 8] = column(i["norm_g_2"][l])
    cols[:, C_QN:C_QN + 2] = column(i["q_norm_2"][0])
    cols[:, C_KVN:C_KVN + 1] = column(i["kv_norm_2"][0])
    cols[:, C_BS:C_BS + 8] = i["gm_bs_2"][0].T
    cols[:, C_SINK:C_SINK + 8] = i["sink0_2"][0][None, :]

    a = np.arange(P)
    k1 = np.zeros((P, N_K1), np.float32)
    for h in range(4):
        lg = np.log1p(-np.exp2(-5.0 - h))
        rel = np.arange(S)[None, :] - a[:, None]
        full = np.where(rel >= 0, np.exp(lg * np.maximum(rel, 0)), 0.0) * 0.125
        k1[:, K_DECAY + 384 * h:K_DECAY + 384 * h + 256] = full
        k1[:, K_DECAY + 384 * h + 256:K_DECAY + 384 * h + 384] = full[:, 0:P]
    k1[:, K_CM + P:K_CM + 2 * P] = np.where(a[None, :] > a[:, None], NEG, 0.0)
    k1[:, K_RESET:K_RESET + S] = (np.arange(S) % GLA_CHUNK != 0)[None, :]
    f = np.float32
    k1[:, K_FREQ:K_FREQ + 32] = f(10000.0) ** (-np.arange(32, dtype=f) * f(2.0) / f(64))
    k1[:, K_FREQ + 32:K_FREQ + 40] = f(500000.0) ** (-np.arange(8, dtype=f) * f(2.0) / f(16))
    gmask = np.zeros((P, len(HALVES), P), np.float32)
    key, query = a[:, None], a[None, :]
    for n, h in enumerate(HALVES):
        gmask[:, n, :] = (key // (2 * h) == query // (2 * h)) & (key % (2 * h) < h) & (query % (2 * h) >= h)
    k2 = np.zeros((P, N_K2 + D), np.float32)
    for at, half in ((K_EROT, 16), (K_OROT, 8)):
        inv = f(10000.0) ** (-np.arange(half, dtype=f) / f(half))
        for t in range(TT):
            tok = t * P + a
            for rc, p in enumerate((tok // 64, tok % 64)):
                ang = p.astype(f)[:, None] * inv[None, :]
                for q, v in enumerate((np.cos(ang), np.sin(ang))):
                    c0 = at + (q * TT + t) * 2 * half + rc * half
                    k2[:, c0:c0 + half] = v
    k2[:, K_NEAR + P:K_NEAR + 2 * P] = np.where(a[None, :] <= a[:, None], 0.0, NEG)
    k2[:, K_NEAR + 512:K_NEAR + 512 + P] = np.where(a[:, None] <= a[None, :], 0.0, NEG)
    k2[:, K_LNG:K_LNG + 512] = i["gm_ln_g_2"][0][None, :]
    k2[:, K_LNB:K_LNB + 512] = i["gm_ln_b_2"][0][None, :]
    k2[:, N_K2:] = i["final_g_2"][None, :]
    return {
        "x": i["x"][0], "pos": np.ascontiguousarray(i["positions"][0].reshape(TT, P).T), "weights": weights,
        "cols": cols, "k1": k1, "gmask": gmask, "ident": np.eye(P, dtype=np.float32),
        "wlr": np.ascontiguousarray(i["gla_w_lr"].transpose(1, 0, 2)), "context": i["ctx_2"][0], "k2": k2,
    }


def kernel(**inputs):
    import concourse.bacc as _bacc
    from concourse.bass_utils import run_bass_kernel_spmd as _run

    arrays = {"in_" + k: np.ascontiguousarray(v) for k, v in lay_out({k: np.asarray(v) for k, v in inputs.items()}).items()}
    nc = _bacc.Bacc("TRN2", target_bir_lowering=False, num_devices=1)
    args = [nc.dram_tensor(k, v.shape, mybir.dt.from_np(v.dtype), kind="ExternalInput").ap() for k, v in arrays.items()]
    out = nc.dram_tensor("out", (1, S, D), F32, kind="ExternalOutput").ap()
    build(nc, *args, out)
    return _run(nc, [arrays], core_ids=[0]).results[0]["out"]
```
